# Optimizing a Trainium2 kernel written in Bass

```python
import jax
import jax.numpy as jnp
from jax import lax
import numpy as np
import jax, jax.numpy as jnp

D_MODEL = 1024
BATCH = 1
SEQ = 256
DEPTH = 2

GRID_W = 64
CTX_LEN = 256
QBLK = 128
ROPE_THETA = 10000.0
EPS = 1e-6

POOL_GROUPS = 4
POOL_CH = 64
POOL_DIM = POOL_GROUPS * POOL_CH
POOL_WINDOWS = (2, 4, 8, 16)

HEAD_DIM = 64
GQA_HEADS = 12
GQA_KV_HEADS = 4
GQA_GROUP = GQA_HEADS // GQA_KV_HEADS
GQA_Q_DIM = GQA_HEADS * HEAD_DIM
GQA_KV_DIM = GQA_KV_HEADS * HEAD_DIM
L0_IN = POOL_DIM + GQA_Q_DIM + 2 * GQA_KV_DIM
L0_MIX = POOL_DIM + GQA_Q_DIM

MLA_HEADS = 8
MLA_NOPE = 64
MLA_ROPE = 32
MLA_QK = MLA_NOPE + MLA_ROPE
MLA_V = 64
MLA_Q_LORA = 384
MLA_KV_LORA = 256

NA_HEADS = 8
NA_HEAD_DIM = 64
NA_DIM = NA_HEADS * NA_HEAD_DIM
NA_ROWS = 8
NA_COLS = 16

L1_IN = MLA_Q_LORA + MLA_KV_LORA + MLA_ROPE + 3 * NA_DIM
L1_MIX = MLA_HEADS * MLA_V + NA_DIM

FFN_DIM = -(-8 * D_MODEL // (3 * 256)) * 256


def rmsnorm(x, g):
    xf = x.astype(jnp.float32)
    y = xf * lax.rsqrt(jnp.mean(xf * xf, axis=-1, keepdims=True) + EPS)
    return y.astype(x.dtype) * g

def rope_1d(x, pos):
    d = x.shape[-1]
    half = d // 2
    inv = (ROPE_THETA ** (-np.arange(half, dtype=np.float32) * 2.0 / d)).astype(np.float32)
    ang = pos.astype(jnp.float32)[:, None] * inv[None, :]
    shape = (1, x.shape[1]) + (1,) * (x.ndim - 3) + (half,)
    cos = jnp.cos(ang).reshape(shape)
    sin = jnp.sin(ang).reshape(shape)
    xf = x.astype(jnp.float32)
    x1, x2 = xf[..., :half], xf[..., half:]
    return jnp.concatenate([x1 * cos - x2 * sin, x1 * sin + x2 * cos], axis=-1).astype(x.dtype)

def axial_rope(x, row, col):
    half = x.shape[-1] // 2
    return jnp.concatenate([rope_1d(x[..., :half], row), rope_1d(x[..., half:], col)], axis=-1)

def split_cols(p, sizes):
    return jnp.split(p, [int(o) for o in np.cumsum(sizes)[:-1]], axis=-1)

def block_attention(q, k, v, scale):
    B, T = q.shape[:2]
    qb = jnp.moveaxis(q.reshape((B, T // QBLK, QBLK) + q.shape[2:]), 1, 0)

    def one_block(q_blk):
        s = jnp.einsum("bqhgd,bkhd->bhgqk", q_blk, k).astype(jnp.float32) * scale
        p = jax.nn.softmax(s, axis=-1).astype(v.dtype)
        return jnp.einsum("bhgqk,bkhd->bqhgd", p, v)

    o = lax.map(one_block, qb)
    return jnp.moveaxis(o, 0, 1).reshape((B, T) + o.shape[3:])

def multiscale_pool(u, w_grp, ch_scale):
    B, T, _ = u.shape
    ug = u.reshape(B, T, POOL_GROUPS, POOL_CH).astype(jnp.float32)
    csum = jnp.concatenate([jnp.zeros((B, 1, POOL_GROUPS, POOL_CH), jnp.float32),
                            jnp.cumsum(ug, axis=1)], axis=1)
    t = np.arange(T)
    lo = np.stack([np.clip(t - w // 2, 0, T) for w in POOL_WINDOWS], axis=-1).astype(np.int32)
    hi = np.stack([np.clip(t - w // 2 + w, 0, T) for w in POOL_WINDOWS], axis=-1).astype(np.int32)
    grp = np.arange(POOL_GROUPS, dtype=np.int32)[None, :]
    win_sum = csum[:, hi, grp] - csum[:, lo, grp]
    count = jnp.asarray((hi - lo).astype(np.float32))[None, :, :, None]
    d = (win_sum / count - ug).astype(u.dtype)
    y = jnp.einsum("btgc,gcd->btgd", d, w_grp).reshape(B, T, POOL_DIM)
    return y * ch_scale

def neighbourhood_attention(q, k, v, k_ctx, v_ctx, rpb, scale):
    B, S, H, dh = q.shape
    rows = S // GRID_W
    kr = min(NA_ROWS, rows)
    kc = NA_COLS
    cols = np.arange(GRID_W)
    key_col = (np.clip(cols - kc // 2, 0, GRID_W - kc)[:, None] + np.arange(kc)[None, :]).astype(np.int32)
    dc_idx = (key_col - cols[:, None] + (NA_COLS - 1)).astype(np.int32)
    n_win = kr * kc
    q_rows = jnp.moveaxis(q.reshape(B, rows, GRID_W, H, dh), 1, 0)

    def one_row(args):
        r, q_r = args
        r0 = jnp.clip(r - kr // 2, 0, rows - kr)
        key_row = r0 + jnp.arange(kr, dtype=jnp.int32)
        idx = (key_row[None, :, None] * GRID_W + key_col[:, None, :]).reshape(GRID_W, n_win)
        k_w = jnp.take(k, idx, axis=1)
        v_w = jnp.take(v, idx, axis=1)
        bias = rpb[:, key_row - r + (NA_ROWS - 1)][:, :, dc_idx]
        bias = jnp.transpose(bias, (0, 2, 1, 3)).reshape(H, GRID_W, n_win)
        s_win = jnp.einsum("bqhd,bqkhd->bhqk", q_r, k_w).astype(jnp.float32) * scale + bias.astype(jnp.float32)
        s_ctx = jnp.einsum("bqhd,bchd->bhqc", q_r, k_ctx).astype(jnp.float32) * scale
        p = jax.nn.softmax(jnp.concatenate([s_win, s_ctx], axis=-1), axis=-1).astype(v.dtype)
        return (jnp.einsum("bhqk,bqkhd->bqhd", p[..., :n_win], v_w)
                + jnp.einsum("bhqc,bchd->bqhd", p[..., n_win:], v_ctx))

    o = lax.map(one_row, (jnp.arange(rows, dtype=jnp.int32), q_rows))
    return jnp.moveaxis(o, 0, 1).reshape(B, S, H, dh)

def adaln(cond, w, b):
    d = w.shape[0]
    m = jax.nn.silu(cond) @ w + b
    return [m[:, None, i * d:(i + 1) * d] for i in range(6)]

def modulate(x, g, shift, scale):
    return rmsnorm(x, g) * (1.0 + scale) + shift

def swiglu(h, wg, wu, wd):
    return (jax.nn.silu(h @ wg) * (h @ wu)) @ wd

def mixer_pool_gqa(h, hc, row, col, need_ctx, w_in, pool_w, pool_scale, q_gain, k_gain, w_out):
    B, S, _ = h.shape
    Tc = hc.shape[1]
    sizes = (POOL_DIM, GQA_Q_DIM, GQA_KV_DIM, GQA_KV_DIM)
    a, q, k, v = split_cols(h @ w_in, sizes)
    ac, qc, kc, vc = split_cols(hc @ w_in, sizes)
    q = axial_rope(rmsnorm(q.reshape(B, S, GQA_KV_HEADS, GQA_GROUP, HEAD_DIM), q_gain), row, col)
    k = axial_rope(rmsnorm(k.reshape(B, S, GQA_KV_HEADS, HEAD_DIM), k_gain), row, col)
    v = v.reshape(B, S, GQA_KV_HEADS, HEAD_DIM)
    kc = rmsnorm(kc.reshape(B, Tc, GQA_KV_HEADS, HEAD_DIM), k_gain)
    vc = vc.reshape(B, Tc, GQA_KV_HEADS, HEAD_DIM)
    scale = HEAD_DIM ** -0.5
    attn = block_attention(q, jnp.concatenate([kc, k], axis=1), jnp.concatenate([vc, v], axis=1),
                           scale).reshape(B, S, GQA_Q_DIM)
    out = jnp.concatenate([multiscale_pool(a, pool_w, pool_scale), attn], axis=-1) @ w_out
    if not need_ctx:
        return out, None
    qc = rmsnorm(qc.reshape(B, Tc, GQA_KV_HEADS, GQA_GROUP, HEAD_DIM), q_gain)
    attn_c = block_attention(qc, kc, vc, scale).reshape(B, Tc, GQA_Q_DIM)
    out_c = jnp.concatenate([multiscale_pool(ac, pool_w, pool_scale), attn_c], axis=-1) @ w_out
    return out, out_c

def mixer_mla_na(h, hc, row, col, need_ctx, w_in, q_a_gain, kv_a_gain, w_uq, w_ukv,
                 mla_q_gain, mla_k_gain, na_q_gain, na_k_gain, na_rpb, w_out):
    B, S, _ = h.shape
    Tc = hc.shape[1]
    sizes = (MLA_Q_LORA, MLA_KV_LORA, MLA_ROPE, NA_DIM, NA_DIM, NA_DIM)
    cq, ckv, kr, nq, nk, nv = split_cols(h @ w_in, sizes)
    cqc, ckvc, krc, nqc, nkc, nvc = split_cols(hc @ w_in, sizes)

    def mla_q(cq_, T):
        q_ = (rmsnorm(cq_, q_a_gain) @ w_uq).reshape(B, T, MLA_HEADS, MLA_QK)
        return rmsnorm(q_, mla_q_gain)

    def mla_kv(ckv_, kr_, T):
        kv = (rmsnorm(ckv_, kv_a_gain) @ w_ukv).reshape(B, T, MLA_HEADS, MLA_NOPE + MLA_V)
        k_rope = jnp.broadcast_to(kr_[:, :, None, :], (B, T, MLA_HEADS, MLA_ROPE))
        k_ = jnp.concatenate([kv[..., :MLA_NOPE], k_rope], axis=-1)
        return rmsnorm(k_, mla_k_gain), kv[..., MLA_NOPE:]

    def rope_tail(t):
        return jnp.concatenate([t[..., :MLA_NOPE], axial_rope(t[..., MLA_NOPE:], row, col)], axis=-1)

    mq = rope_tail(mla_q(cq, S))
    mk, mv = mla_kv(ckv, kr, S)
    mk = rope_tail(mk)
    mkc, mvc = mla_kv(ckvc, krc, Tc)
    mla_scale = MLA_QK ** -0.5
    o_mla = block_attention(mq[:, :, :, None], jnp.concatenate([mkc, mk], axis=1),
                            jnp.concatenate([mvc, mv], axis=1), mla_scale).reshape(B, S, MLA_HEADS * MLA_V)

    q_na = rmsnorm(nq.reshape(B, S, NA_HEADS, NA_HEAD_DIM), na_q_gain)
    k_na = rmsnorm(nk.reshape(B, S, NA_HEADS, NA_HEAD_DIM), na_k_gain)
    v_na = nv.reshape(B, S, NA_HEADS, NA_HEAD_DIM)
    k_nac = rmsnorm(nkc.reshape(B, Tc, NA_HEADS, NA_HEAD_DIM), na_k_gain)
    v_nac = nvc.reshape(B, Tc, NA_HEADS, NA_HEAD_DIM)
    na_scale = NA_HEAD_DIM ** -0.5
    o_na = neighbourhood_attention(q_na, k_na, v_na, k_nac, v_nac, na_rpb, na_scale).reshape(B, S, NA_DIM)

    out = jnp.concatenate([o_mla, o_na], axis=-1) @ w_out
    if not need_ctx:
        return out, None
    mqc = mla_q(cqc, Tc)
    o_mla_c = block_attention(mqc[:, :, :, None], mkc, mvc, mla_scale).reshape(B, Tc, MLA_HEADS * MLA_V)
    q_nac = rmsnorm(nqc.reshape(B, Tc, NA_HEADS, NA_HEAD_DIM), na_q_gain)
    o_na_c = block_attention(q_nac[:, :, :, None], k_nac, v_nac, na_scale).reshape(B, Tc, NA_DIM)
    out_c = jnp.concatenate([o_mla_c, o_na_c], axis=-1) @ w_out
    return out, out_c

def first_inputs(seed: int = 0) -> dict:
    key = jax.random.key(seed)
    ks = iter(jax.random.split(key, 48))

    def nrm(shape, s):
        return jax.random.normal(next(ks), shape, jnp.float32) * s

    def gain(n):
        return 1.0 + nrm((n,), 0.1)

    D = D_MODEL
    inp = {}
    inp["x"] = nrm((BATCH, SEQ, D), 1.0)
    inp["c"] = nrm((BATCH, D), 1.0)
    inp["ctx"] = nrm((BATCH, CTX_LEN, D), 1.0)
    inp["c_ctx"] = nrm((D,), 1.0)
    inp["l0_ada_w"] = nrm((D, 6 * D), 0.5 * D ** -0.5)
    inp["l0_ada_b"] = nrm((6 * D,), 0.02)
    inp["l0_norm_mix"] = gain(D)
    inp["l0_norm_ffn"] = gain(D)
    inp["l0_w_in"] = nrm((D, L0_IN), D ** -0.5)
    inp["l0_pool_w"] = nrm((POOL_GROUPS, POOL_CH, POOL_CH), POOL_CH ** -0.5)
    inp["l0_pool_scale"] = gain(POOL_DIM)
    inp["l0_q_gain"] = gain(HEAD_DIM)
    inp["l0_k_gain"] = gain(HEAD_DIM)
    inp["l0_w_out"] = nrm((L0_MIX, D), L0_MIX ** -0.5)
    inp["l0_ffn_w_gate"] = nrm((D, FFN_DIM), D ** -0.5)
    inp["l0_ffn_w_up"] = nrm((D, FFN_DIM), D ** -0.5)
    inp["l0_ffn_w_down"] = nrm((FFN_DIM, D), FFN_DIM ** -0.5)
    inp["l1_ada_w"] = nrm((D, 6 * D), 0.5 * D ** -0.5)
    inp["l1_ada_b"] = nrm((6 * D,), 0.02)
    inp["l1_norm_mix"] = gain(D)
    inp["l1_norm_ffn"] = gain(D)
    inp["l1_w_in"] = nrm((D, L1_IN), D ** -0.5)
    inp["l1_mla_q_a_gain"] = gain(MLA_Q_LORA)
    inp["l1_mla_kv_a_gain"] = gain(MLA_KV_LORA)
    inp["l1_mla_w_uq"] = nrm((MLA_Q_LORA, MLA_HEADS * MLA_QK), MLA_Q_LORA ** -0.5)
    inp["l1_mla_w_ukv"] = nrm((MLA_KV_LORA, MLA_HEADS * (MLA_NOPE + MLA_V)), MLA_KV_LORA ** -0.5)
    inp["l1_mla_q_gain"] = gain(MLA_QK)
    inp["l1_mla_k_gain"] = gain(MLA_QK)
    inp["l1_na_q_gain"] = gain(NA_HEAD_DIM)
    inp["l1_na_k_gain"] = gain(NA_HEAD_DIM)
    inp["l1_na_rpb"] = nrm((NA_HEADS, 2 * NA_ROWS - 1, 2 * NA_COLS - 1), 0.1)
    inp["l1_w_out"] = nrm((L1_MIX, D), L1_MIX ** -0.5)
    inp["l1_ffn_w_gate"] = nrm((D, FFN_DIM), D ** -0.5)
    inp["l1_ffn_w_up"] = nrm((D, FFN_DIM), D ** -0.5)
    inp["l1_ffn_w_down"] = nrm((FFN_DIM, D), FFN_DIM ** -0.5)
    return inp

def first_block(x, c, ctx, c_ctx,
              l0_ada_w, l0_ada_b, l0_norm_mix, l0_norm_ffn, l0_w_in, l0_pool_w, l0_pool_scale,
              l0_q_gain, l0_k_gain, l0_w_out, l0_ffn_w_gate, l0_ffn_w_up, l0_ffn_w_down,
              l1_ada_w, l1_ada_b, l1_norm_mix, l1_norm_ffn, l1_w_in, l1_mla_q_a_gain, l1_mla_kv_a_gain,
              l1_mla_w_uq, l1_mla_w_ukv, l1_mla_q_gain, l1_mla_k_gain, l1_na_q_gain, l1_na_k_gain,
              l1_na_rpb, l1_w_out, l1_ffn_w_gate, l1_ffn_w_up, l1_ffn_w_down):
    S = x.shape[1]
    tok = jnp.arange(S, dtype=jnp.int32)
    row = tok // GRID_W
    col = tok % GRID_W
    layers = [
        (l0_ada_w, l0_ada_b, l0_norm_mix, l0_norm_ffn, l0_ffn_w_gate, l0_ffn_w_up, l0_ffn_w_down,
         mixer_pool_gqa, (l0_w_in, l0_pool_w, l0_pool_scale, l0_q_gain, l0_k_gain, l0_w_out)),
        (l1_ada_w, l1_ada_b, l1_norm_mix, l1_norm_ffn, l1_ffn_w_gate, l1_ffn_w_up, l1_ffn_w_down,
         mixer_mla_na, (l1_w_in, l1_mla_q_a_gain, l1_mla_kv_a_gain, l1_mla_w_uq, l1_mla_w_ukv,
                        l1_mla_q_gain, l1_mla_k_gain, l1_na_q_gain, l1_na_k_gain, l1_na_rpb, l1_w_out)),
    ]
    xc = ctx
    for i in range(DEPTH):
        ada_w, ada_b, n_mix, n_ffn, wg, wu, wd, mixer, mparams = layers[i]
        need_ctx = i < DEPTH - 1
        sh1, sc1, g1, sh2, sc2, g2 = adaln(c, ada_w, ada_b)
        csh1, csc1, cg1, csh2, csc2, cg2 = adaln(c_ctx[None, :], ada_w, ada_b)
        h = modulate(x, n_mix, sh1, sc1)
        hc = modulate(xc, n_mix, csh1, csc1)
        o, oc = mixer(h, hc, row, col, need_ctx, *mparams)
        x = x + g1 * o
        x = x + g2 * swiglu(modulate(x, n_ffn, sh2, sc2), wg, wu, wd)
        if need_ctx:
            xc = xc + cg1 * oc
            xc = xc + cg2 * swiglu(modulate(xc, n_ffn, csh2, csc2), wg, wu, wd)
    return x


D_MIX = D_MODEL
GLA_HEADS = 4
GLA_DK = 64
GLA_DV = 128
GLA_QK = GLA_HEADS * GLA_DK
GLA_WIDTH = GLA_HEADS * GLA_DV
GLA_LOWRANK = 16
GLA_TAU = 16.0
GLA_CHUNK = 64
SSD_HEADS = 8
SSD_HEADDIM = 64
SSD_WIDTH = SSD_HEADS * SSD_HEADDIM
SSD_GROUPS = 2
SSD_STATE = 64
SSD_BC = SSD_GROUPS * SSD_STATE
SSD_CONV = 4
SSD_CONV_DIM = SSD_WIDTH + 2 * SSD_BC
SSD_CHUNK = 128
D_FF = 3584
N_EXPERTS = 8
TOP_K = 2

IN_SIZES = (GLA_QK, GLA_QK, GLA_WIDTH, GLA_WIDTH, GLA_LOWRANK,
            SSD_WIDTH, SSD_WIDTH, SSD_BC, SSD_BC, SSD_HEADS)
IN_SPLITS = [int(s) for s in np.cumsum(IN_SIZES)[:-1]]
D_IN_PROJ = int(sum(IN_SIZES))


def rmsnorm_2(x, w):
    x32 = x.astype(jnp.float32)
    r = x32 * lax.rsqrt(jnp.mean(x32 * x32, axis=-1, keepdims=True) + EPS)
    return (r * w.astype(jnp.float32)).astype(x.dtype)

def inter_chunk_states(decay, contrib):
    d = jnp.moveaxis(decay, 1, 0)
    u = jnp.moveaxis(contrib, 1, 0)

    def step(s, inp):
        dn, un = inp
        return dn * s + un, s

    _, prev = lax.scan(step, jnp.zeros_like(u[0]), (d, u))
    return jnp.moveaxis(prev, 0, 1)

def gla_chunked(q, k, v, log_a):
    bsz, seq, nh, dk = q.shape
    dv = v.shape[-1]
    nc = seq // GLA_CHUNK
    shp = lambda t: t.astype(jnp.float32).reshape(bsz, nc, GLA_CHUNK, nh, t.shape[-1])
    q, k, v, log_a = shp(q) * (dk ** -0.5), shp(k), shp(v), shp(log_a)
    b = jnp.cumsum(log_a, axis=2)
    qe = q * jnp.exp(b)
    ke = k * jnp.exp(-b)
    causal = jnp.tril(jnp.ones((GLA_CHUNK, GLA_CHUNK), bool))
    att = jnp.einsum('bnihd,bnjhd->bnhij', qe, ke)
    att = jnp.where(causal, att, 0.0)
    o_intra = jnp.einsum('bnhij,bnjhv->bnihv', att, v)
    b_last = b[:, :, -1]
    k_tail = k * jnp.exp(b_last[:, :, None] - b)
    contrib = jnp.einsum('bnjhd,bnjhv->bnhdv', k_tail, v)
    s_prev = inter_chunk_states(jnp.exp(b_last)[..., None], contrib)
    o_inter = jnp.einsum('bnihd,bnhdv->bnihv', qe, s_prev)
    return (o_intra + o_inter).reshape(bsz, seq, nh, dv)

def ssd_chunked(xh, dt, a, bm, cm):
    bsz, seq, nh, p = xh.shape
    rep = nh // bm.shape[2]
    nc = seq // SSD_CHUNK
    f = lambda t: t.astype(jnp.float32).reshape((bsz, nc, SSD_CHUNK) + t.shape[2:])
    xh, dt = f(xh), f(dt)
    bh = f(jnp.repeat(bm, rep, axis=2))
    ch = f(jnp.repeat(cm, rep, axis=2))
    cum = jnp.cumsum(dt * a, axis=2)
    causal = jnp.tril(jnp.ones((SSD_CHUNK, SSD_CHUNK), bool))[:, :, None]
    seg = cum[:, :, :, None, :] - cum[:, :, None, :, :]
    decay = jnp.exp(jnp.where(causal, seg, -jnp.inf))
    xdt = xh * dt[..., None]
    scores = jnp.einsum('bnihs,bnjhs->bnijh', ch, bh) * decay
    y_intra = jnp.einsum('bnijh,bnjhp->bnihp', scores, xdt)
    cum_last = cum[:, :, -1]
    contrib = jnp.einsum('bnjhs,bnjhp->bnhps',
                         bh * jnp.exp(cum_last[:, :, None] - cum)[..., None], xdt)
    s_prev = inter_chunk_states(jnp.exp(cum_last)[..., None, None], contrib)
    y_inter = jnp.einsum('bnihs,bnhps->bnihp', ch * jnp.exp(cum)[..., None], s_prev)
    return (y_intra + y_inter).reshape(bsz, seq, nh, p)

def causal_depthwise_conv(u, w, b):
    kw, cdim = w.shape
    out = lax.conv_general_dilated(u, w.astype(u.dtype)[:, None, :], window_strides=(1,),
                                   padding=[(kw - 1, 0)],
                                   dimension_numbers=('NWC', 'WIO', 'NWC'),
                                   feature_group_count=cdim)
    return out + b.astype(u.dtype)

def hybrid_mixer(h, w_in, gla_a_w, gla_a_b, gla_norm_w, conv_w, conv_b,
                 dt_bias, a_log, d_skip, ssd_norm_w, w_out):
    bsz, seq, _ = h.shape
    proj = h @ w_in
    q, k, v, g, alr, z, xs, bm, cm, dt = jnp.split(proj, IN_SPLITS, axis=-1)
    log_a = jax.nn.log_sigmoid((alr @ gla_a_w + gla_a_b).astype(jnp.float32)) / GLA_TAU
    o = gla_chunked(q.reshape(bsz, seq, GLA_HEADS, GLA_DK),
                    k.reshape(bsz, seq, GLA_HEADS, GLA_DK),
                    v.reshape(bsz, seq, GLA_HEADS, GLA_DV),
                    log_a.reshape(bsz, seq, GLA_HEADS, GLA_DK))
    o = rmsnorm_2(o, gla_norm_w) * jax.nn.silu(g.astype(jnp.float32).reshape(bsz, seq, GLA_HEADS, GLA_DV))
    o = o.reshape(bsz, seq, GLA_WIDTH)
    xbc = jax.nn.silu(causal_depthwise_conv(jnp.concatenate([xs, bm, cm], axis=-1), conv_w, conv_b))
    xs, bm, cm = jnp.split(xbc, [SSD_WIDTH, SSD_WIDTH + SSD_BC], axis=-1)
    dt = jax.nn.softplus(dt.astype(jnp.float32) + dt_bias.astype(jnp.float32))
    a = -jnp.exp(a_log.astype(jnp.float32))
    xh = xs.reshape(bsz, seq, SSD_HEADS, SSD_HEADDIM)
    y = ssd_chunked(xh, dt, a,
                    bm.reshape(bsz, seq, SSD_GROUPS, SSD_STATE),
                    cm.reshape(bsz, seq, SSD_GROUPS, SSD_STATE))
    y = y + d_skip.astype(jnp.float32)[:, None] * xh.astype(jnp.float32)
    y = y.reshape(bsz, seq, SSD_WIDTH) * jax.nn.silu(z.astype(jnp.float32))
    y = rmsnorm_2(y, ssd_norm_w)
    merged = jnp.concatenate([o, y], axis=-1).astype(h.dtype)
    return merged @ w_out

def swiglu_2(t, w_gate, w_up, w_down):
    return (jax.nn.silu(t @ w_gate) * (t @ w_up)) @ w_down

def moe_swiglu(h, router_w, w_gate, w_up, w_down):
    bsz, seq, d = h.shape
    t = h.reshape(bsz * seq, d)
    logits = (t @ router_w).astype(jnp.float32)
    top_v, top_i = lax.top_k(logits, TOP_K)
    top_p = jax.nn.softmax(top_v, axis=-1)
    gates = jnp.sum(jax.nn.one_hot(top_i, N_EXPERTS, dtype=jnp.float32) * top_p[..., None], axis=1)
    gates = gates.astype(h.dtype)
    out = jnp.zeros_like(t)
    for e in range(N_EXPERTS):
        out = out + gates[:, e:e + 1] * swiglu_2(t, w_gate[e], w_up[e], w_down[e])
    return out.reshape(bsz, seq, d)

def second_inputs(seed: int = 0) -> dict:
    key = jax.random.key(seed)
    ks = iter(list(jax.random.split(key, 40)))
    f32 = jnp.float32
    nrm = lambda shape, scale: jax.random.normal(next(ks), shape, f32) * scale
    n_dense = (DEPTH + 1) // 2
    n_moe = DEPTH // 2
    d = D_MODEL
    x = nrm((BATCH, SEQ, d), 1.0)
    c = nrm((BATCH, d), 1.0)
    ada_w = nrm((DEPTH, d, 6 * d), 0.5 * d ** -0.5)
    ada_b = nrm((DEPTH, 6 * d), 0.02)
    norm1_w = 1.0 + nrm((DEPTH, d), 0.02)
    w_in = nrm((DEPTH, d, D_IN_PROJ), d ** -0.5)
    gla_a_w = nrm((DEPTH, GLA_LOWRANK, GLA_QK), GLA_LOWRANK ** -0.5)
    gla_a_b = nrm((DEPTH, GLA_QK), 0.1)
    gla_norm_w = 1.0 + nrm((DEPTH, GLA_DV), 0.02)
    conv_w = nrm((DEPTH, SSD_CONV, SSD_CONV_DIM), SSD_CONV ** -0.5)
    conv_b = nrm((DEPTH, SSD_CONV_DIM), 0.02)
    dt0 = jnp.exp(jax.random.uniform(next(ks), (DEPTH, SSD_HEADS), f32,
                                     np.log(1e-3).astype(np.float32), np.log(1e-1).astype(np.float32)))
    dt_bias = dt0 + jnp.log(-jnp.expm1(-dt0))
    a_log = jnp.log(jax.random.uniform(next(ks), (DEPTH, SSD_HEADS), f32, 1.0, 16.0))
    d_skip = 1.0 + nrm((DEPTH, SSD_HEADS), 0.1)
    ssd_norm_w = 1.0 + nrm((DEPTH, SSD_WIDTH), 0.02)
    w_out = nrm((DEPTH, D_MIX, d), D_MIX ** -0.5)
    norm2_w = 1.0 + nrm((DEPTH, d), 0.02)
    ffn_w_gate = nrm((n_dense, d, D_FF), d ** -0.5)
    ffn_w_up = nrm((n_dense, d, D_FF), d ** -0.5)
    ffn_w_down = nrm((n_dense, D_FF, d), D_FF ** -0.5)
    router_w = nrm((n_moe, d, N_EXPERTS), d ** -0.5)
    moe_w_gate = nrm((n_moe, N_EXPERTS, d, D_FF), d ** -0.5)
    moe_w_up = nrm((n_moe, N_EXPERTS, d, D_FF), d ** -0.5)
    moe_w_down = nrm((n_moe, N_EXPERTS, D_FF, d), D_FF ** -0.5)
    final_norm_w = 1.0 + nrm((d,), 0.02)
    return {"x": x, "c": c, "ada_w": ada_w, "ada_b": ada_b, "norm1_w": norm1_w,
            "w_in": w_in, "gla_a_w": gla_a_w, "gla_a_b": gla_a_b, "gla_norm_w": gla_norm_w,
            "conv_w": conv_w, "conv_b": conv_b, "dt_bias": dt_bias, "a_log": a_log,
            "d_skip": d_skip, "ssd_norm_w": ssd_norm_w, "w_out": w_out, "norm2_w": norm2_w,
            "ffn_w_gate": ffn_w_gate, "ffn_w_up": ffn_w_up, "ffn_w_down": ffn_w_down,
            "router_w": router_w, "moe_w_gate": moe_w_gate, "moe_w_up": moe_w_up,
            "moe_w_down": moe_w_down, "final_norm_w": final_norm_w}

def second_block(x, c, ada_w, ada_b, norm1_w, w_in, gla_a_w, gla_a_b, gla_norm_w,
              conv_w, conv_b, dt_bias, a_log, d_skip, ssd_norm_w, w_out, norm2_w,
              ffn_w_gate, ffn_w_up, ffn_w_down, router_w, moe_w_gate, moe_w_up,
              moe_w_down, final_norm_w):
    s = jax.nn.silu(c)
    for l in range(DEPTH):
        mod = s @ ada_w[l] + ada_b[l]
        sh1, sc1, g1, sh2, sc2, g2 = [m[:, None, :] for m in jnp.split(mod, 6, axis=-1)]
        h = rmsnorm_2(x, norm1_w[l]) * (1.0 + sc1) + sh1
        mix = hybrid_mixer(h, w_in[l], gla_a_w[l], gla_a_b[l], gla_norm_w[l], conv_w[l],
                           conv_b[l], dt_bias[l], a_log[l], d_skip[l], ssd_norm_w[l], w_out[l])
        x = x + g1 * mix
        h = rmsnorm_2(x, norm2_w[l]) * (1.0 + sc2) + sh2
        if l % 2 == 0:
            i = l // 2
            ff = swiglu_2(h, ffn_w_gate[i], ffn_w_up[i], ffn_w_down[i])
        else:
            i = l // 2
            ff = moe_swiglu(h, router_w[i], moe_w_gate[i], moe_w_up[i], moe_w_down[i])
        x = x + g2 * ff
    return rmsnorm_2(x, final_norm_w)


def setup_inputs(seed=0):
    out = dict(first_inputs(seed))
    for name, value in second_inputs(seed + 1).items():
        if name != "x":
            out[name + "_2"] = value
    return out


def reference(
    x, c, ctx, c_ctx, l0_ada_w, l0_ada_b, l0_norm_mix, l0_norm_ffn, l0_w_in, l0_pool_w,
    l0_pool_scale, l0_q_gain, l0_k_gain, l0_w_out, l0_ffn_w_gate, l0_ffn_w_up, l0_ffn_w_down,
    l1_ada_w, l1_ada_b, l1_norm_mix, l1_norm_ffn, l1_w_in, l1_mla_q_a_gain, l1_mla_kv_a_gain,
    l1_mla_w_uq, l1_mla_w_ukv, l1_mla_q_gain, l1_mla_k_gain, l1_na_q_gain, l1_na_k_gain,
    l1_na_rpb, l1_w_out, l1_ffn_w_gate, l1_ffn_w_up, l1_ffn_w_down, c_2, ada_w_2, ada_b_2,
    norm1_w_2, w_in_2, gla_a_w_2, gla_a_b_2, gla_norm_w_2, conv_w_2, conv_b_2, dt_bias_2,
    a_log_2, d_skip_2, ssd_norm_w_2, w_out_2, norm2_w_2, ffn_w_gate_2, ffn_w_up_2, ffn_w_down_2,
    router_w_2, moe_w_gate_2, moe_w_up_2, moe_w_down_2, final_norm_w_2,
):
    x = first_block(
        x, c, ctx, c_ctx, l0_ada_w, l0_ada_b, l0_norm_mix, l0_norm_ffn, l0_w_in, l0_pool_w,
        l0_pool_scale, l0_q_gain, l0_k_gain, l0_w_out, l0_ffn_w_gate, l0_ffn_w_up,
        l0_ffn_w_down, l1_ada_w, l1_ada_b, l1_norm_mix, l1_norm_ffn, l1_w_in, l1_mla_q_a_gain,
        l1_mla_kv_a_gain, l1_mla_w_uq, l1_mla_w_ukv, l1_mla_q_gain, l1_mla_k_gain, l1_na_q_gain,
        l1_na_k_gain, l1_na_rpb, l1_w_out, l1_ffn_w_gate, l1_ffn_w_up, l1_ffn_w_down,
    )
    return second_block(
        x, c_2, ada_w_2, ada_b_2, norm1_w_2, w_in_2, gla_a_w_2, gla_a_b_2, gla_norm_w_2,
        conv_w_2, conv_b_2, dt_bias_2, a_log_2, d_skip_2, ssd_norm_w_2, w_out_2, norm2_w_2,
        ffn_w_gate_2, ffn_w_up_2, ffn_w_down_2, router_w_2, moe_w_gate_2, moe_w_up_2,
        moe_w_down_2, final_norm_w_2,
    )


_drawn_inputs = setup_inputs


def setup_inputs(seed=0):
    import zlib

    import numpy as np

    out = dict(_drawn_inputs(seed))
    spreads = {}
    factors = {'l0_norm_mix': 2.675,
     'l0_pool_scale': 2.695,
     'l0_q_gain': 8.0,
     'l0_k_gain': 8.0,
     'l1_norm_mix': 7.551,
     'l1_mla_q_a_gain': 8.0,
     'l1_mla_kv_a_gain': 6.71,
     'l1_mla_q_gain': 8.0,
     'l1_mla_k_gain': 8.0,
     'l1_na_q_gain': 8.0,
     'l1_na_k_gain': 8.0,
     'l1_na_rpb': 8.0,
     'norm1_w_2': 4.784,
     'gla_a_b_2': 4.927,
     'gla_norm_w_2': 8.0,
     'conv_b_2': 30.759,
     'ssd_norm_w_2': 31.259,
     'norm2_w_2': 3.755,
     'final_norm_w_2': 8.113,
     'd_skip_2': 8.0}
    for name, (base, spread) in spreads.items():
        noise = np.random.default_rng([zlib.crc32(name.encode()), seed]).standard_normal(out[name].shape)
        drawn = base * np.exp(spread * noise) if base else spread * noise
        out[name] = jnp.asarray(drawn.astype(out[name].dtype))
    for name, factor in factors.items():
        out[name] = (out[name] * factor).astype(out[name].dtype)
    return out
```

```python
from contextlib import ExitStack

import numpy as np
import concourse.bass as bass
from concourse import mybir

F32 = mybir.dt.float32
BF16 = mybir.dt.bfloat16
I32 = mybir.dt.int32
ALU = mybir.AluOpType
ACT = mybir.ActivationFunctionType
AX = mybir.AxisListType

D, T, PB = 1024, 256, 128
KD = D // PB
EPS = 1e-6
WC = 384
SLOT, SLOTS = KD * WC, 4
HD = 64
GRID_W, NA_COLS, NA_ROWS = 64, 16, 8
NEG = -1.0e30

CQ, NQ, CKV, KR, NK, NV, L1N = 0, 384, 896, 1152, 1184, 1696, 2208
GQ, GK, GV, GG, GA, SZ, SDT, L2N, CONV = 0, 256, 512, 1024, 1536, 1552, 2064, 2072, 768

F0, F2, NE = 2816, 3584, 8

ROWS = {
    0: dict(qk=(0, 1024), pool=(1024, 256)),
    1: dict(qk=(0, 1024), mq=(1024, 768), mk=(1792, 768)),
    2: dict(ab=(0, 256), gn=(256, 128), sn=(384, 512), dtb=(896, 8), alog=(904, 8), dskip=(912, 8),
            fin=(1024, 1024)),
}
ROWW = 2560
COLS, _at = {}, 0
for _n, _w in (("cond", KD * 3), ("ada_b", 4 * 48), ("n_mix", 4 * KD), ("n_ffn", 4 * KD), ("qa", 3),
               ("kva", 2), ("conv_w", 2 * 24), ("conv_b", 2 * 6), ("router", KD * NE)):
    COLS[_n] = (_at, _w)
    _at += _w
COLW = _at
SQ = ("ident", "tri", "trig", "blkg", "negm", "ones", "iota")


def chunks(n):
    return [(a, min(WC, n - a)) for a in range(0, n, WC)]


class Signal:

    def __init__(self, nc, ctx, name):
        self.sem = ctx.enter_context(nc.semaphore(name))
        self.base = 0

    def at(self, n):
        return self.base + n

    def done(self, n):
        self.base += n


class Place:

    n = 0


class Signals:

    def __init__(self, sig):
        self.ready = sig("ready")
        self.turned = sig("turned")
        self.evacuated = sig("evacuated")
        self.made = sig("made")
        self.scored = sig("scored")
        self.maxed = sig("maxed")
        self.expd = sig("expd")
        self.p_turned = sig("p_turned")
        self.p_copied = sig("p_copied")
        self.summed = sig("summed")
        self.scaled = sig("scaled")
        self.k_made = sig("k_made")
        self.q_made = sig("q_made")
        self.kq_turned = sig("kq_turned")
        self.up_done = sig("up_done")
        self.silu_done = sig("silu_done")
        self.act_done = sig("act_done")
        self.hop_a = sig("hop_a")
        self.hop_b = sig("hop_b")
        self.hop_c = sig("hop_c")
        self.hop_d = sig("hop_d")


class Chain:

    def __init__(self, nc, ctx, name):
        self.sem = ctx.enter_context(nc.semaphore(name))
        self.n = 0

    def __call__(self, eng, ins):
        self.n += 1
        ins.then_inc(self.sem, 1)
        eng.wait_ge(self.sem, self.n)


def program(nc, d, out):
    ctx = ExitStack()
    with ctx:
        build(nc, ctx, d, out)


def build(nc, ctx, d, out):
    def sb(name, shape, dt=F32):
        return ctx.enter_context(nc.sbuf_tensor(name, shape, dt))

    X, XC = sb("x_sb", [PB, 2, D]), sb("ctx_sb", [PB, 2, D])
    XN = sb("normed_or_mix", [PB, 4, D])
    HT = sb("turned", [PB, KD, 512])
    P = sb("projected", [PB, 4 * L1N])
    RING = sb("weights", [PB, SLOTS, SLOT])
    AUX = sb("aux", [PB, 4096])
    EX = sb("extra", [PB, 5120])
    Pb, PT = sb("probs", [PB, 2, 512]), sb("probs_turned", [PB, 2, 512])
    QT, KT = sb("q_turned", [PB, 2, 256]), sb("k_turned", [PB, 2, 512])
    GB = sb("gate_rows", [PB, D])
    ADA = sb("modulations", [PB, 4, 48, 3])
    MA = sb("mod_scale", [PB, 2, KD])
    ROW = sb("row_params", [PB, ROWW])
    COL = sb("column_params", [PB, COLW])
    CS = sb("silu_cond", [PB, KD, 3])
    SQT = sb("square_consts", [PB, len(SQ), PB])
    MKG = sb("gla_mask", [PB, PB], I32)
    ROPE = sb("rope_tables", [PB, 2, 2, 48])
    COUNT = sb("most_tokens", [1, 2], I32)
    SM = sb("small", [PB, 256])
    DG = sb("diag", [PB, 2, PB])
    Z16 = sb("zeros_bf16", [PB, 512], BF16)
    PS = ctx.enter_context(nc.psum_tensor("ps", [PB, 8, 512], F32))
    ident, tri, trig, blkg, negm, ones, iota = (SQT[:, i, :] for i in range(len(SQ)))

    def col(name, i=0, n=1):
        a = COLS[name][0] + i
        return COL[:, a:a + n]

    def row(kind, name):
        a, w = ROWS[kind][name]
        return ROW[:, a:a + w]

    def sig(name):
        return Signal(nc, ctx, name)

    dve_step, act_step = Chain(nc, ctx, "dve_step"), Chain(nc, ctx, "act_step")
    const_in, x_in, rows_in, out_sem = sig("const_in"), sig("x_in"), sig("rows_in"), sig("out_sent")
    slot_in = [sig(f"slot_in{i}") for i in range(SLOTS)]
    slot_used = sig("slot_used")
    hidden_made = sig("hidden_made")
    expert_kept, expert_out = sig("expert_kept"), sig("expert_out")
    S = Signals(sig)

    plan = []

    def planned(name, n):
        plan.extend((name, i) for i in range(n))

    planned("ada", 64)
    planned("l0_w_in", len(chunks(1536)))
    planned("l0_w_out", len(chunks(D)))
    planned("l0_ffn", F0 // PB)
    planned("l0_ffn", F0 // PB)
    planned("l1_w_in", len(chunks(L1N)))
    planned("l1_uq", 2)
    planned("l1_ukv", 3)
    planned("l1_w_out", len(chunks(D)))
    planned("l1_ffn", F0 // PB)
    for layer in range(2):
        planned(f"w_in{layer}", len(chunks(L2N)) + 2)
        planned(f"w_out{layer}", len(chunks(D)))
        planned("ffn2" if layer == 0 else "moe", F2 // PB * (1 if layer == 0 else NE))
    place = Place()

    def load(sp, src, n):
        s = n % SLOTS
        sp.dma_start(RING[:, s, 0:src.shape[1]], src).then_inc(slot_in[s].sem, 16)

    def feed(sp, lo, hi):
        hi = min(hi, len(plan))
        n = lo
        while n < hi:
            name, i = plan[n]
            run = 1
            while n + run < hi and plan[n + run] == (name, i + run):
                run += 1
            if run >= 2 * SLOTS:
                groups = run // SLOTS
                with sp.Fori(0, groups) as g:
                    for j in range(SLOTS):
                        if n >= SLOTS:
                            sp.wait_ge(slot_used.sem, g * SLOTS + (n - SLOTS + j + 1))
                        load(sp, d[name][bass.ds(g * SLOTS + (i + j), 1)].rearrange("o p w -> p (o w)"), n + j)
                n += groups * SLOTS
                continue
            if n >= SLOTS:
                sp.wait_ge(slot_used.sem, n - SLOTS + 1)
            load(sp, d[name][i], n)
            n += 1

    def arrived(eng, n):
        eng.wait_ge(slot_in[n % SLOTS].sem, 16 * (n // SLOTS + 1))

    with nc.Block() as block:
        @block.sync
        def _(sp):
            sp.dma_start(COL[:, :], d["cols"]).then_inc(const_in.sem, 16)
            for n in range(SLOTS):
                load(sp, d["ada"][n], n)
            sp.dma_start(SQT[:, :, :], d["squares"]).then_inc(const_in.sem, 16)
            sp.dma_start(MKG[:, :], d["mask_gla"]).then_inc(const_in.sem, 16)
            sp.dma_start(ROPE[:, :, :, :], d["rope"]).then_inc(const_in.sem, 16)
            sp.dma_start(X[:, :, :], d["x"]).then_inc(x_in.sem, 16)
            sp.dma_start(XC[:, :, :], d["ctx"]).then_inc(x_in.sem, 16)
            sp.wait_ge(const_in.sem, 64)
            sp.wait_ge(x_in.sem, 32)

        @block.scalar
        def _(act):
            act.wait_ge(const_in.sem, 64)
            act_step(act, act.activation(CS[:, :, :].rearrange("p a b -> p (a b)"), col("cond", 0, 3 * KD), ACT.Silu))

        @block.vector
        def _(dve):
            dve_step(dve, dve.memset(Z16[:, :], 0.0))
            dve_step(dve, dve.memset(SM[:, :], 0.0))
            dve_step(dve, dve.memset(SM[:, 0:1], EPS))
            dve_step(dve, dve.memset(SM[:, 1:2], 1.0))
    EPSC, ONEC = SM[:, 0:1], SM[:, 1:2]

    a0, groups = place.n, 64 // SLOTS
    per = WC // PB
    adar = P[0:3, 0:SLOTS * WC].rearrange("p (j n) -> p j n", j=SLOTS)
    with nc.Block() as block:
        @block.sync
        def _(sp):
            feed(sp, a0 + SLOTS, a0 + 64 + SLOTS)

        @block.tensor
        def _(pe):
            with pe.Fori(0, groups) as g:
                for j in range(SLOTS):
                    pe.wait_ge(slot_in[j].sem, g * 16 + 16)
                    for k in range(KD):
                        mm = pe.matmul(PS[0:3, j, 0:WC], CS[:, k, :], RING[:, j, k * WC:(k + 1) * WC],
                                       start=(k == 0), stop=(k == KD - 1))
                    mm.then_inc(slot_used.sem, 1)
                for j in range(SLOTS):
                    pe.wait_ge(S.made.sem, g * SLOTS + (S.made.at(j + 1)))
                    for m in range(per):
                        t = pe.matmul(PS[:, 4 + j, 4 * m:4 * m + 3], adar[:, j, m * PB:(m + 1) * PB],
                                      ident[0:3, 0:3], start=True, stop=True)
                    t.then_inc(S.turned.sem, 1)

        @block.vector
        def _(dve):
            ada = ADA[:, :, :, :].rearrange("p l t c -> p (l t) c")
            with dve.Fori(0, groups) as g:
                for j in range(SLOTS):
                    dve.wait_ge(slot_used.sem, g * SLOTS + (j + 1))
                    dve.tensor_copy(adar[:, j, :], PS[0:3, j, 0:WC]).then_inc(S.made.sem, 1)
                for j in range(SLOTS):
                    dve.wait_ge(S.turned.sem, g * SLOTS + (S.turned.at(j + 1)))
                    src = PS[:, 4 + j, 0:4 * per].rearrange("p (m c) -> p m c", c=4)[:, :, 0:3]
                    b = COL[:, bass.ds(g * (SLOTS * per) + (COLS["ada_b"][0] + j * per), per)]
                    dve.tensor_tensor(ada[:, bass.ds(g * (SLOTS * per) + j * per, per), :], src,
                                      b.unsqueeze(2).broadcast_to([PB, per, 3]), ALU.add)
    place.n += 64
    S.made.done(64)
    S.turned.done(64)

    def refine(dve, r, ss, t, n):
        dve_step(dve, dve.tensor_scalar(ss, ss, 1.0 / n, EPS, ALU.mult, ALU.add))
        dve_step(dve, dve.tensor_tensor(t, r, r, ALU.mult))
        dve_step(dve, dve.tensor_tensor(t, t, ss, ALU.mult))
        dve_step(dve, dve.tensor_scalar(t, t, -0.5, 1.5, ALU.mult, ALU.add))
        return dve.tensor_tensor(r, r, t, ALU.mult)

    def modulate(streams, norm, rows=None):
        nb = 2 * len(streams)
        xs = [st[0][:, b, :] for st in streams for b in range(2)]
        with nc.Block() as block:
            @block.scalar
            def _(act):
                if rows is not None:
                    act.dma_start(ROW[:, :], d["rows"][rows].partition_broadcast(PB)).then_inc(rows_in.sem, 16)
                for b in range(nb):
                    act_step(act, act.activation(XN[:, b, :], xs[b], ACT.Square, accum_out=SM[:, 8 + b:9 + b]))
                act_step(act, act.activation(SM[:, 12:12 + nb], SM[:, 8:8 + nb], ACT.Ln, bias=EPSC, scale=1.0 / D))
                act.activation(SM[:, 16:16 + nb], SM[:, 12:12 + nb], ACT.Exp, scale=-0.5).then_inc(S.hop_a.sem, 1)
                act.wait_ge(S.hop_b.sem, S.hop_b.at(1))
                for b in range(nb):
                    act.activation(XN[:, b, :], xs[b], ACT.Copy, scale=SM[:, 16 + b:17 + b]).then_inc(S.ready.sem, 1)
                if rows is not None:
                    act.wait_ge(rows_in.sem, rows_in.at(16))

            @block.tensor
            def _(pe):
                for k in range(KD):
                    for b in range(nb):
                        if k == 0:
                            pe.wait_ge(S.ready.sem, S.ready.at(b + 1))
                        t = pe.transpose(PS[:, k, b * PB:(b + 1) * PB], XN[:, b, k * PB:(k + 1) * PB], ident)
                    t.then_inc(S.turned.sem, 1)

            @block.vector
            def _(dve):
                dve.wait_ge(S.hop_a.sem, S.hop_a.at(1))
                refine(dve, SM[:, 16:16 + nb], SM[:, 8:8 + nb], SM[:, 20:20 + nb], D).then_inc(S.hop_b.sem, 1)
                for s, (_, layer, part, c) in enumerate(streams):
                    dve_step(dve, dve.scalar_tensor_tensor(
                        out=MA[:, s, :], in0=ADA[:, layer, (part + 1) * KD:(part + 2) * KD, c], scalar=1.0,
                        in1=norm, op0=ALU.add, op1=ALU.mult))
                for k in range(KD):
                    dve.wait_ge(S.turned.sem, S.turned.at(k + 1))
                    for s, (_, layer, part, c) in enumerate(streams):
                        o = slice(s * 256, s * 256 + 256)
                        dve.tensor_scalar(HT[:, k, o], PS[:, k, o], MA[:, s, k:k + 1],
                                          ADA[:, layer, part * KD + k, c:c + 1], ALU.mult, ALU.add)
        S.ready.done(nb)
        S.turned.done(KD)
        S.hop_a.done(1)
        S.hop_b.done(1)
        if rows is not None:
            rows_in.done(16)

    def gate_rows(layer, part, c):
        with nc.Block() as block:
            @block.vector
            def _(dve):
                for k in range(KD):
                    if k >= 2:
                        dve.wait_ge(S.made.sem, S.made.at(k - 1))
                    dve.tensor_scalar(DG[:, k % 2, :], ident, ADA[:, layer, part * KD + k, c:c + 1], None,
                                      ALU.mult).then_inc(S.ready.sem, 1)
                dve.wait_ge(S.made.sem, S.made.at(KD))
                for h in range(2):
                    dve.tensor_copy(GB[:, h * 512:(h + 1) * 512], PS[:, h, :])

            @block.tensor
            def _(pe):
                for k in range(KD):
                    pe.wait_ge(S.ready.sem, S.ready.at(k + 1))
                    pe.matmul(PS[:, k // 4, k % 4 * PB:(k % 4 + 1) * PB], ones, DG[:, k % 2, :], start=True,
                              stop=True).then_inc(S.made.sem, 1)
        S.ready.done(KD)
        S.made.done(KD)

    def turn(src, tiles, nb, dst, scale=None):
        with nc.Block() as block:
            @block.tensor
            def _(pe):
                for k in range(tiles):
                    for b in range(nb):
                        t = pe.transpose(PS[:, k, b * PB:(b + 1) * PB], src(b)[:, k * PB:(k + 1) * PB], ident)
                    t.then_inc(S.turned.sem, 1)

            @block.vector
            def _(dve):
                for k in range(tiles):
                    dve.wait_ge(S.turned.sem, S.turned.at(k + 1))
                    if scale is None:
                        dve.tensor_copy(dst(k), PS[:, k, 0:nb * PB])
                    else:
                        dve.tensor_scalar(dst(k), PS[:, k, 0:nb * PB], scale(k), None, ALU.mult)
        S.turned.done(tiles)

    def linear(src, kt, n, blocks, store, first=0, cols_major=0):
        a = place.n
        ch = chunks(n)
        more = cols_major // WC
        jobs = [(i, c0, w, b) for i, (c0, w) in enumerate(ch) for b in blocks(c0)]
        tiles = [(len(ch) + i, m) for i in range(more) for m in range(WC // PB)]
        total = len(jobs) + len(tiles)
        with nc.Block() as block:
            @block.sync
            def _(sp):
                feed(sp, a + SLOTS, a + len(ch) + more + SLOTS)

            @block.tensor
            def _(pe):
                for q, (i, c0, w, b) in enumerate(jobs):
                    slot = (a + i) % SLOTS
                    if q == 0 or jobs[q - 1][0] != i:
                        arrived(pe, a + i)
                    if q >= 8:
                        pe.wait_ge(S.evacuated.sem, S.evacuated.at(q - 7))
                    for k in range(kt):
                        mm = pe.matmul(PS[:, q % 8, 0:w], src(k)[:, b * PB:(b + 1) * PB],
                                       RING[:, slot, k * w:(k + 1) * w], start=(k == 0), stop=(k == kt - 1))
                    mm.then_inc(S.made.sem, 1)
                for q, (i, m) in enumerate(tiles):
                    slot, q = (a + i) % SLOTS, q + len(jobs)
                    if m == 0:
                        arrived(pe, a + i)
                    if q >= 8:
                        pe.wait_ge(S.evacuated.sem, S.evacuated.at(q - 7))
                    for k in range(kt):
                        mm = pe.matmul(PS[:, q % 8, 0:T], RING[:, slot, k * WC + m * PB:k * WC + (m + 1) * PB],
                                       src(k)[:, 0:T], start=(k == 0), stop=(k == kt - 1))
                    mm.then_inc(S.made.sem, 1)

            @block.vector
            def _(dve):
                for q, (i, c0, w, b) in enumerate(jobs):
                    dve.wait_ge(S.made.sem, S.made.at(q + 1))
                    if q == len(jobs) - 1 or jobs[q + 1][0] != i:
                        dve.sem_inc(slot_used.sem, 1)
                    store(dve, PS[:, q % 8, 0:w], b, c0, w).then_inc(S.evacuated.sem, 1)
                for q, (i, m) in enumerate(tiles):
                    q += len(jobs)
                    dve.wait_ge(S.made.sem, S.made.at(q + 1))
                    if m == WC // PB - 1:
                        dve.sem_inc(slot_used.sem, 1)
                    store(dve, PS[:, q % 8, 0:T], None, q - len(jobs), T).then_inc(S.evacuated.sem, 1)
        S.made.done(total)
        S.evacuated.done(total)
        place.n += len(ch) + more

    def add_gated(x):
        def store(dve, ps, b, c0, w):
            t = AUX[:, 3072 + b % 2 * 512:3072 + b % 2 * 512 + w]
            dve_step(dve, dve.tensor_tensor(t, ps, GB[:, c0:c0 + w], ALU.mult))
            return dve.tensor_tensor(x[:, b % 2, c0:c0 + w], x[:, b % 2, c0:c0 + w], t, ALU.add)
        return store

    def ffn_parts(x, f, o, gates=None):
        a, n = place.n, f // PB * (NE if gates is not None else 1)
        hid = [PS[:, 4 + p, :] for p in range(2)]
        silu = [Pb[:, p, 0:T] for p in range(2)]
        act_t = [Pb[:, p, T:2 * T] for p in range(2)]
        def products(pe):
            def up(c, j, g):
                s = (a + j) % SLOTS
                pe.wait_ge(slot_in[s].sem, g * 16 + 16 * ((a + j) // SLOTS + 1))
                if c is None or c >= 2:
                    pe.wait_ge(S.act_done.sem, g * SLOTS + S.act_done.at(j - 1))
                for half in range(2):
                    for k in range(KD):
                        mm = pe.matmul(hid[j % 2][:, half * T:(half + 1) * T],
                                       RING[:, s, half * D + k * PB:half * D + (k + 1) * PB],
                                       HT[:, k, o:o + T], start=(k == 0), stop=(k == KD - 1))
                mm.then_inc(S.up_done.sem, 1)

            def down(j, g, last=False):
                s = (a + j) % SLOTS
                pe.wait_ge(S.act_done.sem, g * SLOTS + S.act_done.at(j + 1))
                for b in range(2):
                    for h in range(2):
                        mm = pe.matmul(PS[:, 2 * b + h, :], act_t[j % 2][:, b * PB:(b + 1) * PB],
                                       RING[:, s, 2 * D + h * 512:2 * D + (h + 1) * 512],
                                       start=False, stop=last)
                mm.then_inc(slot_used.sem, 1)

            for bank in range(4):
                pe.matmul(PS[:, bank, :], Z16[:, 0:PB], Z16[:, :], start=True, stop=False)
            up(0, 0, 0)
            up(1, 1, 0)
            down(0, 0)
            rounds = (n - 2) // SLOTS
            with pe.Fori(0, rounds) as g:
                for j in range(SLOTS):
                    up(None, 2 + j, g)
                    down(1 + j, g)
            for c in range(rounds * SLOTS + 2, n):
                up(c, c, 0)
                down(c - 1, 0)
            down(n - 1, 0, last=True)

        def silus(act):
            def silu_of(j, g, late=True):
                act.wait_ge(S.up_done.sem, g * SLOTS + S.up_done.at(j + 1))
                if late:
                    act.wait_ge(S.act_done.sem, g * SLOTS + S.act_done.at(j - 1))
                act.activation(silu[j % 2], hid[j % 2][:, 0:T], ACT.Silu).then_inc(S.silu_done.sem, 1)
            silu_of(0, 0, False)
            silu_of(1, 0, False)
            rounds = (n - 2) // SLOTS
            with act.Fori(0, rounds) as g:
                for j in range(2, 2 + SLOTS):
                    silu_of(j, g)
            for c in range(rounds * SLOTS + 2, n):
                silu_of(c, 0)

        def gating(dve):
            def mul(j, g, late=True, e=None):
                dve.wait_ge(S.silu_done.sem, g + S.silu_done.at(j + 1))
                if late:
                    dve.wait_ge(slot_used.sem, g + (a + j - 1))
                if gates is None:
                    dve.tensor_tensor(act_t[j % 2], silu[j % 2], hid[j % 2][:, T:2 * T],
                                      ALU.mult).then_inc(S.act_done.sem, 1)
                    return
                dve.tensor_tensor(PT[:, j % 2, 0:T], silu[j % 2], hid[j % 2][:, T:2 * T],
                                  ALU.mult).then_inc(hidden_made.sem, 1)
                dve.wait_ge(hidden_made.sem, g + (j + 1))
                gate = gates[:, bass.ds(e, 1), :].rearrange("p o t -> p (o t)")
                dve.tensor_tensor(act_t[j % 2], PT[:, j % 2, 0:T], gate, ALU.mult).then_inc(S.act_done.sem, 1)
            if gates is None:
                mul(0, 0, False)
                mul(1, 0, False)
                rounds = (n - 2) // SLOTS
                with dve.Fori(0, rounds) as g:
                    for j in range(2, 2 + SLOTS):
                        mul(j, g * SLOTS)
                for c in range(rounds * SLOTS + 2, n):
                    mul(c, 0)
            else:
                with dve.Fori(0, NE) as e:
                    with dve.Fori(0, f // PB // SLOTS) as g:
                        for j in range(SLOTS):
                            mul(j, e * (f // PB) + g * SLOTS, True, e)
            dve.wait_ge(slot_used.sem, a + n)
            for b in range(2):
                for h in range(2):
                    t = AUX[:, (2 * b + h) * 512:(2 * b + h + 1) * 512]
                    dve_step(dve, dve.tensor_tensor(t, PS[:, 2 * b + h, :], GB[:, h * 512:(h + 1) * 512], ALU.mult))
                    xo = x[:, b, h * 512:(h + 1) * 512]
                    dve.tensor_tensor(xo, xo, t, ALU.add)
        return products, silus, gating

    def ffn(x, f, o):
        a, n = place.n, f // PB
        products, silus, gating = ffn_parts(x, f, o)
        with nc.Block() as block:
            @block.sync
            def _(sp):
                feed(sp, a + SLOTS, a + n + SLOTS)

            @block.tensor
            def _(pe):
                products(pe)

            @block.scalar
            def _(act):
                silus(act)

            @block.vector
            def _(dve):
                gating(dve)
        place.n += n
        for s in (S.up_done, S.silu_done, S.act_done):
            s.done(n)

    def moe_parts(he, put_t, fc):
        a = place.n
        hid = [PS[:, 6 + p, 0:2 * PB] for p in range(2)]
        silu = [Pb[:, p, 0:PB] for p in range(2)]
        act_t = [Pb[:, p, T:T + PB] for p in range(2)]
        oe = AUX[:, 2048:3072]
        flat = he.rearrange("p e k q -> p (e k q)")
        rounds = (fc - 2) // SLOTS

        def products(pe):
            def up(e, j, g=0):
                s = (a + j) % SLOTS
                pe.wait_ge(slot_in[s].sem, (e * (fc // SLOTS) + g) * 16 + 16 * ((a + j) // SLOTS + 1))
                pe.wait_ge(S.act_done.sem, e * fc + g * SLOTS + S.act_done.at(j - 1))
                for half in range(2):
                    for k in range(KD):
                        mm = pe.matmul(hid[j % 2][:, half * PB:(half + 1) * PB],
                                       RING[:, s, half * D + k * PB:half * D + (k + 1) * PB],
                                       flat[:, bass.ds(e * D + k * PB, PB)], start=(k == 0), stop=(k == KD - 1))
                mm.then_inc(S.up_done.sem, 1)

            def down(e, j, g=0, first=False, last=False):
                s = (a + j) % SLOTS
                pe.wait_ge(S.act_done.sem, e * fc + g * SLOTS + S.act_done.at(j + 1))
                for h in range(2):
                    mm = pe.matmul(PS[:, 4 + h, :], act_t[j % 2], RING[:, s, 2 * D + h * 512:2 * D + (h + 1) * 512],
                                   start=first, stop=last)
                mm.then_inc(slot_used.sem, 1)

            for bank in range(4):
                pe.matmul(PS[:, bank, :], Z16[:, 0:PB], Z16[:, :], start=True, stop=False)
            with pe.Fori(0, NE) as e:
                up(e, 0)
                up(e, 1)
                down(e, 0, first=True)
                with pe.Fori(0, rounds) as g:
                    for j in range(SLOTS):
                        up(e, 2 + j, g)
                        down(e, 1 + j, g)
                for c in range(rounds * SLOTS + 2, fc):
                    up(e, c)
                    down(e, c - 1)
                down(e, fc - 1, last=True)
                pe.wait_ge(expert_kept.sem, e + 1)
                for k in range(KD):
                    pe.matmul(PS[:, k // 2, k % 2 * T:(k % 2 + 1) * T], oe[:, k * PB:(k + 1) * PB],
                              put_t[:, bass.ds(e, 1), :].rearrange("p o t -> p (o t)"), start=False, stop=False,
                              skip_group_check=True)
            for bank in range(4):
                mm = pe.matmul(PS[:, bank, :], Z16[:, 0:PB], Z16[:, :], start=False, stop=True)
            mm.then_inc(expert_out.sem, 1)
            pe.wait_ge(expert_out.sem, 2)
            for b in range(2):
                for k in range(KD):
                    t = pe.transpose(PS[:, 4 + 2 * b + k // 4, k % 4 * PB:(k % 4 + 1) * PB],
                                     HT[:, k // 2, k % 2 * T + b * PB:k % 2 * T + (b + 1) * PB], ident)
            t.then_inc(expert_out.sem, 1)

        def silus(act):
            with act.Fori(0, NE) as e:
                with act.Fori(0, fc // SLOTS) as g:
                    for j in range(SLOTS):
                        at = e * fc + g * SLOTS
                        act.wait_ge(S.up_done.sem, at + S.up_done.at(j + 1))
                        act.wait_ge(S.act_done.sem, at + S.act_done.at(j - 1))
                        act.activation(silu[j % 2], hid[j % 2][:, 0:PB], ACT.Silu).then_inc(S.silu_done.sem, 1)

        def gating(dve):
            with dve.Fori(0, NE) as e:
                with dve.Fori(0, fc // SLOTS) as g:
                    for j in range(SLOTS):
                        at = e * fc + g * SLOTS
                        dve.wait_ge(S.silu_done.sem, at + S.silu_done.at(j + 1))
                        dve.wait_ge(slot_used.sem, at + (a + j - 1))
                        dve.tensor_tensor(act_t[j % 2], silu[j % 2], hid[j % 2][:, PB:2 * PB],
                                          ALU.mult).then_inc(S.act_done.sem, 1)
                dve.wait_ge(slot_used.sem, e * fc + (a + fc))
                dve.tensor_copy(oe, PS[:, 4:6, :].rearrange("p a n -> p (a n)")).then_inc(expert_kept.sem, 1)
            dve.wait_ge(expert_out.sem, 1)
            dve.tensor_copy(HT[:, 0:4, :], PS[:, 0:4, :]).then_inc(expert_out.sem, 1)
            dve.wait_ge(expert_out.sem, 3)
            for b in range(2):
                for h in range(2):
                    t = AUX[:, (2 * b + h) * 512:(2 * b + h + 1) * 512]
                    dve_step(dve, dve.tensor_tensor(t, PS[:, 4 + 2 * b + h, :], GB[:, h * 512:(h + 1) * 512], ALU.mult))
                    xo = X[:, b, h * 512:(h + 1) * 512]
                    dve.tensor_tensor(xo, xo, t, ALU.add)
        return products, silus, gating

    def head_norm(jobs):
        with nc.Block() as block:
            @block.vector
            def _(dve):
                for i, (v, gain, tmp, post) in enumerate(jobs):
                    h, w = v.shape[1], v.shape[2]
                    dve_step(dve, dve.tensor_tensor(tmp, v, v, ALU.mult))
                    dve.reduce_sum(SM[:, 32 + 16 * (i % 4):32 + 16 * (i % 4) + h], tmp, AX.X).then_inc(S.hop_a.sem, 1)
                    r = SM[:, 96 + 16 * (i % 4):96 + 16 * (i % 4) + h]
                    dve.wait_ge(S.hop_b.sem, S.hop_b.at(i + 1))
                    a = 16 * (i % 4)
                    dve_step(dve, refine(dve, r, SM[:, 32 + a:32 + a + h], SM[:, 160 + a:160 + a + h], w))
                    dve_step(dve, dve.tensor_tensor(v, v, r.unsqueeze(2).broadcast_to([PB, h, w]), ALU.mult))
                    if gain is not None:
                        dve_step(dve, dve.tensor_tensor(v, v, gain, ALU.mult))
                    if post is not None:
                        post(dve)

            @block.scalar
            def _(act):
                for i, (v, gain, tmp, post) in enumerate(jobs):
                    h, w = v.shape[1], v.shape[2]
                    act.wait_ge(S.hop_a.sem, S.hop_a.at(i + 1))
                    s = 16 * (i % 4)
                    act_step(act, act.activation(SM[:, 160 + s:160 + s + h], SM[:, 32 + s:32 + s + h], ACT.Ln,
                                                 bias=EPSC, scale=1.0 / w))
                    act.activation(SM[:, 96 + s:96 + s + h], SM[:, 160 + s:160 + s + h], ACT.Exp,
                                   scale=-0.5).then_inc(S.hop_b.sem, 1)
        S.hop_a.done(len(jobs))
        S.hop_b.done(len(jobs))

    def rope(dve, v, b, tab, tmp):
        q = v.shape[2] // 4
        h = v.shape[1]
        vv = v.rearrange("p h (a s q) -> p h a s q", a=2, s=2)
        x1, x2 = vv[:, :, :, 0, :], vv[:, :, :, 1, :]
        cs = [ROPE[:, b, i, tab:tab + 2 * q].rearrange("p (a q) -> p a q", a=2).unsqueeze(1)
              .broadcast_to([PB, h, 2, q]) for i in range(2)]
        t = [tmp[:, i * 512:i * 512 + h * 2 * q].rearrange("p (h a q) -> p h a q", h=h, a=2) for i in range(4)]
        dve_step(dve, dve.tensor_tensor(t[0], x1, cs[0], ALU.mult))
        dve_step(dve, dve.tensor_tensor(t[1], x2, cs[1], ALU.mult))
        dve_step(dve, dve.tensor_tensor(t[2], x1, cs[1], ALU.mult))
        dve_step(dve, dve.tensor_tensor(t[3], x2, cs[0], ALU.mult))
        dve_step(dve, dve.tensor_tensor(x1, t[0], t[1], ALU.subtract))
        dve_step(dve, dve.tensor_tensor(x2, t[2], t[3], ALU.add))

    def attention(heads, w, kb, scale, q_of, k_of, v_of, out_of, share=1, bias_of=None):
        units = [(h, b) for h in range(heads) for b in range(2)]
        n, nk = len(units), kb * PB
        top = {}
        for u, (h, b) in enumerate(units):
            top.setdefault(h, u)
        kcount = lambda h: h // share + 1
        with nc.Block() as block:
            @block.tensor
            def _(pe):
                def turn_kq(h):
                    if h >= 1:
                        pe.wait_ge(S.k_made.sem, S.k_made.at(kcount(h - 1)))
                        pe.wait_ge(S.q_made.sem, S.q_made.at(h))
                    if h % share == 0:
                        for j in range(kb):
                            t = pe.transpose(PS[0:w, 6, j * PB:(j + 1) * PB], k_of(h // share, j), ident)
                    for b in range(2):
                        t = pe.transpose(PS[0:w, 7, b * PB:(b + 1) * PB], q_of(h, b), ident)
                    t.then_inc(S.kq_turned.sem, 1)

                def score(u):
                    h, b = units[u]
                    pe.wait_ge(S.k_made.sem, S.k_made.at(kcount(h)))
                    pe.wait_ge(S.q_made.sem, S.q_made.at(h + 1))
                    if u >= 2:
                        pe.wait_ge(S.expd.sem, S.expd.at(u - 1))
                    pe.matmul(PS[:, u % 2, 0:nk], QT[0:w, h % 2, b * PB:(b + 1) * PB],
                              KT[0:w, h // share % 2, 0:nk], start=True, stop=True).then_inc(S.scored.sem, 1)

                def turn_p(u):
                    pe.wait_ge(S.expd.sem, S.expd.at(u + 1))
                    if u >= 2:
                        pe.wait_ge(S.p_copied.sem, S.p_copied.at(u - 1))
                    for j in range(kb):
                        t = pe.transpose(PS[:, 2 + u % 2, j * PB:(j + 1) * PB], Pb[:, u % 2, j * PB:(j + 1) * PB],
                                         ident)
                    t.then_inc(S.p_turned.sem, 1)

                def weigh(u):
                    h, b = units[u]
                    pe.wait_ge(S.p_copied.sem, S.p_copied.at(u + 1))
                    if u >= 2:
                        pe.wait_ge(S.scaled.sem, S.scaled.at(u - 1))
                    for j in range(kb):
                        mm = pe.matmul(PS[:, 4 + u % 2, 0:HD], PT[:, u % 2, j * PB:(j + 1) * PB],
                                       v_of(h // share, j), start=(j == 0), stop=(j == kb - 1))
                    mm.then_inc(S.summed.sem, 1)

                turn_kq(0)
                for t in range(n + 2):
                    if t < n:
                        score(t)
                        h, b = units[t]
                        if b == 1 and h + 1 < heads:
                            turn_kq(h + 1)
                    if 1 <= t <= n:
                        turn_p(t - 1)
                    if t >= 2:
                        weigh(t - 2)

            @block.vector
            def _(dve):
                def copy_k(h):
                    dve.wait_ge(S.kq_turned.sem, S.kq_turned.at(h + 1))
                    dve.tensor_copy(KT[0:w, h // share % 2, 0:nk], PS[0:w, 6, 0:nk]).then_inc(S.k_made.sem, 1)

                def top_of(u):
                    h, b = units[u]
                    m, nm = SM[:, 32 + u % 4:33 + u % 4], SM[:, 36 + u % 4:37 + u % 4]
                    dve.wait_ge(S.scored.sem, S.scored.at(u + 1))
                    s = PS[:, u % 2, 0:nk]
                    if bias_of is not None:
                        dve_step(dve, dve.scalar_tensor_tensor(out=s[:, 0:T], in0=s[:, 0:T], scalar=scale,
                                                               in1=bias_of(h, b), op0=ALU.mult, op1=ALU.add))
                        dve_step(dve, dve.tensor_scalar(s[:, T:nk], s[:, T:nk], scale, None, ALU.mult))
                    dve_step(dve, dve.tensor_reduce(m, s, AX.X, ALU.max))
                    dve.tensor_scalar(nm, m, -1.0 if bias_of is not None else -scale, None,
                                      ALU.mult).then_inc(S.maxed.sem, 1)

                def divide(u):
                    h, b = units[u]
                    dve.wait_ge(S.p_turned.sem, S.p_turned.at(u + 1))
                    r = SM[:, 48 + u % 4:49 + u % 4]
                    dve_step(dve, dve.reciprocal(r, SM[:, 40 + u % 4:41 + u % 4]))
                    dve.wait_ge(S.summed.sem, S.summed.at(u + 1))
                    dve.tensor_scalar(out_of(h, b), PS[:, 4 + u % 2, 0:HD], r, None, ALU.mult).then_inc(S.scaled.sem, 1)

                copy_k(0)
                for t in range(n + 2):
                    if t < n:
                        top_of(t)
                        h, b = units[t]
                        if b == 1 and h + 1 < heads and (h + 1) % share == 0:
                            copy_k(h + 1)
                    if t >= 2:
                        divide(t - 2)

            @block.scalar
            def _(act):
                def copy_q(h):
                    act.wait_ge(S.kq_turned.sem, S.kq_turned.at(h + 1))
                    act.activation(QT[0:w, h % 2, :], PS[0:w, 7, 0:T], ACT.Copy).then_inc(S.q_made.sem, 1)

                def exp(u):
                    act.wait_ge(S.maxed.sem, S.maxed.at(u + 1))
                    if u >= 2:
                        act.wait_ge(S.p_turned.sem, S.p_turned.at(u - 1))
                    if u >= 4:
                        act.wait_ge(S.scaled.sem, S.scaled.at(u - 3))
                    act.activation(Pb[:, u % 2, 0:nk], PS[:, u % 2, 0:nk], ACT.Exp, bias=SM[:, 36 + u % 4:37 + u % 4],
                                   scale=1.0 if bias_of is not None else scale,
                                   accum_out=SM[:, 40 + u % 4:41 + u % 4]).then_inc(S.expd.sem, 1)

                def copy_p(u):
                    act.wait_ge(S.p_turned.sem, S.p_turned.at(u + 1))
                    if u >= 2:
                        act.wait_ge(S.summed.sem, S.summed.at(u - 1))
                    act.activation(PT[:, u % 2, 0:nk], PS[:, 2 + u % 2, 0:nk], ACT.Copy).then_inc(S.p_copied.sem, 1)

                copy_q(0)
                for t in range(n + 1):
                    if t < n:
                        exp(t)
                        h, b = units[t]
                        if b == 1 and h + 1 < heads:
                            copy_q(h + 1)
                    if t >= 1:
                        copy_p(t - 1)
        S.kq_turned.done(heads)
        S.q_made.done(heads)
        S.k_made.done(heads // share)
        for s in (S.scored, S.maxed, S.expd, S.p_turned, S.p_copied, S.summed, S.scaled):
            s.done(n)

    xn = lambda b: XN[:, b, :]
    ht = lambda k: HT[:, k, :]

    L0 = 1536
    p0 = P[:, 0:4 * L0].rearrange("p (b n) -> p b n", b=4)

    def keep(p):
        def store(dve, ps, b, c0, w):
            return dve.tensor_copy(p[:, b, c0:c0 + w], ps)
        return store

    modulate([(X, 0, 0, 0), (XC, 0, 0, 1)], col("n_mix", 0, KD), rows=0)
    linear(ht, KD, L0, lambda c0: range(4), keep(p0))
    qk = [p0[:, b, 256:1280].rearrange("p (h w) -> p h w", w=HD) for b in range(4)]
    scr = HT[:, 0:2, :].rearrange("p a b -> p (a b)")
    rot = HT[:, 4:8, :].rearrange("p a b -> p (a b)")
    gain = row(0, "qk").rearrange("p (h w) -> p h w", w=HD)
    head_norm([(qk[b], gain, scr.rearrange("p (h w) -> p h w", w=HD),
                (lambda dve, b=b: (rope(dve, qk[b][:, 0:8, :], b, 0, rot), rope(dve, qk[b][:, 8:16, :], b, 0, rot)))
                if b < 2 else None) for b in range(4)])

    pool_m = AUX[:, 0:2048].rearrange("p (k g t) -> p k g t", k=2, g=4)
    pool_w = EX[0:64, 0:256]
    dT = EX[0:64, 512:2560].rearrange("p (g t) -> p g t", g=4)
    with nc.Block() as block:
        @block.scalar
        def _(act):
            act.dma_start(AUX[:, 0:2048], d["pool_m"]).then_inc(const_in.sem, 16)
            act.dma_start(pool_w, d["pool_w"]).then_inc(const_in.sem, 16)
            act.wait_ge(const_in.sem, 96)

        @block.tensor
        def _(pe):
            pe.wait_ge(const_in.sem, 96)
            for g in range(4):
                for s in range(2):
                    for k in range(2):
                        mm = pe.matmul(PS[0:64, g, s * T:(s + 1) * T], p0[:, 2 * s + k, g * 64:(g + 1) * 64],
                                       pool_m[:, k, g, :], start=(k == 0), stop=(k == 1))
                mm.then_inc(S.made.sem, 1)
            for g in range(4):
                pe.wait_ge(S.evacuated.sem, S.evacuated.at(g + 1))
                for b in range(4):
                    mm = pe.matmul(PS[:, 4 + b, g * 64:(g + 1) * 64], dT[:, g, b * PB:(b + 1) * PB],
                                   pool_w[:, g * 64:(g + 1) * 64], start=True, stop=True)
            mm.then_inc(S.made.sem, 1)

        @block.vector
        def _(dve):
            for g in range(4):
                dve.wait_ge(S.made.sem, S.made.at(g + 1))
                dve.tensor_copy(dT[:, g, :], PS[0:64, g, :]).then_inc(S.evacuated.sem, 1)
            dve.wait_ge(S.made.sem, S.made.at(5))
            for b in range(4):
                dve.tensor_tensor(XN[:, b, 0:256], PS[:, 4 + b, 0:256], row(0, "pool"), ALU.mult)
    S.made.done(5)
    S.evacuated.done(4)

    kv0 = lambda h, j: p0[:, (2, 3, 0, 1)[j], 1024 + h * HD:1024 + (h + 1) * HD]
    vv0 = lambda h, j: p0[:, (2, 3, 0, 1)[j], 1280 + h * HD:1280 + (h + 1) * HD]
    for s, kb in ((0, 4), (1, 2)):
        attention(12, HD, kb, HD ** -0.5, lambda h, b: p0[:, 2 * s + b, 256 + h * HD:256 + (h + 1) * HD], kv0, vv0,
                  lambda h, b: XN[:, 2 * s + b, 256 + h * HD:256 + (h + 1) * HD], share=3)
    turn(xn, KD, 4, lambda k: HT[:, k, 0:512])
    gate_rows(0, 2, 1)
    with nc.Block() as block:
        @block.vector
        def _(dve):
            dve.tensor_copy(EX[:, 0:D], GB[:, :])
    gate_rows(0, 2, 0)

    def store_both(dve, ps, b, c0, w):
        g, x = (GB, X) if b < 2 else (EX, XC)
        t = AUX[:, 3072 + b % 2 * 512:3072 + b % 2 * 512 + w]
        dve_step(dve, dve.tensor_tensor(t, ps, g[:, c0:c0 + w], ALU.mult))
        return dve.tensor_tensor(x[:, b % 2, c0:c0 + w], x[:, b % 2, c0:c0 + w], t, ALU.add)

    linear(ht, KD, D, lambda c0: range(4), store_both)
    checkpoint(nc, "l0_mix", X)
    modulate([(X, 0, 3, 0), (XC, 0, 3, 1)], col("n_ffn", 0, KD))
    gate_rows(0, 5, 0)
    ffn(X, F0, 0)
    gate_rows(0, 5, 1)
    ffn(XC, F0, T)
    checkpoint(nc, "l0", X)
    checkpoint(nc, "l0c", XC)

    p1 = P[:, :].rearrange("p (b n) -> p b n", b=4)
    modulate([(X, 1, 0, 0), (XC, 1, 0, 1)], col("n_mix", KD, KD), rows=1)
    linear(ht, KD, L1N, lambda c0: range(4) if c0 + WC > CKV else range(2), keep(p1))
    lat = XN[:, 0:2, :].rearrange("p a b -> p (a b)")
    cqT = lat[:, 0:768].rearrange("p (k t) -> p k t", k=3)
    ckvT = lat[:, 768:1792].rearrange("p (k t) -> p k t", k=2)
    tmp = XN[:, 2:4, :].rearrange("p a b -> p (a b)")
    nh = lambda v, w: v.rearrange("p (h w) -> p h w", w=w)
    head_norm([(nh(p1[:, b, CQ:CQ + 384], 384), None, nh(tmp[:, 0:384], 384), None) for b in range(2)]
              + [(nh(p1[:, b, CKV:CKV + 256], 256), None, nh(tmp[:, 0:256], 256), None) for b in range(4)]
              + [(nh(p1[:, b, NQ:NQ + 512], 64), nh(row(1, "qk")[:, 0:512], 64), nh(tmp[:, 0:512], 64), None)
                 for b in range(2)]
              + [(nh(p1[:, b, NK:NK + 512], 64), nh(row(1, "qk")[:, 512:1024], 64), nh(tmp[:, 0:512], 64), None)
                 for b in range(4)])
    turn(lambda b: p1[:, b, CQ:CQ + 384], 3, 2, lambda k: cqT[:, k, :], lambda k: col("qa", k))
    turn(lambda b: p1[:, b, CKV:CKV + 256], 2, 4, lambda k: ckvT[:, k, :], lambda k: col("kva", k))
    q96 = EX[:, 0:1536].rearrange("p (b n) -> p b n", b=2)
    k96 = EX[:, 1536:4608].rearrange("p (b n) -> p b n", b=4)
    kvp = HT[:, :, :].rearrange("p a b -> p (a b)").rearrange("p (b n) -> p b n", b=4)
    linear(lambda k: cqT[:, k, :], 3, 768, lambda c0: range(2), keep(q96))
    linear(lambda k: ckvT[:, k, :], 2, D, lambda c0: range(4), keep(kvp))
    with nc.Block() as block:
        @block.vector
        def _(dve):
            for b in range(4):
                k = nh(k96[:, b, :], 96)
                dve.tensor_copy(k[:, :, 0:64], nh(kvp[:, b, :], 128)[:, :, 0:64])
                dve.tensor_copy(k[:, :, 64:96], p1[:, b, KR:KR + 32].unsqueeze(1).broadcast_to([PB, 8, 32]))
    rot1 = lat
    t96 = nh(tmp[:, 0:768], 96)
    head_norm([(nh(q96[:, b, :], 96), nh(row(1, "mq"), 96), t96,
                (lambda dve, b=b: rope(dve, nh(q96[:, b, :], 96)[:, :, 64:96], b, 32, rot1))) for b in range(2)]
              + [(nh(k96[:, b, :], 96), nh(row(1, "mk"), 96), t96,
                  (lambda dve, b=b: rope(dve, nh(k96[:, b, :], 96)[:, :, 64:96], b, 32, rot1)) if b < 2 else None)
                 for b in range(4)])
    attention(8, 96, 4, 96 ** -0.5, lambda h, b: q96[:, b, h * 96:(h + 1) * 96],
              lambda h, j: k96[:, j, h * 96:(h + 1) * 96], lambda h, j: kvp[:, j, h * PB + 64:(h + 1) * PB],
              lambda h, b: XN[:, b, h * HD:(h + 1) * HD])
    bias = AUX[:, :].rearrange("p (h b k) -> p h b k", h=8, b=2)
    with nc.Block() as block:
        @block.scalar
        def _(act):
            act.dma_start(AUX[:, :], d["na_bias"]).then_inc(const_in.sem, 16)
            act.dma_start(EX[:, 0:512], d["na_mask"]).then_inc(const_in.sem, 16)
            act.wait_ge(const_in.sem, 128)

        @block.vector
        def _(dve):
            dve.wait_ge(const_in.sem, 128)
            m = EX[:, 0:512]
            for h in range(8):
                o = AUX[:, h * 512:(h + 1) * 512]
                dve.tensor_tensor(o, o, m, ALU.add)
    attention(8, HD, 4, HD ** -0.5, lambda h, b: p1[:, b, NQ + h * HD:NQ + (h + 1) * HD],
              lambda h, j: p1[:, j, NK + h * HD:NK + (h + 1) * HD],
              lambda h, j: p1[:, j, NV + h * HD:NV + (h + 1) * HD],
              lambda h, b: XN[:, b, 512 + h * HD:512 + (h + 1) * HD], bias_of=lambda h, b: bias[:, h, b, :])
    turn(xn, KD, 2, lambda k: HT[:, k, 0:T])
    gate_rows(1, 2, 0)
    linear(ht, KD, D, lambda c0: range(2), add_gated(X))
    checkpoint(nc, "l1_mix", X)
    modulate([(X, 1, 3, 0)], col("n_ffn", KD, KD))
    gate_rows(1, 5, 0)
    ffn(X, F0, 0)
    checkpoint(nc, "l1", X)

    p2 = P[:, 0:2 * L2N].rearrange("p (b n) -> p b n", b=2)
    U = XC[:, :, :].rearrange("p a b -> p (a b)")[:, 0:6 * 259].rearrange("p (c t) -> p c t", c=6)
    hx = HT[:, :, :].rearrange("p a b -> p (a b)")
    XB = hx[:, 0:1536].rearrange("p (c t) -> p c t", c=6)
    btok, SS = hx[:, 1536:1664], hx[:, 1664:1920]
    la, bb, eb, enb, ex, qe, ke, kt = (AUX[:, i * 512:(i + 1) * 512].rearrange("p (b n) -> p b n", b=2)
                                       for i in range(8))
    qkT = EX[0:64, 0:2048].rearrange("p (h n) -> p h n", h=4)
    att = EX[:, 2048:3072].rearrange("p (u n) -> p u n", u=8)
    st = EX[0:64, 3072:4608].rearrange("p (h c v) -> p h c v", h=4, c=3)
    og = XN[:, 2, :].rearrange("p (b n) -> p b n", b=2)
    xh = XN[:, 3, :].rearrange("p (b n) -> p b n", b=2)
    zs = P[:, 2 * L2N:2 * L2N + 1024].rearrange("p (b n) -> p b n", b=2)
    gs = P[:, 2 * L2N + 1024:2 * L2N + 2048].rearrange("p (b n) -> p b n", b=2)
    alT = GB[0:16, 0:T]
    aw = GB[0:16, T:2 * T]
    dec = SM[0:64, 200:216]

    for layer in range(2):
        ada = 2 + layer
        modulate([(X, ada, 0, 2)], col("n_mix", ada * KD, KD), rows=2 + layer)
        with nc.Block() as block:
            @block.vector
            def _(dve):
                dve.memset(U[:, :, 0:3], 0.0)

        def store2(dve, ps, b, c0, w):
            if b is None:
                return dve.tensor_copy(U[:, c0, 3:259], ps)
            return dve.tensor_copy(p2[:, b, c0:c0 + w], ps)
        linear(ht, KD, L2N, lambda c0: range(2), store2, cols_major=CONV)

        with nc.Block() as block:
            @block.scalar
            def _(act):
                act.dma_start(aw, d["gla_a_w"][layer]).then_inc(const_in.sem, 16)
                act.activation(gs[:, :, :], p2[:, :, GG:GG + 512], ACT.Silu)
                act.activation(zs[:, :, :], p2[:, :, SZ:SZ + 512], ACT.Silu)
                act.wait_ge(const_in.sem, 144 + 16 * layer)
                act.wait_ge(S.hop_a.sem, S.hop_a.at(1))
                act_step(act, act.activation(bb[:, :, :], la[:, :, :], ACT.Abs))
                act_step(act, act.activation(eb[:, :, :], bb[:, :, :], ACT.Exp, scale=-1.0))
                act.activation(enb[:, :, :], eb[:, :, :], ACT.Ln, bias=ONEC).then_inc(S.hop_b.sem, 1)
                act.wait_ge(S.made.sem, S.made.at(3))
                b_ps = PS[:, 4:6, 0:T]
                act.activation(dec, PS[0:64, 3, 0:16], ACT.Exp)
                act.wait_ge(S.hop_c.sem, S.hop_c.at(1))
                act.activation(eb[:, :, :], b_ps, ACT.Exp)
                act.activation(ex[:, :, :], ex[:, :, :], ACT.Exp)
                act_step(act, act.activation(enb[:, :, :], b_ps, ACT.Exp, scale=-1.0))

            @block.tensor
            def _(pe):
                for b in range(2):
                    t = pe.transpose(PS[0:16, 0, b * PB:(b + 1) * PB], p2[:, b, GA:GA + 16], ident)
                t.then_inc(S.made.sem, 1)
                pe.wait_ge(S.evacuated.sem, S.evacuated.at(1))
                pe.wait_ge(const_in.sem, 144 + 16 * layer)
                for b in range(2):
                    mm = pe.matmul(PS[:, 1 + b, 0:T], alT[:, b * PB:(b + 1) * PB], aw, start=True, stop=True)
                mm.then_inc(S.made.sem, 1)
                pe.wait_ge(S.hop_d.sem, S.hop_d.at(1))
                for b in range(2):
                    pe.matmul(PS[:, 4 + b, 0:T], trig, la[:, b, :], start=True, stop=True)
                    pe.matmul(PS[:, 6 + b, 0:T], blkg, la[:, b, :], start=True, stop=True)
                for c in range(4):
                    o = c % 2 * 64
                    for h in range(4):
                        mm = pe.matmul(PS[0:64, 3, c * 4 + h:c * 4 + h + 1], la[:, c // 2, h * 64:(h + 1) * 64],
                                       blkg[:, o:o + 1], start=True, stop=True)
                mm.then_inc(S.made.sem, 1)

            @block.vector
            def _(dve):
                dve.wait_ge(S.made.sem, S.made.at(1))
                dve.tensor_copy(alT, PS[0:16, 0, 0:T]).then_inc(S.evacuated.sem, 1)
                dve.wait_ge(S.made.sem, S.made.at(2))
                ab = row(2, "ab").unsqueeze(1).broadcast_to([PB, 2, T])
                dve.tensor_tensor(la[:, :, :], PS[:, 1:3, 0:T], ab, ALU.add).then_inc(S.hop_a.sem, 1)
                dve.wait_ge(S.hop_b.sem, S.hop_b.at(1))
                dve.scalar_tensor_tensor(out=la[:, :, :], in0=la[:, :, :], scalar=0.0, in1=enb[:, :, :], op0=ALU.min,
                                         op1=ALU.subtract).then_inc(S.hop_d.sem, 1)
                dve.wait_ge(S.made.sem, S.made.at(3))
                dve_step(dve, dve.tensor_copy(bb[:, :, :], PS[:, 4:6, 0:T]))
                dve.tensor_tensor(ex[:, :, :], PS[:, 6:8, 0:T], bb[:, :, :], ALU.subtract).then_inc(S.hop_c.sem, 1)
        S.made.done(3)
        for s in (S.evacuated, S.hop_a, S.hop_b, S.hop_c, S.hop_d):
            s.done(1)

        with nc.Block() as block:
            @block.vector
            def _(dve):
                dve_step(dve, dve.memset(att[:, :, :], 0.0))
                dve.scalar_tensor_tensor(out=qe[:, :, :], in0=p2[:, :, GQ:GQ + T], scalar=64 ** -0.5, in1=eb[:, :, :],
                                         op0=ALU.mult, op1=ALU.mult).then_inc(S.ready.sem, 1)
                dve.tensor_tensor(ke[:, :, :], p2[:, :, GK:GK + T], enb[:, :, :], ALU.mult).then_inc(S.ready.sem, 1)
                dve.tensor_tensor(kt[:, :, :], p2[:, :, GK:GK + T], ex[:, :, :], ALU.mult).then_inc(S.ready.sem, 1)
                for h in range(4):
                    dve.wait_ge(S.turned.sem, S.turned.at(h + 1))
                    dve.tensor_copy(qkT[:, h, :], PS[0:64, h, :]).then_inc(S.evacuated.sem, 1)
                for u in range(2):
                    dve.wait_ge(S.scored.sem, S.scored.at(u + 1))
                    for i in range(4):
                        cp = dve.copy_predicated(att[:, 4 * u + i, :], MKG[:, :], PS[:, 4 + u, i * PB:(i + 1) * PB])
                    cp.then_inc(S.hop_a.sem, 1)
                for h in range(4):
                    dve.wait_ge(S.summed.sem, S.summed.at(4 + h + 1))
                    dve_step(dve, dve.tensor_copy(st[:, h, 0, :], PS[0:64, h, 0:PB]))
                    for c in (1, 2):
                        dve_step(dve, dve.scalar_tensor_tensor(
                            out=st[:, h, c, :], in0=st[:, h, c - 1, :], scalar=dec[:, c * 4 + h:c * 4 + h + 1],
                            in1=PS[0:64, h, c * PB:(c + 1) * PB], op0=ALU.mult, op1=ALU.add))
                    dve.sem_inc(S.hop_b.sem, 1)
                for b in range(2):
                    dve.wait_ge(S.made.sem, S.made.at(b + 1))
                    dve.tensor_copy(og[:, b, :], PS[:, 6 + b, :])

            @block.tensor
            def _(pe):
                pe.wait_ge(S.ready.sem, S.ready.at(2))
                for h in range(4):
                    for i, src in enumerate((qe, ke)):
                        for b in range(2):
                            t = pe.transpose(PS[0:64, h, i * T + b * PB:i * T + (b + 1) * PB],
                                             src[:, b, h * 64:(h + 1) * 64], ident)
                    t.then_inc(S.turned.sem, 1)
                for u in range(8):
                    h, b = u // 2, u % 2
                    pe.wait_ge(S.evacuated.sem, S.evacuated.at(h + 1))
                    mm = pe.matmul(PS[:, 4 + u // 4, u % 4 * PB:(u % 4 + 1) * PB],
                                   qkT[:, h, T + b * PB:T + (b + 1) * PB], qkT[:, h, b * PB:(b + 1) * PB],
                                   start=True, stop=True)
                    if u % 4 == 3:
                        mm.then_inc(S.scored.sem, 1)
                pe.wait_ge(S.ready.sem, S.ready.at(3))
                for odd, h in ((odd, h) for odd in range(2) for h in range(4)):
                    if odd and h == 0:
                        pe.wait_ge(S.summed.sem, S.summed.at(4))
                    for c in ((0, 2), (1,))[odd]:
                        o = c % 2 * 64
                        mm = pe.matmul(PS[0:64, h, c * PB:(c + 1) * PB], kt[o:o + 64, c // 2, h * 64:(h + 1) * 64],
                                       p2[o:o + 64, c // 2, GV + h * PB:GV + (h + 1) * PB], start=True, stop=True)
                    mm.then_inc(S.summed.sem, 1)
                for b in range(2):
                    for h in range(4):
                        pe.wait_ge(S.hop_a.sem, S.hop_a.at(h // 2 + 1))
                        pe.wait_ge(S.hop_b.sem, S.hop_b.at(h + 1))
                        o = PS[:, 6 + b, h * PB:(h + 1) * PB]
                        mm = pe.matmul(o, att[:, 2 * h + b, :], p2[:, b, GV + h * PB:GV + (h + 1) * PB], start=True,
                                       stop=True)
                        for r in range(2):
                            c = 2 * b + r
                            if c == 0:
                                continue
                            mm = pe.matmul(o[r * 64:(r + 1) * 64, :], qkT[:, h, c * 64:(c + 1) * 64],
                                           st[:, h, c - 1, :], start=False, stop=True, skip_group_check=True)
                    mm.then_inc(S.made.sem, 1)
        for s, k in ((S.ready, 3), (S.turned, 4), (S.evacuated, 4), (S.scored, 2), (S.hop_a, 2), (S.summed, 8),
                     (S.hop_b, 4), (S.made, 2)):
            s.done(k)
        mixv = XN[:, 0:2, :]
        o4 = [og[:, b, :].rearrange("p (h v) -> p h v", h=4) for b in range(2)]
        gn = row(2, "gn").unsqueeze(1).broadcast_to([PB, 4, PB])
        sc4 = AUX[:, 0:512].rearrange("p (h v) -> p h v", h=4)

        def gated(dve, b):
            dve_step(dve, dve.tensor_tensor(mixv[:, b, 0:512], og[:, b, :], gs[:, b, :], ALU.mult))
        head_norm([(o4[b], gn, sc4, (lambda dve, b=b: gated(dve, b))) for b in range(2)])

        cw = lambda c, k: col("conv_w", layer * 24 + c * 4 + k)
        x8, dt, da, cum, ecum, el, dx = (SM[:, 32 + 16 * i:48 + 16 * i].rearrange("p (b h) -> p b h", b=2)
                                         for i in range(7))
        arow = SM[:, 150:158]
        t8, t8b = (SM[:, 160 + 16 * i:176 + 16 * i].rearrange("p (b h) -> p b h", b=2) for i in range(2))
        acc = EX[:, 0:1536].rearrange("p (c t) -> p c t", c=6)
        with nc.Block() as block:
            @block.vector
            def _(dve):
                dve.tensor_tensor(x8, p2[:, :, SDT:SDT + 8], row(2, "dtb").unsqueeze(1).broadcast_to([PB, 2, 8]),
                                  ALU.add).then_inc(S.hop_a.sem, 1)
                for c in range(6):
                    dve_step(dve, dve.tensor_scalar(acc[:, c, :], U[:, c, 0:T], cw(c, 0), None, ALU.mult))
                    for k in range(1, 4):
                        ins = dve.scalar_tensor_tensor(out=acc[:, c, :], in0=U[:, c, k:k + T], scalar=cw(c, k),
                                                       in1=acc[:, c, :], op0=ALU.mult, op1=ALU.add)
                        if k < 3:
                            dve_step(dve, ins)
                    ins.then_inc(S.ready.sem, 1)
                dve.wait_ge(S.hop_b.sem, S.hop_b.at(1))
                dve_step(dve, dve.scalar_tensor_tensor(out=dt, in0=x8, scalar=0.0, in1=t8b, op0=ALU.max, op1=ALU.add))
                dve.scalar_tensor_tensor(out=da, in0=dt, scalar=-1.0, in1=arow.unsqueeze(1).broadcast_to([PB, 2, 8]),
                                         op0=ALU.mult, op1=ALU.mult)

            @block.scalar
            def _(act):
                act.wait_ge(S.hop_a.sem, S.hop_a.at(1))
                act_step(act, act.activation(arow, row(2, "alog"), ACT.Exp))
                act_step(act, act.activation(t8, x8, ACT.Abs))
                act_step(act, act.activation(t8, t8, ACT.Exp, scale=-1.0))
                act.activation(t8b, t8, ACT.Ln, bias=ONEC).then_inc(S.hop_b.sem, 1)
                for c in range(6):
                    act.wait_ge(S.ready.sem, S.ready.at(c + 1))
                    act.activation(XB[:, c, :], acc[:, c, :], ACT.Silu, bias=col("conv_b", layer * 6 + c))
        S.hop_a.done(1)
        S.hop_b.done(1)
        S.ready.done(6)

        W = EX[:, 0:2048].rearrange("p (b h i) -> p b h i", b=2, h=8)
        seg = AUX[:, 0:2048].rearrange("p (b h i) -> p b h i", b=2, h=8)
        xdt = AUX[:, 2048:3072].rearrange("p (b n) -> p b n", b=2)
        xdt2 = AUX[:, 3072:3584]
        with nc.Block() as block:
            @block.tensor
            def _(pe):
                for b in range(2):
                    pe.matmul(PS[:, 2, b * 8:(b + 1) * 8], tri, da[:, b, :], start=True, stop=True)
                    mm = pe.matmul(PS[:, 2, 16 + b * 8:16 + (b + 1) * 8], ones, da[:, b, :], start=True, stop=True)
                mm.then_inc(S.made.sem, 1)
                for b in range(2):
                    for c in range(4):
                        t = pe.transpose(PS[:, b, c * PB:(c + 1) * PB], XB[:, c, b * PB:(b + 1) * PB], ident)
                t = pe.transpose(PS[:, 3, 0:PB], XB[:, 4, 0:PB], ident)
                t.then_inc(S.turned.sem, 1)
                for b in range(2):
                    for h in range(8):
                        mm = pe.matmul(PS[:, 4 + 2 * b + h // 4, h % 4 * PB:(h % 4 + 1) * PB],
                                       da[:, b, h:h + 1].broadcast_to([PB, PB]), tri, start=True, stop=True)
                    mm.then_inc(S.scored.sem, 1)

            @block.vector
            def _(dve):
                dve.wait_ge(S.made.sem, S.made.at(1))
                dve_step(dve, dve.tensor_copy(cum, PS[:, 2, 0:16].rearrange("p (b h) -> p b h", b=2)))
                dve.tensor_tensor(el, PS[:, 2, 16:32].rearrange("p (b h) -> p b h", b=2), cum,
                                  ALU.subtract).then_inc(S.hop_a.sem, 1)
                dve.wait_ge(S.turned.sem, S.turned.at(1))
                dve_step(dve, dve.tensor_copy(xh[:, :, :], PS[:, 0:2, :]))
                dve.tensor_copy(btok, PS[:, 3, 0:PB])
                for b in range(2):
                    xv = xh[:, b, :].rearrange("p (h w) -> p h w", h=8)
                    dve_step(dve, dve.tensor_tensor(xdt[:, b, :].rearrange("p (h w) -> p h w", h=8), xv,
                                                    dt[:, b, :].unsqueeze(2).broadcast_to([PB, 8, 64]), ALU.mult))
                for b in range(2):
                    dve.wait_ge(S.scored.sem, S.scored.at(b + 1))
                    for h in range(8):
                        ins = dve.scalar_tensor_tensor(out=seg[:, b, h, :],
                                                       in0=PS[:, 4 + 2 * b + h // 4, h % 4 * PB:(h % 4 + 1) * PB],
                                                       scalar=cum[:, b, h:h + 1], in1=negm, op0=ALU.subtract,
                                                       op1=ALU.add)
                    ins.then_inc(S.hop_b.sem, 1)
                dve.wait_ge(S.hop_c.sem, S.hop_c.at(1))
                dve.tensor_tensor(xdt2.rearrange("p (h w) -> p h w", h=8),
                                  xdt[:, 0, :].rearrange("p (h w) -> p h w", h=8),
                                  el[:, 0, :].unsqueeze(2).broadcast_to([PB, 8, 64]), ALU.mult)

            @block.scalar
            def _(act):
                act.wait_ge(S.hop_a.sem, S.hop_a.at(1))
                act.activation(ecum, cum, ACT.Exp)
                act.activation(el, el, ACT.Exp).then_inc(S.hop_c.sem, 1)
                for b in range(2):
                    act.wait_ge(S.hop_b.sem, S.hop_b.at(b + 1))
                    act.activation(seg[:, b, :, :], seg[:, b, :, :], ACT.Exp)
        for s in (S.made, S.turned, S.hop_a, S.hop_c):
            s.done(1)
        S.scored.done(2)
        S.hop_b.done(2)

        y = og
        dsk = row(2, "dskip").unsqueeze(2).broadcast_to([PB, 8, 64])
        with nc.Block() as block:
            @block.tensor
            def _(pe):
                for b in range(2):
                    for g in range(2):
                        r = slice(g * 64, (g + 1) * 64)
                        mm = pe.matmul(PS[:, 2 * b + g, 0:PB], XB[r, 4, b * PB:(b + 1) * PB],
                                       XB[r, 5, b * PB:(b + 1) * PB], start=True, stop=True)
                    mm.then_inc(S.scored.sem, 1)
                for g in range(2):
                    mm = pe.matmul(PS[g * 64:(g + 1) * 64, 7, 0:T], btok[:, g * 64:(g + 1) * 64],
                                   xdt2[:, g * T:(g + 1) * T], start=True, stop=True)
                mm.then_inc(S.summed.sem, 1)
                for b in range(2):
                    pe.wait_ge(S.hop_a.sem, S.hop_a.at(b + 1))
                    for h in range(8):
                        mm = pe.matmul(PS[:, 4 + b, h * 64:(h + 1) * 64], W[:, b, h, :],
                                       xdt[:, b, h * 64:(h + 1) * 64], start=True, stop=True)
                pe.wait_ge(S.evacuated.sem, S.evacuated.at(1))
                for g in range(2):
                    r = slice(g * 64, (g + 1) * 64)
                    mm = pe.matmul(PS[:, 6 + g, 0:T], XB[r, 5, PB:2 * PB], SS[r, :], start=True, stop=True)
                mm.then_inc(S.made.sem, 1)

            @block.vector
            def _(dve):
                for b in range(2):
                    dve.wait_ge(S.scored.sem, S.scored.at(b + 1))
                    for g in range(2):
                        sc = PS[:, 2 * b + g, 0:PB].unsqueeze(1).broadcast_to([PB, 4, PB])
                        ins = dve.tensor_tensor(W[:, b, 4 * g:4 * g + 4, :], seg[:, b, 4 * g:4 * g + 4, :], sc, ALU.mult)
                    ins.then_inc(S.hop_a.sem, 1)
                dve.wait_ge(S.summed.sem, S.summed.at(1))
                dve.tensor_copy(SS[:, :], PS[:, 7, 0:T]).then_inc(S.evacuated.sem, 1)
                h8 = lambda v: v.rearrange("p (h w) -> p h w", h=8)
                for b in range(2):
                    dve_step(dve, dve.tensor_tensor(h8(y[:, b, :]), h8(xh[:, b, :]), dsk, ALU.mult))
                dve.wait_ge(S.made.sem, S.made.at(1))
                for b in range(2):
                    dve_step(dve, dve.tensor_tensor(y[:, b, :], y[:, b, :], PS[:, 4 + b, :], ALU.add))
                t = seg[:, 0, 0:4, :].rearrange("p h i -> p (h i)")
                for g in range(2):
                    dve_step(dve, dve.tensor_tensor(
                        t[:, g * T:(g + 1) * T].rearrange("p (h w) -> p h w", h=4),
                        PS[:, 6 + g, 0:T].rearrange("p (h w) -> p h w", h=4),
                        ecum[:, 1, 4 * g:4 * g + 4].unsqueeze(2).broadcast_to([PB, 4, 64]), ALU.mult))
                dve_step(dve, dve.tensor_tensor(y[:, 1, :], y[:, 1, :], t, ALU.add))
                dve.tensor_tensor(y[:, :, :], y[:, :, :], zs[:, :, :], ALU.mult)
        S.scored.done(2)
        S.hop_a.done(2)
        for s in (S.summed, S.evacuated, S.made):
            s.done(1)

        def into_mix(dve, b):
            dve_step(dve, dve.tensor_tensor(mixv[:, b, 512:1024], y[:, b, :], row(2, "sn"), ALU.mult))
        head_norm([(nh(y[:, b, :], 512), None, nh(AUX[:, 2048:2560], 512), (lambda dve, b=b: into_mix(dve, b)))
                   for b in range(2)])
        turn(xn, KD, 2, lambda k: HT[:, k, 0:T])
        gate_rows(ada, 2, 2)
        linear(ht, KD, D, lambda c0: range(2), add_gated(X))
        checkpoint(nc, f"s{layer}_mix", X)
        modulate([(X, ada, 3, 2)], col("n_ffn", ada * KD, KD))
        gate_rows(ada, 5, 2)
        if layer == 0:
            ffn(X, F2, 0)
            checkpoint(nc, "s0", X)
            continue

        lg, ix, h1, h2, gates, sel, pos = (SM[:, 32 + 16 * i:48 + 16 * i].rearrange("p (b e) -> p b e", b=2)
                                           for i in range(7))
        m1, i1, m2, i2, pd = (SM[:, 144 + 2 * i:146 + 2 * i] for i in range(5))
        most = SM[0:1, 156:157]
        bc = lambda v: v.unsqueeze(2).broadcast_to([PB, 2, NE])
        it = iota[:, 0:NE].unsqueeze(1).broadcast_to([PB, 2, NE])
        gate_all = XC[:, :, :].rearrange("p a b -> p (a b)").rearrange("p (e t) -> p e t", e=NE)
        pick = EX[:, 0:2048].rearrange("p (b e q) -> p b e q", b=2, e=NE)
        put = AUX[:, 0:2048].rearrange("p (b e q) -> p b e q", b=2, e=NE)
        putT = EX[:, 2048:4096].rearrange("p (e t) -> p e t", e=NE)
        HE = P[:, 0:NE * D].rearrange("p (e k q) -> p e k q", e=NE, k=KD)
        with nc.Block() as block:
            @block.tensor
            def _(pe):
                for b in range(2):
                    for k in range(KD):
                        mm = pe.matmul(PS[:, 0, b * NE:(b + 1) * NE], HT[:, k, b * PB:(b + 1) * PB],
                                       col("router", k * NE, NE), start=(k == 0), stop=(k == KD - 1))
                mm.then_inc(S.made.sem, 1)
                for b in range(2):
                    for k in range(KD):
                        t = pe.transpose(PS[:, 4 + 2 * b + k // 4, k % 4 * PB:(k % 4 + 1) * PB],
                                         HT[:, k, b * PB:(b + 1) * PB], ident)
                t.then_inc(S.turned.sem, 1)
                pe.wait_ge(S.ready.sem, S.ready.at(1))
                pe.matmul(PS[:, 0, 0:NE], tri, sel[:, 0, :], start=True, stop=True)
                pe.matmul(PS[:, 0, NE:2 * NE], tri, sel[:, 1, :], start=True, stop=False)
                pe.matmul(PS[:, 0, NE:2 * NE], ones, sel[:, 0, :], start=False, stop=True)
                pe.matmul(PS[:, 0, 2 * NE:3 * NE], ones, sel[:, 0, :], start=True, stop=False)
                pe.matmul(PS[:, 0, 2 * NE:3 * NE], ones, sel[:, 1, :], start=False, stop=True).then_inc(S.made.sem, 1)

            @block.vector
            def _(dve):
                def step(ins):
                    dve_step(dve, ins)
                dve.wait_ge(S.made.sem, S.made.at(1))
                step(dve.tensor_copy(lg, PS[:, 0, 0:2 * NE].rearrange("p (b e) -> p b e", b=2)))
                for m, i, hot in ((m1, i1, h1), (m2, i2, h2)):
                    step(dve.tensor_reduce(m, lg, AX.X, ALU.max))
                    step(dve.tensor_tensor(ix, lg, bc(m), ALU.is_lt))
                    step(dve.scalar_tensor_tensor(out=ix, in0=ix, scalar=100.0, in1=it, op0=ALU.mult, op1=ALU.add))
                    step(dve.tensor_reduce(i, ix, AX.X, ALU.min))
                    step(dve.tensor_tensor(hot, it, bc(i), ALU.is_equal))
                    if m is m1:
                        step(dve.scalar_tensor_tensor(out=lg, in0=hot, scalar=-3.0e38, in1=lg, op0=ALU.mult,
                                                      op1=ALU.add))
                dve.tensor_tensor(sel, h1, h2, ALU.add).then_inc(S.ready.sem, 1)
                dve.tensor_tensor(pd, m2, m1, ALU.subtract).then_inc(S.hop_a.sem, 1)
                dve.wait_ge(S.hop_b.sem, S.hop_b.at(1))
                step(dve.tensor_scalar(m1, pd, 1.0, None, ALU.add))
                step(dve.reciprocal(m2, m1))
                step(dve.tensor_tensor(i1, m2, pd, ALU.mult))
                step(dve.tensor_tensor(h1, h1, bc(m2), ALU.mult))
                step(dve.tensor_tensor(h2, h2, bc(i1), ALU.mult))
                step(dve.tensor_tensor(gates, h1, h2, ALU.add))
                dve.wait_ge(S.made.sem, S.made.at(2))
                step(dve.tensor_scalar(pos, PS[:, 0, 0:2 * NE].rearrange("p (b e) -> p b e", b=2), -1.0, None, ALU.add))
                step(dve.tensor_reduce(most, PS[0:1, 0, 2 * NE:3 * NE], AX.X, ALU.max))
                dve.tensor_copy(COUNT[0:1, 0:1], most)
                for e in range(NE):
                    for b in range(2):
                        dve.tensor_scalar(pick[:, b, e, :], iota, pos[:, b, e:e + 1], sel[:, b, e:e + 1],
                                          ALU.is_equal, ALU.mult)
                        dve.tensor_scalar(put[:, b, e, :], iota, pos[:, b, e:e + 1], gates[:, b, e:e + 1],
                                          ALU.is_equal, ALU.mult)

            @block.scalar
            def _(act):
                act.wait_ge(S.turned.sem, S.turned.at(1))
                for b in range(2):
                    act.activation(XN[:, b, :], PS[:, 4 + 2 * b:6 + 2 * b, :].rearrange("p a n -> p (a n)"), ACT.Copy)
                act.wait_ge(S.hop_a.sem, S.hop_a.at(1))
                act.activation(pd, pd, ACT.Exp).then_inc(S.hop_b.sem, 1)
        S.made.done(2)
        for s in (S.ready, S.hop_a, S.hop_b, S.turned):
            s.done(1)

        with nc.Block() as block:
            @block.tensor
            def _(pe):
                for e in range(NE):
                    for b in range(2):
                        t = pe.transpose(PS[:, e // 2, e % 2 * T + b * PB:e % 2 * T + (b + 1) * PB],
                                         put[:, b, e, :], ident)
                t.then_inc(S.turned.sem, 1)
                for q in range(2 * KD):
                    k, half = q // 2, q % 2
                    if q >= 4:
                        pe.wait_ge(S.evacuated.sem, S.evacuated.at(q - 3))
                    for b in range(2):
                        mm = pe.matmul(PS[:, 4 + q % 4, :], XN[:, b, k * PB:(k + 1) * PB],
                                       pick[:, b, 4 * half:4 * half + 4, :].rearrange("p e q -> p (e q)"),
                                       start=(b == 0), stop=(b == 1))
                    mm.then_inc(S.made.sem, 1)
                pe.wait_ge(S.ready.sem, S.ready.at(1))
                for e in range(NE):
                    for b in range(2):
                        mm = pe.matmul(PS[:, e // 2, e % 2 * T + b * PB:e % 2 * T + (b + 1) * PB],
                                       gates[:, b, e:e + 1].broadcast_to([PB, PB]), ident, start=True, stop=True)
                mm.then_inc(S.turned.sem, 1)

            @block.vector
            def _(dve):
                for q in range(2 * KD):
                    k, half = q // 2, q % 2
                    dve.wait_ge(S.made.sem, S.made.at(q + 1))
                    dve.tensor_copy(HE[:, 4 * half:4 * half + 4, k, :],
                                    PS[:, 4 + q % 4, :].rearrange("p (e q) -> p e q", e=4)).then_inc(S.evacuated.sem, 1)

            @block.scalar
            def _(act):
                act.wait_ge(S.turned.sem, S.turned.at(1))
                for i in range(4):
                    c = act.activation(putT[:, 2 * i:2 * i + 2, :].rearrange("p e t -> p (e t)"), PS[:, i, :], ACT.Copy)
                c.then_inc(S.ready.sem, 1)
                act.wait_ge(S.turned.sem, S.turned.at(2))
                for i in range(4):
                    act.activation(gate_all[:, 2 * i:2 * i + 2, :].rearrange("p e t -> p (e t)"), PS[:, i, :], ACT.Copy)
        S.turned.done(2)
        S.ready.done(1)
        for s in (S.made, S.evacuated):
            s.done(2 * KD)

        a, fc = place.n, F2 // PB
        n = fc * NE
        gathered = moe_parts(HE, putT, fc)
        general = ffn_parts(X, F2, 0, gates=gate_all)
        with nc.Block() as block:
            @block.sync
            def _(sp):
                feed(sp, a + SLOTS, a + n + SLOTS)

            @block.tensor
            def _(pe):
                few = pe.value_load(COUNT[0:1, 0:1], min_val=0, max_val=T) <= PB
                with pe.If(few):
                    gathered[0](pe)
                with pe.Else():
                    general[0](pe)

            @block.scalar
            def _(act):
                few = act.value_load(COUNT[0:1, 0:1], min_val=0, max_val=T) <= PB
                with act.If(few):
                    gathered[1](act)
                with act.Else():
                    general[1](act)

            @block.vector
            def _(dve):
                few = dve.value_load(COUNT[0:1, 0:1], min_val=0, max_val=T) <= PB
                steps = dve_step.n
                with dve.If(few):
                    gathered[2](dve)
                dve_step.n = steps
                with dve.Else():
                    general[2](dve)
        place.n += n
        checkpoint(nc, "s1", X)

    with nc.Block() as block:
        @block.scalar
        def _(act):
            for b in range(2):
                act_step(act, act.activation(XN[:, b, :], X[:, b, :], ACT.Square, accum_out=SM[:, 8 + b:9 + b]))
            act_step(act, act.activation(SM[:, 12:14], SM[:, 8:10], ACT.Ln, bias=EPSC, scale=1.0 / D))
            act.activation(SM[:, 16:18], SM[:, 12:14], ACT.Exp, scale=-0.5).then_inc(S.hop_a.sem, 1)
            act.wait_ge(S.hop_b.sem, S.hop_b.at(1))
            for b in range(2):
                act.activation(XN[:, b, :], X[:, b, :], ACT.Copy, scale=SM[:, 16 + b:17 + b]).then_inc(S.ready.sem, 1)

        @block.vector
        def _(dve):
            dve.wait_ge(S.hop_a.sem, S.hop_a.at(1))
            refine(dve, SM[:, 16:18], SM[:, 8:10], SM[:, 20:22], D).then_inc(S.hop_b.sem, 1)
            for b in range(2):
                dve.wait_ge(S.ready.sem, S.ready.at(b + 1))
                dve.tensor_tensor(XN[:, b, :], XN[:, b, :], row(2, "fin"), ALU.mult).then_inc(S.made.sem, 1)

        @block.sync
        def _(sp):
            for b in range(2):
                sp.wait_ge(S.made.sem, S.made.at(b + 1))
                sp.dma_start(out[b * PB:(b + 1) * PB, :], XN[:, b, :]).then_inc(out_sem.sem, 16)
            sp.wait_ge(out_sem.sem, 32)


def checkpoint(nc, name, t):
    pass


def packed(w, cols=None):
    k, n = w.shape
    kt = k // PB
    out = np.zeros((len(chunks(n)), PB, kt * WC), w.dtype)
    for i, (a, c) in enumerate(chunks(n)):
        out[i, :, :kt * c] = w[:, a:a + c].reshape(kt, PB, c).transpose(1, 0, 2).reshape(PB, kt * c)
    return out


def packed_ffn(wg, wu, wd):
    f = wg.shape[1] // PB
    out = np.empty((f, PB, 3, D), wg.dtype)
    for i, w in enumerate((wg, wu)):
        out[:, :, i, :] = w.reshape(KD, PB, f, PB).transpose(2, 1, 0, 3).reshape(f, PB, D)
    out[:, :, 2, :] = wd.reshape(f, PB, D)
    return out.reshape(f, PB, 3 * D)


def columns(v):
    return np.ascontiguousarray(v.reshape(-1, PB).T)


def constants():
    f = np.float32
    t = np.arange(T)
    m = np.zeros((4, T, T), f)
    for g, w in enumerate((2, 4, 8, 16)):
        lo, hi = np.clip(t - w // 2, 0, T), np.clip(t - w // 2 + w, 0, T)
        for i in t:
            m[g, i, lo[i]:hi[i]] = f(1) / f(hi[i] - lo[i])
            m[g, i, i] -= 1
    pool = np.ascontiguousarray(m.transpose(2, 0, 1).reshape(2, PB, 4, T).transpose(1, 0, 2, 3).reshape(PB, 2048))
    i, j = np.arange(PB)[:, None], np.arange(PB)[None, :]
    same = i // 64 == j // 64
    sq = np.stack([i == j, i <= j, ((i <= j) & same) / 16, same / 16, np.where(i <= j, 0, NEG), np.ones((PB, PB)),
                   np.broadcast_to(j, (PB, PB))],
                  1).astype(f)
    rope = np.zeros((PB, 2, 2, 48), f)
    for b in range(2):
        tok = b * PB + np.arange(PB)
        for at, d in ((0, 32), (32, 16)):
            inv = (f(10000.0) ** (-np.arange(d // 2, dtype=f) * f(2.0) / f(d))).astype(f)
            for a, pos in enumerate((tok // GRID_W, tok % GRID_W)):
                ang = pos.astype(f)[:, None] * inv[None]
                s = slice(at + a * d // 2, at + (a + 1) * d // 2)
                rope[:, b, 0, s], rope[:, b, 1, s] = np.cos(ang), np.sin(ang)
    q = t.reshape(2, PB).T[:, :, None]
    k = t[None, None, :]
    c0 = np.clip(q % GRID_W - NA_COLS // 2, 0, GRID_W - NA_COLS)
    seen = (k % GRID_W >= c0) & (k % GRID_W < c0 + NA_COLS)
    dr = k // GRID_W - q // GRID_W + NA_ROWS - 1
    dc = np.clip(k % GRID_W - q % GRID_W + NA_COLS - 1, 0, 2 * NA_COLS - 2)
    na_mask = np.where(seen, 0, NEG).astype(f).reshape(PB, 512)
    return dict(pool_m=pool, squares=sq, rope=rope, na_mask=na_mask,
                mask_gla=((i <= j) & same).astype(np.int32)), dr, dc


def laid_out(i):
    i = {k: np.asarray(v) for k, v in i.items()}
    con, dr, dc = constants()
    a = dict(con)
    for n in ("x", "ctx"):
        a[n] = np.ascontiguousarray(i[n][0].reshape(2, PB, D).transpose(1, 0, 2))
    ada_w = [i["l0_ada_w"], i["l1_ada_w"], i["ada_w_2"][0], i["ada_w_2"][1]]
    a["ada"] = np.concatenate([packed(w) for w in ada_w])
    ada_b = np.concatenate([columns(b) for b in (i["l0_ada_b"], i["l1_ada_b"], i["ada_b_2"][0], i["ada_b_2"][1])], 1)
    a["l0_w_in"], a["l0_w_out"], a["l1_w_out"] = packed(i["l0_w_in"]), packed(i["l0_w_out"]), packed(i["l1_w_out"])
    for n in (0, 1):
        a[f"l{n}_ffn"] = packed_ffn(i[f"l{n}_ffn_w_gate"], i[f"l{n}_ffn_w_up"], i[f"l{n}_ffn_w_down"])
    cq, ckv, kr, nq, nk, nv = np.split(i["l1_w_in"], np.cumsum([384, 256, 32, 512, 512]), axis=1)
    a["l1_w_in"] = packed(np.concatenate([cq, nq, ckv, kr, nk, nv], 1))
    a["l1_uq"], a["l1_ukv"] = packed(i["l1_mla_w_uq"]), packed(i["l1_mla_w_ukv"])
    for n in (0, 1):
        q, k, v, g, al, z, xs, bm, cm, dt = np.split(i["w_in_2"][n], np.cumsum([256, 256, 512, 512, 16, 512, 512, 128,
                                                                             128]), axis=1)
        a[f"w_in{n}"] = np.concatenate([packed(np.concatenate([q, k, v, g, al, z, dt], 1)),
                                        packed(np.concatenate([xs, bm, cm], 1))])
        a[f"w_out{n}"] = packed(i["w_out_2"][n])
    a["ffn2"] = packed_ffn(i["ffn_w_gate_2"][0], i["ffn_w_up_2"][0], i["ffn_w_down_2"][0])
    moe = np.empty((NE * F2 // PB, PB, 3 * D), np.float32)
    for e in range(NE):
        moe[e * F2 // PB:(e + 1) * F2 // PB] = packed_ffn(i["moe_w_gate_2"][0, e], i["moe_w_up_2"][0, e],
                                                          i["moe_w_down_2"][0, e])
    a["moe"] = moe
    a["pool_w"] = np.ascontiguousarray(i["l0_pool_w"].transpose(1, 0, 2).reshape(64, 256))
    a["gla_a_w"] = i["gla_a_w_2"]
    rpb = i["l1_na_rpb"][:, dr, dc]
    a["na_bias"] = np.ascontiguousarray(rpb.transpose(1, 0, 2, 3).reshape(PB, 4096))
    cond = np.stack([columns(i["c"]), columns(i["c_ctx"]), columns(i["c_2"])], 2).reshape(PB, KD * 3)
    n_mix = [columns(v) for v in (i["l0_norm_mix"], i["l1_norm_mix"], i["norm1_w_2"])]
    n_ffn = [columns(v) for v in (i["l0_norm_ffn"], i["l1_norm_ffn"], i["norm2_w_2"])]
    conv_w = i["conv_w_2"].reshape(2, 4, 6, PB).transpose(3, 0, 2, 1).reshape(PB, 48)
    a["cols"] = np.ascontiguousarray(np.concatenate(
        [cond, ada_b, *n_mix, *n_ffn, columns(i["l1_mla_q_a_gain"]), columns(i["l1_mla_kv_a_gain"]), conv_w,
         columns(i["conv_b_2"]), i["router_w_2"][0].reshape(KD, PB, NE).transpose(1, 0, 2).reshape(PB, KD * NE)], 1))
    rows = np.zeros((4, ROWW), np.float32)

    def put(r, kind, name, v):
        at, w = ROWS[kind][name]
        rows[r, at:at + w] = v
    put(0, 0, "qk", np.concatenate([np.tile(i["l0_q_gain"], 12), np.tile(i["l0_k_gain"], 4)]))
    put(0, 0, "pool", i["l0_pool_scale"])
    put(1, 1, "qk", np.concatenate([np.tile(i["l1_na_q_gain"], 8), np.tile(i["l1_na_k_gain"], 8)]))
    put(1, 1, "mq", np.tile(i["l1_mla_q_gain"], 8))
    put(1, 1, "mk", np.tile(i["l1_mla_k_gain"], 8))
    for n in (0, 1):
        for name, v in (("ab", "gla_a_b_2"), ("gn", "gla_norm_w_2"), ("sn", "ssd_norm_w_2"), ("dtb", "dt_bias_2"),
                        ("alog", "a_log_2"), ("dskip", "d_skip_2")):
            put(2 + n, 2, name, i[v][n])
        put(2 + n, 2, "fin", i["final_norm_w_2"])
    a["rows"] = rows
    return a


def kernel(**inputs):
    import concourse.bacc as bacc
    from concourse.bass_utils import run_bass_kernel_spmd

    arrays = laid_out(inputs)
    nc = bacc.Bacc("TRN2", target_bir_lowering=False, num_devices=1)
    d = {n: nc.dram_tensor(n, v.shape, mybir.dt.from_np(v.dtype), kind="ExternalInput").ap() for n, v in arrays.items()}
    out = nc.dram_tensor("out", (T, D), F32, kind="ExternalOutput").ap()
    program(nc, d, out)
    r = run_bass_kernel_spmd(nc, [arrays], core_ids=[0])
    return r.results[0]["out"].reshape(1, T, D)
```

```python
from contextlib import ExitStack

import numpy as np
import concourse.bass as bass
from concourse import mybir

F32 = mybir.dt.float32
BF16 = mybir.dt.bfloat16
I32 = mybir.dt.int32
ALU = mybir.AluOpType
ACT = mybir.ActivationFunctionType
AX = mybir.AxisListType

D, T, PB = 1024, 256, 128
KD = D // PB
EPS = 1e-6
WC = 384
SLOT, SLOTS = KD * WC, 4
HD = 64
GRID_W, NA_COLS, NA_ROWS = 64, 16, 8
NEG = -1.0e30

CQ, NQ, CKV, KR, NK, NV, L1N = 0, 384, 896, 1152, 1184, 1696, 2208
GQ, GK, GV, GG, GA, SZ, SDT, L2N, CONV = 0, 256, 512, 1024, 1536, 1552, 2064, 2072, 768

F0, F2, NE = 2816, 3584, 8

ROWS = {
    0: dict(qk=(0, 1024), pool=(1024, 256)),
    1: dict(qk=(0, 1024), mq=(1024, 768), mk=(1792, 768)),
    2: dict(ab=(0, 256), gn=(256, 128), sn=(384, 512), dtb=(896, 8), alog=(904, 8), dskip=(912, 8),
            fin=(1024, 1024)),
}
ROWW = 2560
COLS, _at = {}, 0
for _n, _w in (("cond", KD * 3), ("ada_b", 4 * 48), ("n_mix", 4 * KD), ("n_ffn", 4 * KD), ("qa", 3),
               ("kva", 2), ("conv_w", 2 * 24), ("conv_b", 2 * 6), ("router", KD * NE)):
    COLS[_n] = (_at, _w)
    _at += _w
COLW = _at
SQ = ("ident", "tri", "trig", "blkg", "negm", "ones", "iota")


def chunks(n):
    return [(a, min(WC, n - a)) for a in range(0, n, WC)]


class Signal:

    def __init__(self, nc, ctx, name):
        self.sem = ctx.enter_context(nc.semaphore(name))
        self.base = 0

    def at(self, n):
        return self.base + n

    def done(self, n):
        self.base += n


class Place:

    n = 0


class Signals:

    def __init__(self, sig):
        self.ready = sig("ready")
        self.turned = sig("turned")
        self.evacuated = sig("evacuated")
        self.made = sig("made")
        self.scored = sig("scored")
        self.maxed = sig("maxed")
        self.expd = sig("expd")
        self.p_turned = sig("p_turned")
        self.p_copied = sig("p_copied")
        self.summed = sig("summed")
        self.scaled = sig("scaled")
        self.k_made = sig("k_made")
        self.q_made = sig("q_made")
        self.kq_turned = sig("kq_turned")
        self.up_done = sig("up_done")
        self.silu_done = sig("silu_done")
        self.act_done = sig("act_done")
        self.hop_a = sig("hop_a")
        self.hop_b = sig("hop_b")
        self.hop_c = sig("hop_c")
        self.hop_d = sig("hop_d")
        self.down_done = sig("down_done")
        self.hi_gu = sig("hi_gate_up")
        self.hi_d = sig("hi_down")
        self.gu_split = sig("gate_up_split")
        self.d_split = sig("down_split")
        self.prod = sig("product_made")
        self.act_hi = sig("hidden_hi")
        self.ada_rows = sig("ada_rows")
        self.ada_kept = sig("ada_kept")
        self.ada_cols = sig("ada_cols")
        self.ada_out = sig("ada_out")


class Chain:

    def __init__(self, nc, ctx, name):
        self.sem = ctx.enter_context(nc.semaphore(name))
        self.n = 0

    def __call__(self, eng, ins):
        self.n += 1
        ins.then_inc(self.sem, 1)
        eng.wait_ge(self.sem, self.n)


def program(nc, d, out):
    ctx = ExitStack()
    with ctx:
        build(nc, ctx, d, out)


def build(nc, ctx, d, out):
    def sb(name, shape, dt=F32):
        return ctx.enter_context(nc.sbuf_tensor(name, shape, dt))

    X, XC = sb("x_sb", [PB, 2, D]), sb("ctx_sb", [PB, 2, D])
    XN = sb("normed_or_mix", [PB, 4, D])
    HT = sb("turned", [PB, KD, 512])
    P = sb("projected", [PB, 4 * L1N])
    RING = sb("weights", [PB, SLOTS, SLOT])
    AUX = sb("aux", [PB, 4096])
    EX = sb("extra", [PB, 5120])
    Pb, PT = sb("probs", [PB, 2, 512]), sb("probs_turned", [PB, 2, 512])
    QT, KT = sb("q_turned", [PB, 2, 256]), sb("k_turned", [PB, 2, 512])
    GB = sb("gate_rows", [PB, D])
    ADA = sb("modulations", [PB, 4, 48, 3])
    MA = sb("mod_scale", [PB, 2, KD])
    ROW = sb("row_params", [PB, ROWW])
    COL = sb("column_params", [PB, COLW])
    CS = sb("silu_cond", [PB, KD, 3])
    SQT = sb("square_consts", [PB, len(SQ), PB])
    MKG = sb("gla_mask", [PB, PB], I32)
    ROPE = sb("rope_tables", [PB, 2, 2, 48])
    COUNT = sb("most_tokens", [1, 2], I32)
    SM = sb("small", [PB, 256])
    DG = sb("diag", [PB, 2, PB])
    Z16 = sb("zeros_bf16", [PB, 512], BF16)
    PS = ctx.enter_context(nc.psum_tensor("ps", [PB, 8, 512], F32))
    ident, tri, trig, blkg, negm, ones, iota = (SQT[:, i, :] for i in range(len(SQ)))

    def col(name, i=0, n=1):
        a = COLS[name][0] + i
        return COL[:, a:a + n]

    def row(kind, name):
        a, w = ROWS[kind][name]
        return ROW[:, a:a + w]

    def sig(name):
        return Signal(nc, ctx, name)

    dve_step, act_step = Chain(nc, ctx, "dve_step"), Chain(nc, ctx, "act_step")
    first_in, const_in, x_in, rows_in, out_sem = sig("first_in"), sig("const_in"), sig("x_in"), sig("rows_in"), sig("out_sent")
    slot_in = [sig(f"slot_in{i}") for i in range(SLOTS)]
    slot_used = sig("slot_used")
    hidden_made = sig("hidden_made")
    expert_kept, expert_out = sig("expert_kept"), sig("expert_out")
    S = Signals(sig)

    plan = []

    def planned(name, n, first=0):
        plan.extend((name, first + i) for i in range(n))

    planned("ada", 6)
    planned("l0_w_in", len(chunks(1536)))
    planned("ada", 13, 6)
    planned("l0_w_out", len(chunks(D)))
    planned("ada", 3, 19)
    planned("l0_ffn", F0 // PB)
    planned("l0_ffn", F0 // PB)
    planned("l1_w_in", len(chunks(L1N)))
    planned("ada", 12, 22)
    planned("l1_uq", 2)
    planned("l1_ukv", 3)
    planned("ada", 7, 34)
    planned("l1_w_out", len(chunks(D)))
    planned("ada", 3, 41)
    planned("l1_ffn", F0 // PB)
    for layer in range(2):
        planned(f"w_in{layer}", len(chunks(L2N)) + 2)
        planned("ada", 10, 44 + 10 * layer)
        planned(f"w_out{layer}", len(chunks(D)))
        planned("ffn2" if layer == 0 else "moe", F2 // PB * (1 if layer == 0 else NE))
    place = Place()

    def load(sp, src, n):
        s = n % SLOTS
        sp.dma_start(RING[:, s, 0:src.shape[1]], src).then_inc(slot_in[s].sem, 16)

    def feed(sp, lo, hi):
        hi = min(hi, len(plan))
        n = lo
        while n < hi:
            name, i = plan[n]
            run = 1
            while n + run < hi and plan[n + run] == (name, i + run):
                run += 1
            if run >= 2 * SLOTS:
                groups = run // SLOTS
                with sp.Fori(0, groups) as g:
                    for j in range(SLOTS):
                        if n >= SLOTS:
                            sp.wait_ge(slot_used.sem, g * SLOTS + (n - SLOTS + j + 1))
                        load(sp, d[name][bass.ds(g * SLOTS + (i + j), 1)].rearrange("o p w -> p (o w)"), n + j)
                n += groups * SLOTS
                continue
            if n >= SLOTS:
                sp.wait_ge(slot_used.sem, n - SLOTS + 1)
            load(sp, d[name][i], n)
            n += 1

    def arrived(eng, n):
        eng.wait_ge(slot_in[n % SLOTS].sem, 16 * (n // SLOTS + 1))

    with nc.Block() as block:
        @block.sync
        def _(sp):
            sp.dma_start(COL[:, :], d["cols"]).then_inc(first_in.sem, 16)
            sp.dma_start(SQT[:, :, :], d["squares"]).then_inc(first_in.sem, 16)
            for n in range(SLOTS):
                load(sp, d["ada"][n], n)
            sp.wait_ge(first_in.sem, 32)

        @block.scalar
        def _(act):
            act.wait_ge(first_in.sem, 32)
            act_step(act, act.activation(CS[:, :, :].rearrange("p a b -> p (a b)"), col("cond", 0, 3 * KD), ACT.Silu))

        @block.vector
        def _(dve):
            dve_step(dve, dve.memset(Z16[:, :], 0.0))
            dve_step(dve, dve.memset(SM[:, :], 0.0))
            dve_step(dve, dve.memset(SM[:, 0:1], EPS))
            dve_step(dve, dve.memset(SM[:, 1:2], 1.0))
    EPSC, ONEC = SM[:, 0:1], SM[:, 1:2]

    per = WC // PB
    adar = GB[0:3, 0:2 * WC].rearrange("p (j n) -> p j n", j=2)
    ada = ADA[:, :, :, :].rearrange("p l t c -> p (l t) c")

    def ada_products(pe, n):
        a = place.n

        def rows(i):
            arrived(pe, a + i)
            if i >= 2:
                pe.wait_ge(S.ada_kept.sem, S.ada_kept.at(i - 1))
            for k in range(KD):
                mm = pe.matmul(PS[0:3, 5 + i % 2, 0:WC], CS[:, k, :], RING[:, (a + i) % SLOTS, k * WC:(k + 1) * WC],
                               start=(k == 0), stop=(k == KD - 1))
            mm.then_inc(S.ada_rows.sem, 1)

        rows(0)
        for i in range(n):
            if i + 1 < n:
                rows(i + 1)
            pe.wait_ge(S.ada_kept.sem, S.ada_kept.at(i + 1))
            if i >= 1:
                pe.wait_ge(S.ada_out.sem, S.ada_out.at(i))
            for m in range(per):
                t = pe.matmul(PS[:, 7, 4 * m:4 * m + 3], adar[:, i % 2, m * PB:(m + 1) * PB], ident[0:3, 0:3],
                              start=True, stop=True)
            t.then_inc(S.ada_cols.sem, 1)

    def ada_copies(act, i):
        c = plan[place.n + i][1]
        act.wait_ge(S.ada_rows.sem, S.ada_rows.at(i + 1))
        if i >= 2:
            act.wait_ge(S.ada_cols.sem, S.ada_cols.at(i - 1))
        act.sem_inc(slot_used.sem, 1)
        act.activation(adar[:, i % 2, :], PS[0:3, 5 + i % 2, 0:WC], ACT.Copy).then_inc(S.ada_kept.sem, 1)
        act.wait_ge(S.ada_cols.sem, S.ada_cols.at(i + 1))
        act.activation(ada[:, c * per:(c + 1) * per, :],
                       PS[:, 7, 0:4 * per].rearrange("p (m c) -> p m c", c=4)[:, :, 0:3],
                       ACT.Copy).then_inc(S.ada_out.sem, 1)

    def ada_bias(dve, n):
        c = plan[place.n][1]
        o = ada[:, c * per:(c + n) * per, :]
        dve.wait_ge(S.ada_out.sem, S.ada_out.at(n))
        dve.tensor_tensor(o, o, col("ada_b", c * per, n * per).unsqueeze(2).broadcast_to([PB, n * per, 3]), ALU.add)

    def ada_done(n):
        place.n += n
        for s in (S.ada_rows, S.ada_kept, S.ada_cols, S.ada_out):
            s.done(n)

    def feed_batch(block, n):
        @block.sync
        def _(sp):
            feed(sp, place.n + SLOTS, place.n + n + SLOTS)

    with nc.Block() as block:
        feed_batch(block, 6)

        @block.tensor
        def _(pe):
            ada_products(pe, 6)

        @block.scalar
        def _(act):
            act.dma_start(X[:, :, :], d["x"]).then_inc(x_in.sem, 16)
            act.dma_start(XC[:, :, :], d["ctx"]).then_inc(x_in.sem, 16)
            act.dma_start(MKG[:, :], d["mask_gla"]).then_inc(const_in.sem, 16)
            act.dma_start(ROPE[:, :, :, :], d["rope"]).then_inc(const_in.sem, 16)
            for i in range(6):
                ada_copies(act, i)
            act.wait_ge(const_in.sem, 32)
            act.wait_ge(x_in.sem, 32)

        @block.vector
        def _(dve):
            ada_bias(dve, 6)
    ada_done(6)

    def refine(dve, r, ss, t, n):
        dve_step(dve, dve.tensor_scalar(ss, ss, 1.0 / n, EPS, ALU.mult, ALU.add))
        dve_step(dve, dve.tensor_tensor(t, r, r, ALU.mult))
        dve_step(dve, dve.tensor_tensor(t, t, ss, ALU.mult))
        dve_step(dve, dve.tensor_scalar(t, t, -0.5, 1.5, ALU.mult, ALU.add))
        return dve.tensor_tensor(r, r, t, ALU.mult)

    def modulate(streams, norm, rows=None, batch=0):
        nb = 2 * len(streams)
        xs = [st[0][:, b, :] for st in streams for b in range(2)]
        with nc.Block() as block:
            feed_batch(block, batch)

            @block.scalar
            def _(act):
                if rows is not None:
                    act.dma_start(ROW[:, :], d["rows"][rows].partition_broadcast(PB)).then_inc(rows_in.sem, 16)
                for b in range(0, nb, 2):
                    act_step(act, act.activation(XN[:, b, :], xs[b], ACT.Square, accum_out=SM[:, 8 + b:9 + b]))
                act.wait_ge(S.hop_c.sem, S.hop_c.at(nb // 2))
                act_step(act, act.activation(SM[:, 12:12 + nb], SM[:, 8:8 + nb], ACT.Ln, bias=EPSC, scale=1.0 / D))
                act.activation(SM[:, 16:16 + nb], SM[:, 12:12 + nb], ACT.Exp, scale=-0.5).then_inc(S.hop_a.sem, 1)
                act.wait_ge(S.hop_b.sem, S.hop_b.at(1))
                for b in range(0, nb, 2):
                    act.activation(XN[:, b, :], xs[b], ACT.Copy, scale=SM[:, 16 + b:17 + b]).then_inc(S.ready.sem, 1)
                for i in range(batch):
                    ada_copies(act, i)
                if rows is not None:
                    act.wait_ge(rows_in.sem, rows_in.at(16))

            @block.tensor
            def _(pe):
                if batch:
                    ada_products(pe, batch)
                    pe.wait_ge(S.ada_out.sem, S.ada_out.at(batch))
                pe.wait_ge(S.ready.sem, S.ready.at(nb // 2))
                pe.wait_ge(S.hop_c.sem, S.hop_c.at(nb))
                for k in range(KD):
                    for b in range(nb):
                        t = pe.transpose(PS[:, k, b * PB:(b + 1) * PB], XN[:, b, k * PB:(k + 1) * PB], ident)
                    t.then_inc(S.turned.sem, 1)

            @block.vector
            def _(dve):
                for b in range(1, nb, 2):
                    dve_step(dve, dve.tensor_tensor(XN[:, b, :], xs[b], xs[b], ALU.mult))
                    dve.reduce_sum(SM[:, 8 + b:9 + b], XN[:, b, :], AX.X).then_inc(S.hop_c.sem, 1)
                dve.wait_ge(S.hop_a.sem, S.hop_a.at(1))
                refine(dve, SM[:, 16:16 + nb], SM[:, 8:8 + nb], SM[:, 20:20 + nb], D).then_inc(S.hop_b.sem, 1)
                dve.wait_ge(S.hop_b.sem, S.hop_b.at(1))
                for b in range(1, nb, 2):
                    dve.tensor_scalar(XN[:, b, :], xs[b], SM[:, 16 + b:17 + b], None, ALU.mult).then_inc(S.hop_c.sem, 1)
                for s, (_, layer, part, c) in enumerate(streams):
                    dve_step(dve, dve.scalar_tensor_tensor(
                        out=MA[:, s, :], in0=ADA[:, layer, (part + 1) * KD:(part + 2) * KD, c], scalar=1.0,
                        in1=norm, op0=ALU.add, op1=ALU.mult))
                for k in range(KD):
                    dve.wait_ge(S.turned.sem, S.turned.at(k + 1))
                    for s, (_, layer, part, c) in enumerate(streams):
                        o = slice(s * 256, s * 256 + 256)
                        dve.tensor_scalar(HT[:, k, o], PS[:, k, o], MA[:, s, k:k + 1],
                                          ADA[:, layer, part * KD + k, c:c + 1], ALU.mult, ALU.add)
                if batch:
                    ada_bias(dve, batch)
        S.ready.done(nb // 2)
        S.hop_c.done(nb)
        S.turned.done(KD)
        ada_done(batch)
        S.hop_a.done(1)
        S.hop_b.done(1)
        if rows is not None:
            rows_in.done(16)

    def gate_rows(layer, part, c):
        with nc.Block() as block:
            @block.vector
            def _(dve):
                for k in range(KD):
                    if k >= 2:
                        dve.wait_ge(S.made.sem, S.made.at(k - 1))
                    dve.tensor_scalar(DG[:, k % 2, :], ident, ADA[:, layer, part * KD + k, c:c + 1], None,
                                      ALU.mult).then_inc(S.ready.sem, 1)
                dve.wait_ge(S.made.sem, S.made.at(KD))
                for h in range(2):
                    dve.tensor_copy(GB[:, h * 512:(h + 1) * 512], PS[:, h, :])

            @block.tensor
            def _(pe):
                for k in range(KD):
                    pe.wait_ge(S.ready.sem, S.ready.at(k + 1))
                    pe.matmul(PS[:, k // 4, k % 4 * PB:(k % 4 + 1) * PB], ones, DG[:, k % 2, :], start=True,
                              stop=True).then_inc(S.made.sem, 1)
        S.ready.done(KD)
        S.made.done(KD)

    def turn(src, tiles, nb, dst, scale=None):
        with nc.Block() as block:
            @block.tensor
            def _(pe):
                for k in range(tiles):
                    for b in range(nb):
                        t = pe.transpose(PS[:, k, b * PB:(b + 1) * PB], src(b)[:, k * PB:(k + 1) * PB], ident)
                    t.then_inc(S.turned.sem, 1)

            @block.vector
            def _(dve):
                for k in range(tiles):
                    dve.wait_ge(S.turned.sem, S.turned.at(k + 1))
                    if scale is None:
                        dve.tensor_copy(dst(k), PS[:, k, 0:nb * PB])
                    else:
                        dve.tensor_scalar(dst(k), PS[:, k, 0:nb * PB], scale(k), None, ALU.mult)
        S.turned.done(tiles)

    def linear(src, kt, n, blocks, store, first=0, cols_major=0):
        a = place.n
        ch = chunks(n)
        more = cols_major // WC
        jobs = [(i, c0, w, b) for i, (c0, w) in enumerate(ch) for b in blocks(c0)]
        tiles = [(len(ch) + i, m) for i in range(more) for m in range(WC // PB)]
        total = len(jobs) + len(tiles)
        with nc.Block() as block:
            @block.sync
            def _(sp):
                feed(sp, a + SLOTS, a + len(ch) + more + SLOTS)

            @block.tensor
            def _(pe):
                for q, (i, c0, w, b) in enumerate(jobs):
                    slot = (a + i) % SLOTS
                    if q == 0 or jobs[q - 1][0] != i:
                        arrived(pe, a + i)
                    if q >= 8:
                        pe.wait_ge(S.evacuated.sem, S.evacuated.at(q - 7))
                    for k in range(kt):
                        mm = pe.matmul(PS[:, q % 8, 0:w], src(k)[:, b * PB:(b + 1) * PB],
                                       RING[:, slot, k * w:(k + 1) * w], start=(k == 0), stop=(k == kt - 1))
                    mm.then_inc(S.made.sem, 1)
                for q, (i, m) in enumerate(tiles):
                    slot, q = (a + i) % SLOTS, q + len(jobs)
                    if m == 0:
                        arrived(pe, a + i)
                    if q >= 8:
                        pe.wait_ge(S.evacuated.sem, S.evacuated.at(q - 7))
                    for k in range(kt):
                        mm = pe.matmul(PS[:, q % 8, 0:T], RING[:, slot, k * WC + m * PB:k * WC + (m + 1) * PB],
                                       src(k)[:, 0:T], start=(k == 0), stop=(k == kt - 1))
                    mm.then_inc(S.made.sem, 1)

            @block.vector
            def _(dve):
                for q, (i, c0, w, b) in enumerate(jobs):
                    dve.wait_ge(S.made.sem, S.made.at(q + 1))
                    if q == len(jobs) - 1 or jobs[q + 1][0] != i:
                        dve.sem_inc(slot_used.sem, 1)
                    store(dve, PS[:, q % 8, 0:w], b, c0, w).then_inc(S.evacuated.sem, 1)
                for q, (i, m) in enumerate(tiles):
                    q += len(jobs)
                    dve.wait_ge(S.made.sem, S.made.at(q + 1))
                    if m == WC // PB - 1:
                        dve.sem_inc(slot_used.sem, 1)
                    store(dve, PS[:, q % 8, 0:T], None, q - len(jobs), T).then_inc(S.evacuated.sem, 1)
        S.made.done(total)
        S.evacuated.done(total)
        place.n += len(ch) + more

    def add_gated(x):
        def store(dve, ps, b, c0, w):
            t = AUX[:, 3072 + b % 2 * 512:3072 + b % 2 * 512 + w]
            dve_step(dve, dve.tensor_tensor(t, ps, GB[:, c0:c0 + w], ALU.mult))
            return dve.tensor_tensor(x[:, b % 2, c0:c0 + w], x[:, b % 2, c0:c0 + w], t, ALU.add)
        return store

    xnf = XN[:, :, :].rearrange("p a b -> p (a b)")
    spots = [xnf[:, i * 512:(i + 1) * 512] for i in range(8)] + [AUX[:, i * 512:(i + 1) * 512] for i in range(4)]
    split = [[[spots[6 * p + 2 * w + h].bitcast(BF16) for h in range(2)] for w in range(3)] for p in range(2)]
    hid_f = [PT[:, p, 0:T] for p in range(2)]
    hid_g = [PT[:, p, T:2 * T] for p in range(2)]
    hid_hl = [[Pb[:, p, T + h * PB:T + (h + 1) * PB].bitcast(BF16) for h in range(2)] for p in range(2)]
    silu = [Pb[:, p, 0:T] for p in range(2)]
    parity = lambda j: j % 2

    def cast_hi(act, which, j, n):
        a = place.n
        s = (a + j) % SLOTS
        act.wait_ge(slot_in[s].sem, (n - j) * (16 // SLOTS) + 16 * ((a + j) // SLOTS + 1))
        if which == 0:
            act.wait_ge(S.up_done.sem, n + S.up_done.at(1))
            for w in range(2):
                c = act.activation(split[parity(j)][w][0], RING[:, s, w * D:(w + 1) * D], ACT.Copy)
            c.then_inc(S.hi_gu.sem, 1)
        else:
            act.wait_ge(S.down_done.sem, n + S.down_done.at(1))
            act.activation(split[parity(j)][2][0], RING[:, s, 2 * D:3 * D], ACT.Copy).then_inc(S.hi_d.sem, 1)

    def make_lo(dve, which, j, n):
        s = (place.n + j) % SLOTS
        if which == 0:
            dve.wait_ge(S.hi_gu.sem, n + S.hi_gu.at(1))
            for w in range(2):
                c = dve.tensor_tensor(split[parity(j)][w][1], RING[:, s, w * D:(w + 1) * D], split[parity(j)][w][0],
                                      ALU.subtract)
            c.then_inc(S.gu_split.sem, 1)
        else:
            dve.wait_ge(S.hi_d.sem, n + S.hi_d.at(1))
            dve.tensor_tensor(split[parity(j)][2][1], RING[:, s, 2 * D:3 * D], split[parity(j)][2][0],
                              ALU.subtract).then_inc(slot_used.sem, 1)

    def up_products(pe, j, n, hid, width, h_hi, h_lo):
        pe.wait_ge(S.gu_split.sem, n + S.gu_split.at(1))
        pe.wait_ge(S.act_done.sem, n + S.act_done.at(1))
        for w in range(2):
            for k in range(KD):
                hi, lo = (split[parity(j)][w][h][:, k * PB:(k + 1) * PB] for h in range(2))
                o = hid[parity(j)][:, w * T:w * T + width]
                pe.matmul(o, hi, h_hi(k), start=(k == 0), stop=False)
                pe.matmul(o, hi, h_lo(k), start=False, stop=False)
                mm = pe.matmul(o, lo, h_hi(k), start=False, stop=(k == KD - 1))
        mm.then_inc(S.up_done.sem, 1)

    def down_products(pe, j, n, outs, start=False, stop=False):
        pe.wait_ge(slot_used.sem, n + (place.n + 1))
        pe.wait_ge(S.act_done.sem, n + S.act_done.at(3))
        hi, lo = (hid_hl[parity(j)][h] for h in range(2))
        w_hi, w_lo = split[parity(j)][2]
        for b, banks in outs:
            o = slice(b * PB, (b + 1) * PB)
            for h, bank in enumerate(banks):
                c = slice(h * 512, (h + 1) * 512)
                pe.matmul(PS[:, bank, :], hi[:, o], w_hi[:, c], start=start, stop=False)
                pe.matmul(PS[:, bank, :], hi[:, o], w_lo[:, c], start=False, stop=False)
                mm = pe.matmul(PS[:, bank, :], lo[:, o], w_hi[:, c], start=False, stop=stop)
        mm.then_inc(S.down_done.sem, 1)

    def silu_of(act, j, n, hid, width):
        act.wait_ge(S.up_done.sem, n + S.up_done.at(3))
        act.wait_ge(S.prod.sem, n + S.prod.at(1))
        act.activation(silu[parity(j)][:, 0:width], hid[parity(j)][:, 0:width], ACT.Silu).then_inc(S.silu_done.sem, 1)

    def gate_of(dve, j, n, hid, width, gate=None):
        p = parity(j)
        dve.wait_ge(S.silu_done.sem, n + S.silu_done.at(1))
        f = hid_f[p][:, 0:width]
        dve.tensor_tensor(f, silu[p][:, 0:width], hid[p][:, T:T + width], ALU.mult).then_inc(S.prod.sem, 1)
        dve.wait_ge(S.prod.sem, n + S.prod.at(3))
        if gate is not None:
            g = hid_g[p][:, 0:width]
            dve.tensor_tensor(g, f, gate, ALU.mult).then_inc(hidden_made.sem, 1)
            dve.wait_ge(hidden_made.sem, n + 1)
            f = g
        dve.wait_ge(S.down_done.sem, n + S.down_done.at(1))
        dve.tensor_copy(hid_hl[p][0][:, 0:width], f).then_inc(S.act_hi.sem, 1)
        dve.wait_ge(S.act_hi.sem, n + S.act_hi.at(1))
        dve.tensor_tensor(hid_hl[p][1][:, 0:width], f, hid_hl[p][0][:, 0:width],
                          ALU.subtract).then_inc(S.act_done.sem, 1)

    def ffn_done(n):
        place.n += n
        for s in (S.up_done, S.down_done, S.act_done, S.prod):
            s.done(n + 2)
        for s in (S.silu_done, S.act_hi, S.hi_gu, S.hi_d, S.gu_split):
            s.done(n)

    def ffn_parts(x, f, o, gates=None):
        a, n = place.n, f // PB * (NE if gates is not None else 1)
        hid = [PS[:, 4 + p, :] for p in range(2)]
        h_hi, h_lo = (P[:, i * 1024:(i + 1) * 1024].bitcast(BF16).rearrange("p (k t) -> p k t", k=KD)
                      for i in range(2))
        h = HT[:, :, o:o + T]
        outs = ((0, (0, 1)), (1, (2, 3)))
        rounds = (n - 2) // SLOTS

        def products(pe):
            for bank in range(4):
                pe.matmul(PS[:, bank, :], Z16[:, 0:PB], Z16[:, :], start=True, stop=False)
            pe.sem_inc(S.up_done.sem, 2)
            pe.sem_inc(S.down_done.sem, 2)
            pe.wait_ge(S.hop_d.sem, S.hop_d.at(2))

            def up(j, n):
                up_products(pe, j, n, hid, T, lambda k: h_hi[:, k, :], lambda k: h_lo[:, k, :])
            up(0, 0)
            with pe.Fori(0, rounds) as g:
                for j in range(SLOTS):
                    up(j + 1, g * SLOTS + (j + 1))
                    down_products(pe, j, g * SLOTS + j, outs)
            for c in range(rounds * SLOTS, n):
                if c + 1 < n:
                    up(c + 1, c + 1)
                down_products(pe, c, c, outs, stop=(c == n - 1))

        def silus(act):
            act.activation(h_hi, h, ACT.Copy).then_inc(S.hop_d.sem, 1)
            cast_hi(act, 0, 0, 0)
            cast_hi(act, 0, 1, 1)
            cast_hi(act, 1, 0, 0)
            with act.Fori(0, rounds) as g:
                for j in range(SLOTS):
                    silu_of(act, j, g * SLOTS + j, hid, T)
                    cast_hi_loop(act, 0, j + 2, g, 0)
                    cast_hi_loop(act, 1, j + 1, g, 0)
            for c in range(rounds * SLOTS, n):
                silu_of(act, c, c, hid, T)
                if c + 2 < n:
                    cast_hi(act, 0, c + 2, c + 2)
                if c + 1 < n:
                    cast_hi(act, 1, c + 1, c + 1)

        def gating(dve):
            dve.sem_inc(S.act_done.sem, 2)
            dve.sem_inc(S.prod.sem, 2)
            dve.wait_ge(S.hop_d.sem, S.hop_d.at(1))
            dve.tensor_tensor(h_lo, h, h_hi, ALU.subtract).then_inc(S.hop_d.sem, 1)
            make_lo(dve, 0, 0, 0)
            make_lo(dve, 0, 1, 1)
            make_lo(dve, 1, 0, 0)
            if gates is None:
                with dve.Fori(0, rounds) as g:
                    for j in range(SLOTS):
                        gate_of(dve, j, g * SLOTS + j, hid, T)
                        make_lo(dve, 0, j + 2, g * SLOTS + (j + 2))
                        make_lo(dve, 1, j + 1, g * SLOTS + (j + 1))
                for c in range(rounds * SLOTS, n):
                    gate_of(dve, c, c, hid, T)
                    if c + 2 < n:
                        make_lo(dve, 0, c + 2, c + 2)
                    if c + 1 < n:
                        make_lo(dve, 1, c + 1, c + 1)
            else:
                fc = f // PB
                def steps(e, j, c, more=2):
                    gate_of(dve, j, c, hid, T, gates[:, bass.ds(e, 1), :].rearrange("p o t -> p (o t)"))
                    if more > 1:
                        make_lo(dve, 0, j + 2, c + 2)
                    if more > 0:
                        make_lo(dve, 1, j + 1, c + 1)
                with dve.Fori(0, NE - 1) as e:
                    with dve.Fori(0, fc // SLOTS) as g:
                        for j in range(SLOTS):
                            steps(e, j, e * fc + g * SLOTS + j)
                with dve.Fori(0, fc // SLOTS - 1) as g:
                    for j in range(SLOTS):
                        steps(NE - 1, j, g * SLOTS + ((NE - 1) * fc + j))
                for j in range(SLOTS):
                    steps(NE - 1, j, n - SLOTS + j, SLOTS - 1 - j)
            dve.wait_ge(S.down_done.sem, S.down_done.at(n + 2))
            for b in range(2):
                for h_ in range(2):
                    t = AUX[:, (2 * b + h_) * 512:(2 * b + h_ + 1) * 512]
                    dve_step(dve, dve.tensor_tensor(t, PS[:, 2 * b + h_, :], GB[:, h_ * 512:(h_ + 1) * 512], ALU.mult))
                    xo = x[:, b, h_ * 512:(h_ + 1) * 512]
                    dve.tensor_tensor(xo, xo, t, ALU.add)
        return products, silus, gating

    def cast_hi_loop(act, which, j, g, before):
        a = place.n
        s = (a + j) % SLOTS
        n = g * SLOTS + (before + j)
        act.wait_ge(slot_in[s].sem, g * 16 + (before * (16 // SLOTS) + 16 * ((a + j) // SLOTS + 1)))
        if which == 0:
            act.wait_ge(S.up_done.sem, n + S.up_done.at(1))
            for w in range(2):
                c = act.activation(split[parity(j)][w][0], RING[:, s, w * D:(w + 1) * D], ACT.Copy)
            c.then_inc(S.hi_gu.sem, 1)
        else:
            act.wait_ge(S.down_done.sem, n + S.down_done.at(1))
            act.activation(split[parity(j)][2][0], RING[:, s, 2 * D:3 * D], ACT.Copy).then_inc(S.hi_d.sem, 1)

    def ffn(x, f, o):
        a, n = place.n, f // PB
        products, silus, gating = ffn_parts(x, f, o)
        with nc.Block() as block:
            @block.sync
            def _(sp):
                feed(sp, a + SLOTS, a + n + SLOTS)

            @block.tensor
            def _(pe):
                products(pe)

            @block.scalar
            def _(act):
                silus(act)

            @block.vector
            def _(dve):
                gating(dve)
        ffn_done(n)
        S.hop_d.done(2)

    def moe_parts(he_hi, he_lo, put_t, fc):
        a, n = place.n, fc * NE
        hid = [PS[:, 6 + p, :] for p in range(2)]
        oe = AUX[:, 2048:3072]
        outs = ((0, (4, 5)),)
        rounds = n // SLOTS - 1

        def products(pe):
            def up(e, j, c):
                up_products(pe, j, c, hid, PB, lambda k: he_hi[:, bass.ds(e * D + k * PB, PB)],
                            lambda k: he_lo[:, bass.ds(e * D + k * PB, PB)])

            def expert(e, last=False):
                at = e * fc
                for j in range(SLOTS):
                    up(e, j + 1, at + (j + 1))
                    down_products(pe, j, at + j, outs, start=(j == 0))
                with pe.Fori(1, fc // SLOTS - 1) as g:
                    for j in range(SLOTS):
                        up(e, j + 1, at + g * SLOTS + (j + 1))
                        down_products(pe, j, at + g * SLOTS + j, outs)
                for j in range(SLOTS):
                    c = fc - SLOTS + j
                    if j < SLOTS - 1:
                        up(e, c + 1, at + (c + 1))
                    elif not last:
                        up(e + 1, c + 1, at + (c + 1))
                    down_products(pe, c, at + c, outs, stop=(j == SLOTS - 1))
                pe.wait_ge(expert_kept.sem, e + 1)
                for k in range(KD):
                    pe.matmul(PS[:, k // 2, k % 2 * T:(k % 2 + 1) * T], oe[:, k * PB:(k + 1) * PB],
                              put_t[:, bass.ds(e, 1), :].rearrange("p o t -> p (o t)"), start=False, stop=False,
                              skip_group_check=True)

            for bank in range(4):
                pe.matmul(PS[:, bank, :], Z16[:, 0:PB], Z16[:, :], start=True, stop=False)
            pe.sem_inc(S.up_done.sem, 2)
            pe.sem_inc(S.down_done.sem, 2)
            up(0, 0, 0)
            with pe.Fori(0, NE - 1) as e:
                expert(e)
            expert(NE - 1, last=True)
            for bank in range(4):
                mm = pe.matmul(PS[:, bank, :], Z16[:, 0:PB], Z16[:, :], start=False, stop=True)
            mm.then_inc(expert_out.sem, 1)
            pe.wait_ge(expert_out.sem, 2)
            for b in range(2):
                for k in range(KD):
                    t = pe.transpose(PS[:, 4 + 2 * b + k // 4, k % 4 * PB:(k % 4 + 1) * PB],
                                     HT[:, k // 2, k % 2 * T + b * PB:k % 2 * T + (b + 1) * PB], ident)
            t.then_inc(expert_out.sem, 1)

        def silus(act):
            cast_hi(act, 0, 0, 0)
            cast_hi(act, 0, 1, 1)
            cast_hi(act, 1, 0, 0)
            with act.Fori(0, rounds) as g:
                for j in range(SLOTS):
                    silu_of(act, j, g * SLOTS + j, hid, PB)
                    cast_hi_loop(act, 0, j + 2, g, 0)
                    cast_hi_loop(act, 1, j + 1, g, 0)
            for c in range(rounds * SLOTS, n):
                silu_of(act, c, c, hid, PB)
                if c + 2 < n:
                    cast_hi(act, 0, c + 2, c + 2)
                if c + 1 < n:
                    cast_hi(act, 1, c + 1, c + 1)

        def gating(dve):
            def step(j, c, more=2):
                gate_of(dve, j, c, hid, PB)
                if more > 1:
                    make_lo(dve, 0, j + 2, c + 2)
                if more > 0:
                    make_lo(dve, 1, j + 1, c + 1)

            def keep_output(e):
                dve.wait_ge(S.down_done.sem, e * fc + S.down_done.at(fc + 2))
                dve.tensor_copy(oe, PS[:, 4:6, :].rearrange("p a n -> p (a n)")).then_inc(expert_kept.sem, 1)
            dve.sem_inc(S.act_done.sem, 2)
            dve.sem_inc(S.prod.sem, 2)
            make_lo(dve, 0, 0, 0)
            make_lo(dve, 0, 1, 1)
            make_lo(dve, 1, 0, 0)
            with dve.Fori(0, NE - 1) as e:
                with dve.Fori(0, fc // SLOTS) as g:
                    for j in range(SLOTS):
                        step(j, e * fc + g * SLOTS + j)
                keep_output(e)
            with dve.Fori(0, fc // SLOTS - 1) as g:
                for j in range(SLOTS):
                    step(j, g * SLOTS + ((NE - 1) * fc + j))
            for j in range(SLOTS):
                step(j, n - SLOTS + j, SLOTS - 1 - j)
            keep_output(NE - 1)
            dve.wait_ge(expert_out.sem, 1)
            dve.tensor_copy(HT[:, 0:4, :], PS[:, 0:4, :]).then_inc(expert_out.sem, 1)
            dve.wait_ge(expert_out.sem, 3)
            for b in range(2):
                for h in range(2):
                    t = AUX[:, (2 * b + h) * 512:(2 * b + h + 1) * 512]
                    dve_step(dve, dve.tensor_tensor(t, PS[:, 4 + 2 * b + h, :], GB[:, h * 512:(h + 1) * 512], ALU.mult))
                    xo = X[:, b, h * 512:(h + 1) * 512]
                    dve.tensor_tensor(xo, xo, t, ALU.add)
        return products, silus, gating

    def head_norm(jobs, batch=0):
        with nc.Block() as block:
            if batch:
                feed_batch(block, batch)

                @block.tensor
                def _(pe):
                    ada_products(pe, batch)

            @block.vector
            def _(dve):
                for i, (v, gain, tmp, post) in enumerate(jobs):
                    h, w = v.shape[1], v.shape[2]
                    dve_step(dve, dve.tensor_tensor(tmp, v, v, ALU.mult))
                    dve.reduce_sum(SM[:, 32 + 16 * (i % 4):32 + 16 * (i % 4) + h], tmp, AX.X).then_inc(S.hop_a.sem, 1)
                    r = SM[:, 96 + 16 * (i % 4):96 + 16 * (i % 4) + h]
                    dve.wait_ge(S.hop_b.sem, S.hop_b.at(i + 1))
                    a = 16 * (i % 4)
                    dve_step(dve, refine(dve, r, SM[:, 32 + a:32 + a + h], SM[:, 160 + a:160 + a + h], w))
                    dve_step(dve, dve.tensor_tensor(v, v, r.unsqueeze(2).broadcast_to([PB, h, w]), ALU.mult))
                    if gain is not None:
                        dve_step(dve, dve.tensor_tensor(v, v, gain, ALU.mult))
                    if post is not None:
                        post(dve)
                if batch:
                    ada_bias(dve, batch)

            @block.scalar
            def _(act):
                for i, (v, gain, tmp, post) in enumerate(jobs):
                    h, w = v.shape[1], v.shape[2]
                    act.wait_ge(S.hop_a.sem, S.hop_a.at(i + 1))
                    s = 16 * (i % 4)
                    act_step(act, act.activation(SM[:, 160 + s:160 + s + h], SM[:, 32 + s:32 + s + h], ACT.Ln,
                                                 bias=EPSC, scale=1.0 / w))
                    act.activation(SM[:, 96 + s:96 + s + h], SM[:, 160 + s:160 + s + h], ACT.Exp,
                                   scale=-0.5).then_inc(S.hop_b.sem, 1)
                    for c in range(batch * i // len(jobs), batch * (i + 1) // len(jobs)):
                        ada_copies(act, c)
        S.hop_a.done(len(jobs))
        ada_done(batch)
        S.hop_b.done(len(jobs))

    def rope(dve, v, b, tab, tmp):
        q = v.shape[2] // 4
        h = v.shape[1]
        vv = v.rearrange("p h (a s q) -> p h a s q", a=2, s=2)
        x1, x2 = vv[:, :, :, 0, :], vv[:, :, :, 1, :]
        cs = [ROPE[:, b, i, tab:tab + 2 * q].rearrange("p (a q) -> p a q", a=2).unsqueeze(1)
              .broadcast_to([PB, h, 2, q]) for i in range(2)]
        t = [tmp[:, i * 512:i * 512 + h * 2 * q].rearrange("p (h a q) -> p h a q", h=h, a=2) for i in range(4)]
        dve_step(dve, dve.tensor_tensor(t[0], x1, cs[0], ALU.mult))
        dve_step(dve, dve.tensor_tensor(t[1], x2, cs[1], ALU.mult))
        dve_step(dve, dve.tensor_tensor(t[2], x1, cs[1], ALU.mult))
        dve_step(dve, dve.tensor_tensor(t[3], x2, cs[0], ALU.mult))
        dve_step(dve, dve.tensor_tensor(x1, t[0], t[1], ALU.subtract))
        dve_step(dve, dve.tensor_tensor(x2, t[2], t[3], ALU.add))

    def attention(heads, w, kb, scale, q_of, k_of, v_of, out_of, share=1, bias_of=None):
        units = [(h, b) for h in range(heads) for b in range(2)]
        n, nk = len(units), kb * PB
        top = {}
        for u, (h, b) in enumerate(units):
            top.setdefault(h, u)
        kcount = lambda h: h // share + 1
        with nc.Block() as block:
            @block.tensor
            def _(pe):
                def turn_kq(h):
                    if h >= 1:
                        pe.wait_ge(S.k_made.sem, S.k_made.at(kcount(h - 1)))
                        pe.wait_ge(S.q_made.sem, S.q_made.at(h))
                    if h % share == 0:
                        for j in range(kb):
                            t = pe.transpose(PS[0:w, 6, j * PB:(j + 1) * PB], k_of(h // share, j), ident)
                    for b in range(2):
                        t = pe.transpose(PS[0:w, 7, b * PB:(b + 1) * PB], q_of(h, b), ident)
                    t.then_inc(S.kq_turned.sem, 1)

                def score(u):
                    h, b = units[u]
                    pe.wait_ge(S.k_made.sem, S.k_made.at(kcount(h)))
                    pe.wait_ge(S.q_made.sem, S.q_made.at(h + 1))
                    if u >= 2:
                        pe.wait_ge(S.expd.sem, S.expd.at(u - 1))
                    pe.matmul(PS[:, u % 2, 0:nk], QT[0:w, h % 2, b * PB:(b + 1) * PB],
                              KT[0:w, h // share % 2, 0:nk], start=True, stop=True).then_inc(S.scored.sem, 1)

                def turn_p(u):
                    pe.wait_ge(S.expd.sem, S.expd.at(u + 1))
                    if u >= 2:
                        pe.wait_ge(S.p_copied.sem, S.p_copied.at(u - 1))
                    for j in range(kb):
                        t = pe.transpose(PS[:, 2 + u % 2, j * PB:(j + 1) * PB], Pb[:, u % 2, j * PB:(j + 1) * PB],
                                         ident)
                    t.then_inc(S.p_turned.sem, 1)

                def weigh(u):
                    h, b = units[u]
                    pe.wait_ge(S.p_copied.sem, S.p_copied.at(u + 1))
                    if u >= 2:
                        pe.wait_ge(S.scaled.sem, S.scaled.at(u - 1))
                    for j in range(kb):
                        mm = pe.matmul(PS[:, 4 + u % 2, 0:HD], PT[:, u % 2, j * PB:(j + 1) * PB],
                                       v_of(h // share, j), start=(j == 0), stop=(j == kb - 1))
                    mm.then_inc(S.summed.sem, 1)

                turn_kq(0)
                for t in range(n + 2):
                    if t < n:
                        score(t)
                        h, b = units[t]
                        if b == 1 and h + 1 < heads:
                            turn_kq(h + 1)
                    if 1 <= t <= n:
                        turn_p(t - 1)
                    if t >= 2:
                        weigh(t - 2)

            @block.vector
            def _(dve):
                def copy_k(h):
                    dve.wait_ge(S.kq_turned.sem, S.kq_turned.at(h + 1))
                    dve.tensor_copy(KT[0:w, h // share % 2, 0:nk], PS[0:w, 6, 0:nk]).then_inc(S.k_made.sem, 1)

                def top_of(u):
                    h, b = units[u]
                    m, nm = SM[:, 32 + u % 4:33 + u % 4], SM[:, 36 + u % 4:37 + u % 4]
                    dve.wait_ge(S.scored.sem, S.scored.at(u + 1))
                    s = PS[:, u % 2, 0:nk]
                    if bias_of is not None:
                        dve_step(dve, dve.scalar_tensor_tensor(out=s[:, 0:T], in0=s[:, 0:T], scalar=scale,
                                                               in1=bias_of(h, b), op0=ALU.mult, op1=ALU.add))
                        dve_step(dve, dve.tensor_scalar(s[:, T:nk], s[:, T:nk], scale, None, ALU.mult))
                    dve_step(dve, dve.tensor_reduce(m, s, AX.X, ALU.max))
                    dve.tensor_scalar(nm, m, -1.0 if bias_of is not None else -scale, None,
                                      ALU.mult).then_inc(S.maxed.sem, 1)

                def divide(u):
                    h, b = units[u]
                    dve.wait_ge(S.p_turned.sem, S.p_turned.at(u + 1))
                    r = SM[:, 48 + u % 4:49 + u % 4]
                    dve_step(dve, dve.reciprocal(r, SM[:, 40 + u % 4:41 + u % 4]))
                    dve.wait_ge(S.summed.sem, S.summed.at(u + 1))
                    dve.tensor_scalar(out_of(h, b), PS[:, 4 + u % 2, 0:HD], r, None, ALU.mult).then_inc(S.scaled.sem, 1)

                copy_k(0)
                for t in range(n + 2):
                    if t < n:
                        top_of(t)
                        h, b = units[t]
                        if b == 1 and h + 1 < heads and (h + 1) % share == 0:
                            copy_k(h + 1)
                    if t >= 2:
                        divide(t - 2)

            @block.scalar
            def _(act):
                def copy_q(h):
                    act.wait_ge(S.kq_turned.sem, S.kq_turned.at(h + 1))
                    act.activation(QT[0:w, h % 2, :], PS[0:w, 7, 0:T], ACT.Copy).then_inc(S.q_made.sem, 1)

                def exp(u):
                    act.wait_ge(S.maxed.sem, S.maxed.at(u + 1))
                    if u >= 2:
                        act.wait_ge(S.p_turned.sem, S.p_turned.at(u - 1))
                    if u >= 4:
                        act.wait_ge(S.scaled.sem, S.scaled.at(u - 3))
                    act.activation(Pb[:, u % 2, 0:nk], PS[:, u % 2, 0:nk], ACT.Exp, bias=SM[:, 36 + u % 4:37 + u % 4],
                                   scale=1.0 if bias_of is not None else scale,
                                   accum_out=SM[:, 40 + u % 4:41 + u % 4]).then_inc(S.expd.sem, 1)

                def copy_p(u):
                    act.wait_ge(S.p_turned.sem, S.p_turned.at(u + 1))
                    if u >= 2:
                        act.wait_ge(S.summed.sem, S.summed.at(u - 1))
                    act.activation(PT[:, u % 2, 0:nk], PS[:, 2 + u % 2, 0:nk], ACT.Copy).then_inc(S.p_copied.sem, 1)

                copy_q(0)
                for t in range(n + 1):
                    if t < n:
                        exp(t)
                        h, b = units[t]
                        if b == 1 and h + 1 < heads:
                            copy_q(h + 1)
                    if t >= 1:
                        copy_p(t - 1)
        S.kq_turned.done(heads)
        S.q_made.done(heads)
        S.k_made.done(heads // share)
        for s in (S.scored, S.maxed, S.expd, S.p_turned, S.p_copied, S.summed, S.scaled):
            s.done(n)

    xn = lambda b: XN[:, b, :]
    ht = lambda k: HT[:, k, :]

    L0 = 1536
    p0 = P[:, 0:4 * L0].rearrange("p (b n) -> p b n", b=4)

    def keep(p):
        def store(dve, ps, b, c0, w):
            return dve.tensor_copy(p[:, b, c0:c0 + w], ps)
        return store

    modulate([(X, 0, 0, 0), (XC, 0, 0, 1)], col("n_mix", 0, KD), rows=0)
    linear(ht, KD, L0, lambda c0: range(4), keep(p0))
    qk = [p0[:, b, 256:1280].rearrange("p (h w) -> p h w", w=HD) for b in range(4)]
    scr = HT[:, 0:2, :].rearrange("p a b -> p (a b)")
    rot = HT[:, 4:8, :].rearrange("p a b -> p (a b)")
    gain = row(0, "qk").rearrange("p (h w) -> p h w", w=HD)
    head_norm([(qk[b], gain, scr.rearrange("p (h w) -> p h w", w=HD),
                (lambda dve, b=b: (rope(dve, qk[b][:, 0:8, :], b, 0, rot), rope(dve, qk[b][:, 8:16, :], b, 0, rot)))
                if b < 2 else None) for b in range(4)], batch=13)

    pool_m = AUX[:, 0:2048].rearrange("p (k g t) -> p k g t", k=2, g=4)
    pool_w = EX[0:64, 0:256]
    dT = EX[0:64, 512:2560].rearrange("p (g t) -> p g t", g=4)
    with nc.Block() as block:
        @block.scalar
        def _(act):
            act.dma_start(AUX[:, 0:2048], d["pool_m"]).then_inc(const_in.sem, 16)
            act.dma_start(pool_w, d["pool_w"]).then_inc(const_in.sem, 16)
            act.wait_ge(const_in.sem, 64)

        @block.tensor
        def _(pe):
            pe.wait_ge(const_in.sem, 64)
            for g in range(4):
                for s in range(2):
                    for k in range(2):
                        mm = pe.matmul(PS[0:64, g, s * T:(s + 1) * T], p0[:, 2 * s + k, g * 64:(g + 1) * 64],
                                       pool_m[:, k, g, :], start=(k == 0), stop=(k == 1))
                mm.then_inc(S.made.sem, 1)
            for g in range(4):
                pe.wait_ge(S.evacuated.sem, S.evacuated.at(g + 1))
                for b in range(4):
                    mm = pe.matmul(PS[:, 4 + b, g * 64:(g + 1) * 64], dT[:, g, b * PB:(b + 1) * PB],
                                   pool_w[:, g * 64:(g + 1) * 64], start=True, stop=True)
            mm.then_inc(S.made.sem, 1)

        @block.vector
        def _(dve):
            for g in range(4):
                dve.wait_ge(S.made.sem, S.made.at(g + 1))
                dve.tensor_copy(dT[:, g, :], PS[0:64, g, :]).then_inc(S.evacuated.sem, 1)
            dve.wait_ge(S.made.sem, S.made.at(5))
            for b in range(4):
                dve.tensor_tensor(XN[:, b, 0:256], PS[:, 4 + b, 0:256], row(0, "pool"), ALU.mult)
    S.made.done(5)
    S.evacuated.done(4)

    kv0 = lambda h, j: p0[:, (2, 3, 0, 1)[j], 1024 + h * HD:1024 + (h + 1) * HD]
    vv0 = lambda h, j: p0[:, (2, 3, 0, 1)[j], 1280 + h * HD:1280 + (h + 1) * HD]
    for s, kb in ((0, 4), (1, 2)):
        attention(12, HD, kb, HD ** -0.5, lambda h, b: p0[:, 2 * s + b, 256 + h * HD:256 + (h + 1) * HD], kv0, vv0,
                  lambda h, b: XN[:, 2 * s + b, 256 + h * HD:256 + (h + 1) * HD], share=3)
    turn(xn, KD, 4, lambda k: HT[:, k, 0:512])
    gate_rows(0, 2, 1)
    with nc.Block() as block:
        @block.vector
        def _(dve):
            dve.tensor_copy(EX[:, 0:D], GB[:, :])
    gate_rows(0, 2, 0)

    def store_both(dve, ps, b, c0, w):
        g, x = (GB, X) if b < 2 else (EX, XC)
        t = AUX[:, 3072 + b % 2 * 512:3072 + b % 2 * 512 + w]
        dve_step(dve, dve.tensor_tensor(t, ps, g[:, c0:c0 + w], ALU.mult))
        return dve.tensor_tensor(x[:, b % 2, c0:c0 + w], x[:, b % 2, c0:c0 + w], t, ALU.add)

    linear(ht, KD, D, lambda c0: range(4), store_both)
    checkpoint(nc, "l0_mix", X)
    modulate([(X, 0, 3, 0), (XC, 0, 3, 1)], col("n_ffn", 0, KD), batch=3)
    gate_rows(0, 5, 0)
    ffn(X, F0, 0)
    gate_rows(0, 5, 1)
    ffn(XC, F0, T)
    checkpoint(nc, "l0", X)
    checkpoint(nc, "l0c", XC)

    p1 = P[:, :].rearrange("p (b n) -> p b n", b=4)
    modulate([(X, 1, 0, 0), (XC, 1, 0, 1)], col("n_mix", KD, KD), rows=1)
    linear(ht, KD, L1N, lambda c0: range(4) if c0 + WC > CKV else range(2), keep(p1))
    lat = XN[:, 0:2, :].rearrange("p a b -> p (a b)")
    cqT = lat[:, 0:768].rearrange("p (k t) -> p k t", k=3)
    ckvT = lat[:, 768:1792].rearrange("p (k t) -> p k t", k=2)
    tmp = XN[:, 2:4, :].rearrange("p a b -> p (a b)")
    nh = lambda v, w: v.rearrange("p (h w) -> p h w", w=w)
    head_norm([(nh(p1[:, b, CQ:CQ + 384], 384), None, nh(tmp[:, 0:384], 384), None) for b in range(2)]
              + [(nh(p1[:, b, CKV:CKV + 256], 256), None, nh(tmp[:, 0:256], 256), None) for b in range(4)]
              + [(nh(p1[:, b, NQ:NQ + 512], 64), nh(row(1, "qk")[:, 0:512], 64), nh(tmp[:, 0:512], 64), None)
                 for b in range(2)]
              + [(nh(p1[:, b, NK:NK + 512], 64), nh(row(1, "qk")[:, 512:1024], 64), nh(tmp[:, 0:512], 64), None)
                 for b in range(4)], batch=12)
    turn(lambda b: p1[:, b, CQ:CQ + 384], 3, 2, lambda k: cqT[:, k, :], lambda k: col("qa", k))
    turn(lambda b: p1[:, b, CKV:CKV + 256], 2, 4, lambda k: ckvT[:, k, :], lambda k: col("kva", k))
    q96 = EX[:, 0:1536].rearrange("p (b n) -> p b n", b=2)
    k96 = EX[:, 1536:4608].rearrange("p (b n) -> p b n", b=4)
    kvp = HT[:, :, :].rearrange("p a b -> p (a b)").rearrange("p (b n) -> p b n", b=4)
    linear(lambda k: cqT[:, k, :], 3, 768, lambda c0: range(2), keep(q96))
    linear(lambda k: ckvT[:, k, :], 2, D, lambda c0: range(4), keep(kvp))
    with nc.Block() as block:
        @block.vector
        def _(dve):
            for b in range(4):
                k = nh(k96[:, b, :], 96)
                dve.tensor_copy(k[:, :, 0:64], nh(kvp[:, b, :], 128)[:, :, 0:64])
                dve.tensor_copy(k[:, :, 64:96], p1[:, b, KR:KR + 32].unsqueeze(1).broadcast_to([PB, 8, 32]))
    rot1 = lat
    t96 = nh(tmp[:, 0:768], 96)
    head_norm([(nh(q96[:, b, :], 96), nh(row(1, "mq"), 96), t96,
                (lambda dve, b=b: rope(dve, nh(q96[:, b, :], 96)[:, :, 64:96], b, 32, rot1))) for b in range(2)]
              + [(nh(k96[:, b, :], 96), nh(row(1, "mk"), 96), t96,
                  (lambda dve, b=b: rope(dve, nh(k96[:, b, :], 96)[:, :, 64:96], b, 32, rot1)) if b < 2 else None)
                 for b in range(4)], batch=7)
    attention(8, 96, 4, 96 ** -0.5, lambda h, b: q96[:, b, h * 96:(h + 1) * 96],
              lambda h, j: k96[:, j, h * 96:(h + 1) * 96], lambda h, j: kvp[:, j, h * PB + 64:(h + 1) * PB],
              lambda h, b: XN[:, b, h * HD:(h + 1) * HD])
    bias = AUX[:, :].rearrange("p (h b k) -> p h b k", h=8, b=2)
    with nc.Block() as block:
        @block.scalar
        def _(act):
            act.dma_start(AUX[:, :], d["na_bias"]).then_inc(const_in.sem, 16)
            act.dma_start(EX[:, 0:512], d["na_mask"]).then_inc(const_in.sem, 16)
            act.wait_ge(const_in.sem, 96)

        @block.vector
        def _(dve):
            dve.wait_ge(const_in.sem, 96)
            m = EX[:, 0:512]
            for h in range(8):
                o = AUX[:, h * 512:(h + 1) * 512]
                dve.tensor_tensor(o, o, m, ALU.add)
    attention(8, HD, 4, HD ** -0.5, lambda h, b: p1[:, b, NQ + h * HD:NQ + (h + 1) * HD],
              lambda h, j: p1[:, j, NK + h * HD:NK + (h + 1) * HD],
              lambda h, j: p1[:, j, NV + h * HD:NV + (h + 1) * HD],
              lambda h, b: XN[:, b, 512 + h * HD:512 + (h + 1) * HD], bias_of=lambda h, b: bias[:, h, b, :])
    turn(xn, KD, 2, lambda k: HT[:, k, 0:T])
    gate_rows(1, 2, 0)
    linear(ht, KD, D, lambda c0: range(2), add_gated(X))
    checkpoint(nc, "l1_mix", X)
    modulate([(X, 1, 3, 0)], col("n_ffn", KD, KD), batch=3)
    gate_rows(1, 5, 0)
    ffn(X, F0, 0)
    checkpoint(nc, "l1", X)

    p2 = P[:, 0:2 * L2N].rearrange("p (b n) -> p b n", b=2)
    U = XC[:, :, :].rearrange("p a b -> p (a b)")[:, 0:6 * 259].rearrange("p (c t) -> p c t", c=6)
    hx = HT[:, :, :].rearrange("p a b -> p (a b)")
    XB = hx[:, 0:1536].rearrange("p (c t) -> p c t", c=6)
    btok, SS = hx[:, 1536:1664], hx[:, 1664:1920]
    la, bb, eb, enb, ex, qe, ke, kt = (AUX[:, i * 512:(i + 1) * 512].rearrange("p (b n) -> p b n", b=2)
                                       for i in range(8))
    qkT = EX[0:64, 0:2048].rearrange("p (h n) -> p h n", h=4)
    att = EX[:, 2048:3072].rearrange("p (u n) -> p u n", u=8)
    st = EX[0:64, 3072:4608].rearrange("p (h c v) -> p h c v", h=4, c=3)
    og = XN[:, 2, :].rearrange("p (b n) -> p b n", b=2)
    xh = XN[:, 3, :].rearrange("p (b n) -> p b n", b=2)
    zs = P[:, 2 * L2N:2 * L2N + 1024].rearrange("p (b n) -> p b n", b=2)
    gs = P[:, 2 * L2N + 1024:2 * L2N + 2048].rearrange("p (b n) -> p b n", b=2)
    alT = GB[0:16, 0:T]
    aw = GB[0:16, T:2 * T]
    dec = SM[0:64, 200:216]

    for layer in range(2):
        lay = 2 + layer
        modulate([(X, lay, 0, 2)], col("n_mix", lay * KD, KD), rows=2 + layer)
        with nc.Block() as block:
            @block.vector
            def _(dve):
                dve.memset(U[:, :, 0:3], 0.0)

        def store2(dve, ps, b, c0, w):
            if b is None:
                return dve.tensor_copy(U[:, c0, 3:259], ps)
            return dve.tensor_copy(p2[:, b, c0:c0 + w], ps)
        linear(ht, KD, L2N, lambda c0: range(2), store2, cols_major=CONV)

        with nc.Block() as block:
            @block.scalar
            def _(act):
                act.dma_start(aw, d["gla_a_w"][layer]).then_inc(const_in.sem, 16)
                act.activation(gs[:, :, :], p2[:, :, GG:GG + 512], ACT.Silu)
                act.activation(zs[:, :, :], p2[:, :, SZ:SZ + 512], ACT.Silu)
                act.wait_ge(const_in.sem, 112 + 16 * layer)
                act.wait_ge(S.hop_a.sem, S.hop_a.at(1))
                act_step(act, act.activation(bb[:, :, :], la[:, :, :], ACT.Abs))
                act_step(act, act.activation(eb[:, :, :], bb[:, :, :], ACT.Exp, scale=-1.0))
                act.activation(enb[:, :, :], eb[:, :, :], ACT.Ln, bias=ONEC).then_inc(S.hop_b.sem, 1)
                act.wait_ge(S.made.sem, S.made.at(3))
                b_ps = PS[:, 4:6, 0:T]
                act.activation(dec, PS[0:64, 3, 0:16], ACT.Exp)
                act.wait_ge(S.hop_c.sem, S.hop_c.at(1))
                act.activation(eb[:, :, :], b_ps, ACT.Exp)
                act.activation(ex[:, :, :], ex[:, :, :], ACT.Exp)
                act_step(act, act.activation(enb[:, :, :], b_ps, ACT.Exp, scale=-1.0))

            @block.tensor
            def _(pe):
                for b in range(2):
                    t = pe.transpose(PS[0:16, 0, b * PB:(b + 1) * PB], p2[:, b, GA:GA + 16], ident)
                t.then_inc(S.made.sem, 1)
                pe.wait_ge(S.evacuated.sem, S.evacuated.at(1))
                pe.wait_ge(const_in.sem, 112 + 16 * layer)
                for b in range(2):
                    mm = pe.matmul(PS[:, 1 + b, 0:T], alT[:, b * PB:(b + 1) * PB], aw, start=True, stop=True)
                mm.then_inc(S.made.sem, 1)
                pe.wait_ge(S.hop_d.sem, S.hop_d.at(1))
                for b in range(2):
                    pe.matmul(PS[:, 4 + b, 0:T], trig, la[:, b, :], start=True, stop=True)
                    pe.matmul(PS[:, 6 + b, 0:T], blkg, la[:, b, :], start=True, stop=True)
                for c in range(4):
                    o = c % 2 * 64
                    for h in range(4):
                        mm = pe.matmul(PS[0:64, 3, c * 4 + h:c * 4 + h + 1], la[:, c // 2, h * 64:(h + 1) * 64],
                                       blkg[:, o:o + 1], start=True, stop=True)
                mm.then_inc(S.made.sem, 1)

            @block.vector
            def _(dve):
                dve.wait_ge(S.made.sem, S.made.at(1))
                dve.tensor_copy(alT, PS[0:16, 0, 0:T]).then_inc(S.evacuated.sem, 1)
                dve.wait_ge(S.made.sem, S.made.at(2))
                ab = row(2, "ab").unsqueeze(1).broadcast_to([PB, 2, T])
                dve.tensor_tensor(la[:, :, :], PS[:, 1:3, 0:T], ab, ALU.add).then_inc(S.hop_a.sem, 1)
                dve.wait_ge(S.hop_b.sem, S.hop_b.at(1))
                dve.scalar_tensor_tensor(out=la[:, :, :], in0=la[:, :, :], scalar=0.0, in1=enb[:, :, :], op0=ALU.min,
                                         op1=ALU.subtract).then_inc(S.hop_d.sem, 1)
                dve.wait_ge(S.made.sem, S.made.at(3))
                dve_step(dve, dve.tensor_copy(bb[:, :, :], PS[:, 4:6, 0:T]))
                dve.tensor_tensor(ex[:, :, :], PS[:, 6:8, 0:T], bb[:, :, :], ALU.subtract).then_inc(S.hop_c.sem, 1)
        S.made.done(3)
        for s in (S.evacuated, S.hop_a, S.hop_b, S.hop_c, S.hop_d):
            s.done(1)

        with nc.Block() as block:
            @block.vector
            def _(dve):
                dve_step(dve, dve.memset(att[:, :, :], 0.0))
                dve.scalar_tensor_tensor(out=qe[:, :, :], in0=p2[:, :, GQ:GQ + T], scalar=64 ** -0.5, in1=eb[:, :, :],
                                         op0=ALU.mult, op1=ALU.mult).then_inc(S.ready.sem, 1)
                dve.tensor_tensor(ke[:, :, :], p2[:, :, GK:GK + T], enb[:, :, :], ALU.mult).then_inc(S.ready.sem, 1)
                dve.tensor_tensor(kt[:, :, :], p2[:, :, GK:GK + T], ex[:, :, :], ALU.mult).then_inc(S.ready.sem, 1)
                for h in range(4):
                    dve.wait_ge(S.turned.sem, S.turned.at(h + 1))
                    dve.tensor_copy(qkT[:, h, :], PS[0:64, h, :]).then_inc(S.evacuated.sem, 1)
                for u in range(2):
                    dve.wait_ge(S.scored.sem, S.scored.at(u + 1))
                    for i in range(4):
                        cp = dve.copy_predicated(att[:, 4 * u + i, :], MKG[:, :], PS[:, 4 + u, i * PB:(i + 1) * PB])
                    cp.then_inc(S.hop_a.sem, 1)
                for h in range(4):
                    dve.wait_ge(S.summed.sem, S.summed.at(4 + h + 1))
                    dve_step(dve, dve.tensor_copy(st[:, h, 0, :], PS[0:64, h, 0:PB]))
                    for c in (1, 2):
                        dve_step(dve, dve.scalar_tensor_tensor(
                            out=st[:, h, c, :], in0=st[:, h, c - 1, :], scalar=dec[:, c * 4 + h:c * 4 + h + 1],
                            in1=PS[0:64, h, c * PB:(c + 1) * PB], op0=ALU.mult, op1=ALU.add))
                    dve.sem_inc(S.hop_b.sem, 1)
                for b in range(2):
                    dve.wait_ge(S.made.sem, S.made.at(b + 1))
                    dve.tensor_copy(og[:, b, :], PS[:, 6 + b, :])

            @block.tensor
            def _(pe):
                pe.wait_ge(S.ready.sem, S.ready.at(2))
                for h in range(4):
                    for i, src in enumerate((qe, ke)):
                        for b in range(2):
                            t = pe.transpose(PS[0:64, h, i * T + b * PB:i * T + (b + 1) * PB],
                                             src[:, b, h * 64:(h + 1) * 64], ident)
                    t.then_inc(S.turned.sem, 1)
                for u in range(8):
                    h, b = u // 2, u % 2
                    pe.wait_ge(S.evacuated.sem, S.evacuated.at(h + 1))
                    mm = pe.matmul(PS[:, 4 + u // 4, u % 4 * PB:(u % 4 + 1) * PB],
                                   qkT[:, h, T + b * PB:T + (b + 1) * PB], qkT[:, h, b * PB:(b + 1) * PB],
                                   start=True, stop=True)
                    if u % 4 == 3:
                        mm.then_inc(S.scored.sem, 1)
                pe.wait_ge(S.ready.sem, S.ready.at(3))
                for odd, h in ((odd, h) for odd in range(2) for h in range(4)):
                    if odd and h == 0:
                        pe.wait_ge(S.summed.sem, S.summed.at(4))
                    for c in ((0, 2), (1,))[odd]:
                        o = c % 2 * 64
                        mm = pe.matmul(PS[0:64, h, c * PB:(c + 1) * PB], kt[o:o + 64, c // 2, h * 64:(h + 1) * 64],
                                       p2[o:o + 64, c // 2, GV + h * PB:GV + (h + 1) * PB], start=True, stop=True)
                    mm.then_inc(S.summed.sem, 1)
                for b in range(2):
                    for h in range(4):
                        pe.wait_ge(S.hop_a.sem, S.hop_a.at(h // 2 + 1))
                        pe.wait_ge(S.hop_b.sem, S.hop_b.at(h + 1))
                        o = PS[:, 6 + b, h * PB:(h + 1) * PB]
                        mm = pe.matmul(o, att[:, 2 * h + b, :], p2[:, b, GV + h * PB:GV + (h + 1) * PB], start=True,
                                       stop=True)
                        for r in range(2):
                            c = 2 * b + r
                            if c == 0:
                                continue
                            mm = pe.matmul(o[r * 64:(r + 1) * 64, :], qkT[:, h, c * 64:(c + 1) * 64],
                                           st[:, h, c - 1, :], start=False, stop=True, skip_group_check=True)
                    mm.then_inc(S.made.sem, 1)
        for s, k in ((S.ready, 3), (S.turned, 4), (S.evacuated, 4), (S.scored, 2), (S.hop_a, 2), (S.summed, 8),
                     (S.hop_b, 4), (S.made, 2)):
            s.done(k)
        mixv = XN[:, 0:2, :]
        o4 = [og[:, b, :].rearrange("p (h v) -> p h v", h=4) for b in range(2)]
        gn = row(2, "gn").unsqueeze(1).broadcast_to([PB, 4, PB])
        sc4 = AUX[:, 0:512].rearrange("p (h v) -> p h v", h=4)

        def gated(dve, b):
            dve_step(dve, dve.tensor_tensor(mixv[:, b, 0:512], og[:, b, :], gs[:, b, :], ALU.mult))
        head_norm([(o4[b], gn, sc4, (lambda dve, b=b: gated(dve, b))) for b in range(2)], batch=4)

        cw = lambda c, k: col("conv_w", layer * 24 + c * 4 + k)
        x8, dt, da, cum, ecum, el, dx = (SM[:, 32 + 16 * i:48 + 16 * i].rearrange("p (b h) -> p b h", b=2)
                                         for i in range(7))
        arow = SM[:, 150:158]
        t8, t8b = (SM[:, 160 + 16 * i:176 + 16 * i].rearrange("p (b h) -> p b h", b=2) for i in range(2))
        acc = EX[:, 0:1536].rearrange("p (c t) -> p c t", c=6)
        with nc.Block() as block:
            feed_batch(block, 4)

            @block.tensor
            def _(pe):
                ada_products(pe, 4)

            @block.vector
            def _(dve):
                dve.tensor_tensor(x8, p2[:, :, SDT:SDT + 8], row(2, "dtb").unsqueeze(1).broadcast_to([PB, 2, 8]),
                                  ALU.add).then_inc(S.hop_a.sem, 1)
                for c in range(6):
                    dve_step(dve, dve.tensor_scalar(acc[:, c, :], U[:, c, 0:T], cw(c, 0), None, ALU.mult))
                    for k in range(1, 4):
                        ins = dve.scalar_tensor_tensor(out=acc[:, c, :], in0=U[:, c, k:k + T], scalar=cw(c, k),
                                                       in1=acc[:, c, :], op0=ALU.mult, op1=ALU.add)
                        if k < 3:
                            dve_step(dve, ins)
                    ins.then_inc(S.ready.sem, 1)
                dve.wait_ge(S.hop_b.sem, S.hop_b.at(1))
                dve_step(dve, dve.scalar_tensor_tensor(out=dt, in0=x8, scalar=0.0, in1=t8b, op0=ALU.max, op1=ALU.add))
                dve.scalar_tensor_tensor(out=da, in0=dt, scalar=-1.0, in1=arow.unsqueeze(1).broadcast_to([PB, 2, 8]),
                                         op0=ALU.mult, op1=ALU.mult)
                ada_bias(dve, 4)

            @block.scalar
            def _(act):
                act.wait_ge(S.hop_a.sem, S.hop_a.at(1))
                act_step(act, act.activation(arow, row(2, "alog"), ACT.Exp))
                act_step(act, act.activation(t8, x8, ACT.Abs))
                act_step(act, act.activation(t8, t8, ACT.Exp, scale=-1.0))
                act.activation(t8b, t8, ACT.Ln, bias=ONEC).then_inc(S.hop_b.sem, 1)
                for c in range(6):
                    act.wait_ge(S.ready.sem, S.ready.at(c + 1))
                    act.activation(XB[:, c, :], acc[:, c, :], ACT.Silu, bias=col("conv_b", layer * 6 + c))
                    if c < 4:
                        ada_copies(act, c)
        ada_done(4)
        S.hop_a.done(1)
        S.hop_b.done(1)
        S.ready.done(6)

        W = EX[:, 0:2048].rearrange("p (b h i) -> p b h i", b=2, h=8)
        seg = AUX[:, 0:2048].rearrange("p (b h i) -> p b h i", b=2, h=8)
        xdt = AUX[:, 2048:3072].rearrange("p (b n) -> p b n", b=2)
        xdt2 = AUX[:, 3072:3584]
        with nc.Block() as block:
            @block.tensor
            def _(pe):
                for b in range(2):
                    pe.matmul(PS[:, 2, b * 8:(b + 1) * 8], tri, da[:, b, :], start=True, stop=True)
                    mm = pe.matmul(PS[:, 2, 16 + b * 8:16 + (b + 1) * 8], ones, da[:, b, :], start=True, stop=True)
                mm.then_inc(S.made.sem, 1)
                for b in range(2):
                    for c in range(4):
                        t = pe.transpose(PS[:, b, c * PB:(c + 1) * PB], XB[:, c, b * PB:(b + 1) * PB], ident)
                t = pe.transpose(PS[:, 3, 0:PB], XB[:, 4, 0:PB], ident)
                t.then_inc(S.turned.sem, 1)
                for b in range(2):
                    for h in range(8):
                        mm = pe.matmul(PS[:, 4 + 2 * b + h // 4, h % 4 * PB:(h % 4 + 1) * PB],
                                       da[:, b, h:h + 1].broadcast_to([PB, PB]), tri, start=True, stop=True)
                    mm.then_inc(S.scored.sem, 1)

            @block.vector
            def _(dve):
                dve.wait_ge(S.made.sem, S.made.at(1))
                dve_step(dve, dve.tensor_copy(cum, PS[:, 2, 0:16].rearrange("p (b h) -> p b h", b=2)))
                dve.tensor_tensor(el, PS[:, 2, 16:32].rearrange("p (b h) -> p b h", b=2), cum,
                                  ALU.subtract).then_inc(S.hop_a.sem, 1)
                dve.wait_ge(S.turned.sem, S.turned.at(1))
                dve_step(dve, dve.tensor_copy(xh[:, :, :], PS[:, 0:2, :]))
                dve.tensor_copy(btok, PS[:, 3, 0:PB])
                for b in range(2):
                    xv = xh[:, b, :].rearrange("p (h w) -> p h w", h=8)
                    dve_step(dve, dve.tensor_tensor(xdt[:, b, :].rearrange("p (h w) -> p h w", h=8), xv,
                                                    dt[:, b, :].unsqueeze(2).broadcast_to([PB, 8, 64]), ALU.mult))
                for b in range(2):
                    dve.wait_ge(S.scored.sem, S.scored.at(b + 1))
                    for h in range(8):
                        ins = dve.scalar_tensor_tensor(out=seg[:, b, h, :],
                                                       in0=PS[:, 4 + 2 * b + h // 4, h % 4 * PB:(h % 4 + 1) * PB],
                                                       scalar=cum[:, b, h:h + 1], in1=negm, op0=ALU.subtract,
                                                       op1=ALU.add)
                    ins.then_inc(S.hop_b.sem, 1)
                dve.wait_ge(S.hop_c.sem, S.hop_c.at(1))
                dve.tensor_tensor(xdt2.rearrange("p (h w) -> p h w", h=8),
                                  xdt[:, 0, :].rearrange("p (h w) -> p h w", h=8),
                                  el[:, 0, :].unsqueeze(2).broadcast_to([PB, 8, 64]), ALU.mult)

            @block.scalar
            def _(act):
                act.wait_ge(S.hop_a.sem, S.hop_a.at(1))
                act.activation(ecum, cum, ACT.Exp)
                act.activation(el, el, ACT.Exp).then_inc(S.hop_c.sem, 1)
                for b in range(2):
                    act.wait_ge(S.hop_b.sem, S.hop_b.at(b + 1))
                    act.activation(seg[:, b, :, :], seg[:, b, :, :], ACT.Exp)
        for s in (S.made, S.turned, S.hop_a, S.hop_c):
            s.done(1)
        S.scored.done(2)
        S.hop_b.done(2)

        y = og
        dsk = row(2, "dskip").unsqueeze(2).broadcast_to([PB, 8, 64])
        with nc.Block() as block:
            @block.tensor
            def _(pe):
                for b in range(2):
                    for g in range(2):
                        r = slice(g * 64, (g + 1) * 64)
                        mm = pe.matmul(PS[:, 2 * b + g, 0:PB], XB[r, 4, b * PB:(b + 1) * PB],
                                       XB[r, 5, b * PB:(b + 1) * PB], start=True, stop=True)
                    mm.then_inc(S.scored.sem, 1)
                for g in range(2):
                    mm = pe.matmul(PS[g * 64:(g + 1) * 64, 7, 0:T], btok[:, g * 64:(g + 1) * 64],
                                   xdt2[:, g * T:(g + 1) * T], start=True, stop=True)
                mm.then_inc(S.summed.sem, 1)
                for b in range(2):
                    pe.wait_ge(S.hop_a.sem, S.hop_a.at(b + 1))
                    for h in range(8):
                        mm = pe.matmul(PS[:, 4 + b, h * 64:(h + 1) * 64], W[:, b, h, :],
                                       xdt[:, b, h * 64:(h + 1) * 64], start=True, stop=True)
                pe.wait_ge(S.evacuated.sem, S.evacuated.at(1))
                for g in range(2):
                    r = slice(g * 64, (g + 1) * 64)
                    mm = pe.matmul(PS[:, 6 + g, 0:T], XB[r, 5, PB:2 * PB], SS[r, :], start=True, stop=True)
                mm.then_inc(S.made.sem, 1)

            @block.vector
            def _(dve):
                for b in range(2):
                    dve.wait_ge(S.scored.sem, S.scored.at(b + 1))
                    for g in range(2):
                        sc = PS[:, 2 * b + g, 0:PB].unsqueeze(1).broadcast_to([PB, 4, PB])
                        ins = dve.tensor_tensor(W[:, b, 4 * g:4 * g + 4, :], seg[:, b, 4 * g:4 * g + 4, :], sc, ALU.mult)
                    ins.then_inc(S.hop_a.sem, 1)
                dve.wait_ge(S.summed.sem, S.summed.at(1))
                dve.tensor_copy(SS[:, :], PS[:, 7, 0:T]).then_inc(S.evacuated.sem, 1)
                h8 = lambda v: v.rearrange("p (h w) -> p h w", h=8)
                for b in range(2):
                    dve_step(dve, dve.tensor_tensor(h8(y[:, b, :]), h8(xh[:, b, :]), dsk, ALU.mult))
                dve.wait_ge(S.made.sem, S.made.at(1))
                for b in range(2):
                    dve_step(dve, dve.tensor_tensor(y[:, b, :], y[:, b, :], PS[:, 4 + b, :], ALU.add))
                t = seg[:, 0, 0:4, :].rearrange("p h i -> p (h i)")
                for g in range(2):
                    dve_step(dve, dve.tensor_tensor(
                        t[:, g * T:(g + 1) * T].rearrange("p (h w) -> p h w", h=4),
                        PS[:, 6 + g, 0:T].rearrange("p (h w) -> p h w", h=4),
                        ecum[:, 1, 4 * g:4 * g + 4].unsqueeze(2).broadcast_to([PB, 4, 64]), ALU.mult))
                dve_step(dve, dve.tensor_tensor(y[:, 1, :], y[:, 1, :], t, ALU.add))
                dve.tensor_tensor(y[:, :, :], y[:, :, :], zs[:, :, :], ALU.mult)
        S.scored.done(2)
        S.hop_a.done(2)
        for s in (S.summed, S.evacuated, S.made):
            s.done(1)

        def into_mix(dve, b):
            dve_step(dve, dve.tensor_tensor(mixv[:, b, 512:1024], y[:, b, :], row(2, "sn"), ALU.mult))
        head_norm([(nh(y[:, b, :], 512), None, nh(AUX[:, 2048:2560], 512), (lambda dve, b=b: into_mix(dve, b)))
                   for b in range(2)], batch=2)
        turn(xn, KD, 2, lambda k: HT[:, k, 0:T])
        gate_rows(lay, 2, 2)
        linear(ht, KD, D, lambda c0: range(2), add_gated(X))
        checkpoint(nc, f"s{layer}_mix", X)
        modulate([(X, lay, 3, 2)], col("n_ffn", lay * KD, KD))
        gate_rows(lay, 5, 2)
        if layer == 0:
            ffn(X, F2, 0)
            checkpoint(nc, "s0", X)
            continue

        lg, ix, h1, h2, gates, sel, pos = (SM[:, 32 + 16 * i:48 + 16 * i].rearrange("p (b e) -> p b e", b=2)
                                           for i in range(7))
        m1, i1, m2, i2, pd = (SM[:, 144 + 2 * i:146 + 2 * i] for i in range(5))
        most = SM[0:1, 156:157]
        bc = lambda v: v.unsqueeze(2).broadcast_to([PB, 2, NE])
        it = iota[:, 0:NE].unsqueeze(1).broadcast_to([PB, 2, NE])
        gate_all = XC[:, :, :].rearrange("p a b -> p (a b)").rearrange("p (e t) -> p e t", e=NE)
        pick = EX[:, 0:2048].rearrange("p (b e q) -> p b e q", b=2, e=NE)
        put = AUX[:, 0:2048].rearrange("p (b e q) -> p b e q", b=2, e=NE)
        putT = EX[:, 2048:4096].rearrange("p (e t) -> p e t", e=NE)
        he_hi, he_lo = (P[:, i * NE * D // 2:(i + 1) * NE * D // 2].bitcast(BF16) for i in range(2))
        HEH, HEL = (v.rearrange("p (e k q) -> p e k q", e=NE, k=KD) for v in (he_hi, he_lo))
        with nc.Block() as block:
            @block.tensor
            def _(pe):
                for b in range(2):
                    for k in range(KD):
                        mm = pe.matmul(PS[:, 0, b * NE:(b + 1) * NE], HT[:, k, b * PB:(b + 1) * PB],
                                       col("router", k * NE, NE), start=(k == 0), stop=(k == KD - 1))
                mm.then_inc(S.made.sem, 1)
                for b in range(2):
                    for k in range(KD):
                        t = pe.transpose(PS[:, 4 + 2 * b + k // 4, k % 4 * PB:(k % 4 + 1) * PB],
                                         HT[:, k, b * PB:(b + 1) * PB], ident)
                t.then_inc(S.turned.sem, 1)
                pe.wait_ge(S.ready.sem, S.ready.at(1))
                pe.matmul(PS[:, 0, 0:NE], tri, sel[:, 0, :], start=True, stop=True)
                pe.matmul(PS[:, 0, NE:2 * NE], tri, sel[:, 1, :], start=True, stop=False)
                pe.matmul(PS[:, 0, NE:2 * NE], ones, sel[:, 0, :], start=False, stop=True)
                pe.matmul(PS[:, 0, 2 * NE:3 * NE], ones, sel[:, 0, :], start=True, stop=False)
                pe.matmul(PS[:, 0, 2 * NE:3 * NE], ones, sel[:, 1, :], start=False, stop=True).then_inc(S.made.sem, 1)

            @block.vector
            def _(dve):
                def step(ins):
                    dve_step(dve, ins)
                dve.wait_ge(S.made.sem, S.made.at(1))
                step(dve.tensor_copy(lg, PS[:, 0, 0:2 * NE].rearrange("p (b e) -> p b e", b=2)))
                for m, i, hot in ((m1, i1, h1), (m2, i2, h2)):
                    step(dve.tensor_reduce(m, lg, AX.X, ALU.max))
                    step(dve.tensor_tensor(ix, lg, bc(m), ALU.is_lt))
                    step(dve.scalar_tensor_tensor(out=ix, in0=ix, scalar=100.0, in1=it, op0=ALU.mult, op1=ALU.add))
                    step(dve.tensor_reduce(i, ix, AX.X, ALU.min))
                    step(dve.tensor_tensor(hot, it, bc(i), ALU.is_equal))
                    if m is m1:
                        step(dve.scalar_tensor_tensor(out=lg, in0=hot, scalar=-3.0e38, in1=lg, op0=ALU.mult,
                                                      op1=ALU.add))
                dve.tensor_tensor(sel, h1, h2, ALU.add).then_inc(S.ready.sem, 1)
                dve.tensor_tensor(pd, m2, m1, ALU.subtract).then_inc(S.hop_a.sem, 1)
                dve.wait_ge(S.hop_b.sem, S.hop_b.at(1))
                step(dve.tensor_scalar(m1, pd, 1.0, None, ALU.add))
                step(dve.reciprocal(m2, m1))
                step(dve.tensor_tensor(i1, m2, pd, ALU.mult))
                step(dve.tensor_tensor(h1, h1, bc(m2), ALU.mult))
                step(dve.tensor_tensor(h2, h2, bc(i1), ALU.mult))
                step(dve.tensor_tensor(gates, h1, h2, ALU.add))
                dve.wait_ge(S.made.sem, S.made.at(2))
                step(dve.tensor_scalar(pos, PS[:, 0, 0:2 * NE].rearrange("p (b e) -> p b e", b=2), -1.0, None, ALU.add))
                step(dve.tensor_reduce(most, PS[0:1, 0, 2 * NE:3 * NE], AX.X, ALU.max))
                dve.tensor_copy(COUNT[0:1, 0:1], most)
                for e in range(NE):
                    for b in range(2):
                        dve.tensor_scalar(pick[:, b, e, :], iota, pos[:, b, e:e + 1], sel[:, b, e:e + 1],
                                          ALU.is_equal, ALU.mult)
                        dve.tensor_scalar(put[:, b, e, :], iota, pos[:, b, e:e + 1], gates[:, b, e:e + 1],
                                          ALU.is_equal, ALU.mult)

            @block.scalar
            def _(act):
                act.wait_ge(S.turned.sem, S.turned.at(1))
                for b in range(2):
                    act.activation(XN[:, b, :], PS[:, 4 + 2 * b:6 + 2 * b, :].rearrange("p a n -> p (a n)"), ACT.Copy)
                act.wait_ge(S.hop_a.sem, S.hop_a.at(1))
                act.activation(pd, pd, ACT.Exp).then_inc(S.hop_b.sem, 1)
        S.made.done(2)
        for s in (S.ready, S.hop_a, S.hop_b, S.turned):
            s.done(1)

        with nc.Block() as block:
            @block.tensor
            def _(pe):
                for e in range(NE):
                    for b in range(2):
                        t = pe.transpose(PS[:, e // 2, e % 2 * T + b * PB:e % 2 * T + (b + 1) * PB],
                                         put[:, b, e, :], ident)
                t.then_inc(S.turned.sem, 1)
                for q in range(2 * KD):
                    k, half = q // 2, q % 2
                    if q >= 4:
                        pe.wait_ge(S.evacuated.sem, S.evacuated.at(q - 3))
                    for b in range(2):
                        mm = pe.matmul(PS[:, 4 + q % 4, :], XN[:, b, k * PB:(k + 1) * PB],
                                       pick[:, b, 4 * half:4 * half + 4, :].rearrange("p e q -> p (e q)"),
                                       start=(b == 0), stop=(b == 1))
                    mm.then_inc(S.made.sem, 1)
                pe.wait_ge(S.ready.sem, S.ready.at(1))
                for e in range(NE):
                    for b in range(2):
                        mm = pe.matmul(PS[:, e // 2, e % 2 * T + b * PB:e % 2 * T + (b + 1) * PB],
                                       gates[:, b, e:e + 1].broadcast_to([PB, PB]), ident, start=True, stop=True)
                mm.then_inc(S.turned.sem, 1)

            @block.vector
            def _(dve):
                for q in range(2 * KD):
                    k, half = q // 2, q % 2
                    dve.wait_ge(S.made.sem, S.made.at(q + 1))
                    e4 = slice(4 * half, 4 * half + 4)
                    src = PS[:, 4 + q % 4, :].rearrange("p (e q) -> p e q", e=4)
                    dve_step(dve, dve.tensor_copy(HEH[:, e4, k, :], src))
                    dve.tensor_tensor(HEL[:, e4, k, :], src, HEH[:, e4, k, :], ALU.subtract).then_inc(S.evacuated.sem, 1)

            @block.scalar
            def _(act):
                act.wait_ge(S.turned.sem, S.turned.at(1))
                for i in range(4):
                    c = act.activation(putT[:, 2 * i:2 * i + 2, :].rearrange("p e t -> p (e t)"), PS[:, i, :], ACT.Copy)
                c.then_inc(S.ready.sem, 1)
                act.wait_ge(S.turned.sem, S.turned.at(2))
                for i in range(4):
                    act.activation(gate_all[:, 2 * i:2 * i + 2, :].rearrange("p e t -> p (e t)"), PS[:, i, :], ACT.Copy)
        S.turned.done(2)
        S.ready.done(1)
        for s in (S.made, S.evacuated):
            s.done(2 * KD)

        a, fc = place.n, F2 // PB
        n = fc * NE
        gathered = moe_parts(he_hi, he_lo, putT, fc)
        general = ffn_parts(X, F2, 0, gates=gate_all)
        with nc.Block() as block:
            @block.sync
            def _(sp):
                feed(sp, a + SLOTS, a + n + SLOTS)

            @block.tensor
            def _(pe):
                few = pe.value_load(COUNT[0:1, 0:1], min_val=0, max_val=T) <= PB
                with pe.If(few):
                    gathered[0](pe)
                with pe.Else():
                    general[0](pe)

            @block.scalar
            def _(act):
                few = act.value_load(COUNT[0:1, 0:1], min_val=0, max_val=T) <= PB
                with act.If(few):
                    gathered[1](act)
                with act.Else():
                    general[1](act)

            @block.vector
            def _(dve):
                few = dve.value_load(COUNT[0:1, 0:1], min_val=0, max_val=T) <= PB
                steps = dve_step.n
                with dve.If(few):
                    gathered[2](dve)
                dve_step.n = steps
                with dve.Else():
                    general[2](dve)
        ffn_done(n)
        checkpoint(nc, "s1", X)

    with nc.Block() as block:
        @block.scalar
        def _(act):
            for b in range(2):
                act_step(act, act.activation(XN[:, b, :], X[:, b, :], ACT.Square, accum_out=SM[:, 8 + b:9 + b]))
            act_step(act, act.activation(SM[:, 12:14], SM[:, 8:10], ACT.Ln, bias=EPSC, scale=1.0 / D))
            act.activation(SM[:, 16:18], SM[:, 12:14], ACT.Exp, scale=-0.5).then_inc(S.hop_a.sem, 1)
            act.wait_ge(S.hop_b.sem, S.hop_b.at(1))
            for b in range(2):
                act.activation(XN[:, b, :], X[:, b, :], ACT.Copy, scale=SM[:, 16 + b:17 + b]).then_inc(S.ready.sem, 1)

        @block.vector
        def _(dve):
            dve.wait_ge(S.hop_a.sem, S.hop_a.at(1))
            refine(dve, SM[:, 16:18], SM[:, 8:10], SM[:, 20:22], D).then_inc(S.hop_b.sem, 1)
            for b in range(2):
                dve.wait_ge(S.ready.sem, S.ready.at(b + 1))
                dve.tensor_tensor(XN[:, b, :], XN[:, b, :], row(2, "fin"), ALU.mult).then_inc(S.made.sem, 1)

        @block.sync
        def _(sp):
            for b in range(2):
                sp.wait_ge(S.made.sem, S.made.at(b + 1))
                sp.dma_start(out[b * PB:(b + 1) * PB, :], XN[:, b, :]).then_inc(out_sem.sem, 16)
            sp.wait_ge(out_sem.sem, 32)


def checkpoint(nc, name, t):
    pass


def packed(w, cols=None):
    k, n = w.shape
    kt = k // PB
    out = np.zeros((len(chunks(n)), PB, kt * WC), w.dtype)
    for i, (a, c) in enumerate(chunks(n)):
        out[i, :, :kt * c] = w[:, a:a + c].reshape(kt, PB, c).transpose(1, 0, 2).reshape(PB, kt * c)
    return out


def packed_ffn(wg, wu, wd):
    f = wg.shape[1] // PB
    out = np.empty((f, PB, 3, D), wg.dtype)
    for i, w in enumerate((wg, wu)):
        out[:, :, i, :] = w.reshape(KD, PB, f, PB).transpose(2, 1, 0, 3).reshape(f, PB, D)
    out[:, :, 2, :] = wd.reshape(f, PB, D)
    return out.reshape(f, PB, 3 * D)


def columns(v):
    return np.ascontiguousarray(v.reshape(-1, PB).T)


def constants():
    f = np.float32
    t = np.arange(T)
    m = np.zeros((4, T, T), f)
    for g, w in enumerate((2, 4, 8, 16)):
        lo, hi = np.clip(t - w // 2, 0, T), np.clip(t - w // 2 + w, 0, T)
        for i in t:
            m[g, i, lo[i]:hi[i]] = f(1) / f(hi[i] - lo[i])
            m[g, i, i] -= 1
    pool = np.ascontiguousarray(m.transpose(2, 0, 1).reshape(2, PB, 4, T).transpose(1, 0, 2, 3).reshape(PB, 2048))
    i, j = np.arange(PB)[:, None], np.arange(PB)[None, :]
    same = i // 64 == j // 64
    sq = np.stack([i == j, i <= j, ((i <= j) & same) / 16, same / 16, np.where(i <= j, 0, NEG), np.ones((PB, PB)),
                   np.broadcast_to(j, (PB, PB))],
                  1).astype(f)
    rope = np.zeros((PB, 2, 2, 48), f)
    for b in range(2):
        tok = b * PB + np.arange(PB)
        for at, d in ((0, 32), (32, 16)):
            inv = (f(10000.0) ** (-np.arange(d // 2, dtype=f) * f(2.0) / f(d))).astype(f)
            for a, pos in enumerate((tok // GRID_W, tok % GRID_W)):
                ang = pos.astype(f)[:, None] * inv[None]
                s = slice(at + a * d // 2, at + (a + 1) * d // 2)
                rope[:, b, 0, s], rope[:, b, 1, s] = np.cos(ang), np.sin(ang)
    q = t.reshape(2, PB).T[:, :, None]
    k = t[None, None, :]
    c0 = np.clip(q % GRID_W - NA_COLS // 2, 0, GRID_W - NA_COLS)
    seen = (k % GRID_W >= c0) & (k % GRID_W < c0 + NA_COLS)
    dr = k // GRID_W - q // GRID_W + NA_ROWS - 1
    dc = np.clip(k % GRID_W - q % GRID_W + NA_COLS - 1, 0, 2 * NA_COLS - 2)
    na_mask = np.where(seen, 0, NEG).astype(f).reshape(PB, 512)
    return dict(pool_m=pool, squares=sq, rope=rope, na_mask=na_mask,
                mask_gla=((i <= j) & same).astype(np.int32)), dr, dc


def laid_out(i):
    i = {k: np.asarray(v) for k, v in i.items()}
    con, dr, dc = constants()
    a = dict(con)
    for n in ("x", "ctx"):
        a[n] = np.ascontiguousarray(i[n][0].reshape(2, PB, D).transpose(1, 0, 2))
    ada_w = [i["l0_ada_w"], i["l1_ada_w"], i["ada_w_2"][0], i["ada_w_2"][1]]
    a["ada"] = np.concatenate([packed(w) for w in ada_w])
    ada_b = np.concatenate([columns(b) for b in (i["l0_ada_b"], i["l1_ada_b"], i["ada_b_2"][0], i["ada_b_2"][1])], 1)
    a["l0_w_in"], a["l0_w_out"], a["l1_w_out"] = packed(i["l0_w_in"]), packed(i["l0_w_out"]), packed(i["l1_w_out"])
    for n in (0, 1):
        a[f"l{n}_ffn"] = packed_ffn(i[f"l{n}_ffn_w_gate"], i[f"l{n}_ffn_w_up"], i[f"l{n}_ffn_w_down"])
    cq, ckv, kr, nq, nk, nv = np.split(i["l1_w_in"], np.cumsum([384, 256, 32, 512, 512]), axis=1)
    a["l1_w_in"] = packed(np.concatenate([cq, nq, ckv, kr, nk, nv], 1))
    a["l1_uq"], a["l1_ukv"] = packed(i["l1_mla_w_uq"]), packed(i["l1_mla_w_ukv"])
    for n in (0, 1):
        q, k, v, g, al, z, xs, bm, cm, dt = np.split(i["w_in_2"][n], np.cumsum([256, 256, 512, 512, 16, 512, 512, 128,
                                                                             128]), axis=1)
        a[f"w_in{n}"] = np.concatenate([packed(np.concatenate([q, k, v, g, al, z, dt], 1)),
                                        packed(np.concatenate([xs, bm, cm], 1))])
        a[f"w_out{n}"] = packed(i["w_out_2"][n])
    a["ffn2"] = packed_ffn(i["ffn_w_gate_2"][0], i["ffn_w_up_2"][0], i["ffn_w_down_2"][0])
    moe = np.empty((NE * F2 // PB, PB, 3 * D), np.float32)
    for e in range(NE):
        moe[e * F2 // PB:(e + 1) * F2 // PB] = packed_ffn(i["moe_w_gate_2"][0, e], i["moe_w_up_2"][0, e],
                                                          i["moe_w_down_2"][0, e])
    a["moe"] = moe
    a["pool_w"] = np.ascontiguousarray(i["l0_pool_w"].transpose(1, 0, 2).reshape(64, 256))
    a["gla_a_w"] = i["gla_a_w_2"]
    rpb = i["l1_na_rpb"][:, dr, dc]
    a["na_bias"] = np.ascontiguousarray(rpb.transpose(1, 0, 2, 3).reshape(PB, 4096))
    cond = np.stack([columns(i["c"]), columns(i["c_ctx"]), columns(i["c_2"])], 2).reshape(PB, KD * 3)
    n_mix = [columns(v) for v in (i["l0_norm_mix"], i["l1_norm_mix"], i["norm1_w_2"])]
    n_ffn = [columns(v) for v in (i["l0_norm_ffn"], i["l1_norm_ffn"], i["norm2_w_2"])]
    conv_w = i["conv_w_2"].reshape(2, 4, 6, PB).transpose(3, 0, 2, 1).reshape(PB, 48)
    a["cols"] = np.ascontiguousarray(np.concatenate(
        [cond, ada_b, *n_mix, *n_ffn, columns(i["l1_mla_q_a_gain"]), columns(i["l1_mla_kv_a_gain"]), conv_w,
         columns(i["conv_b_2"]), i["router_w_2"][0].reshape(KD, PB, NE).transpose(1, 0, 2).reshape(PB, KD * NE)], 1))
    rows = np.zeros((4, ROWW), np.float32)

    def put(r, kind, name, v):
        at, w = ROWS[kind][name]
        rows[r, at:at + w] = v
    put(0, 0, "qk", np.concatenate([np.tile(i["l0_q_gain"], 12), np.tile(i["l0_k_gain"], 4)]))
    put(0, 0, "pool", i["l0_pool_scale"])
    put(1, 1, "qk", np.concatenate([np.tile(i["l1_na_q_gain"], 8), np.tile(i["l1_na_k_gain"], 8)]))
    put(1, 1, "mq", np.tile(i["l1_mla_q_gain"], 8))
    put(1, 1, "mk", np.tile(i["l1_mla_k_gain"], 8))
    for n in (0, 1):
        for name, v in (("ab", "gla_a_b_2"), ("gn", "gla_norm_w_2"), ("sn", "ssd_norm_w_2"), ("dtb", "dt_bias_2"),
                        ("alog", "a_log_2"), ("dskip", "d_skip_2")):
            put(2 + n, 2, name, i[v][n])
        put(2 + n, 2, "fin", i["final_norm_w_2"])
    a["rows"] = rows
    return a


def kernel(**inputs):
    import concourse.bacc as bacc
    from concourse.bass_utils import run_bass_kernel_spmd

    arrays = laid_out(inputs)
    nc = bacc.Bacc("TRN2", target_bir_lowering=False, num_devices=1)
    d = {n: nc.dram_tensor(n, v.shape, mybir.dt.from_np(v.dtype), kind="ExternalInput").ap() for n, v in arrays.items()}
    out = nc.dram_tensor("out", (T, D), F32, kind="ExternalOutput").ap()
    program(nc, d, out)
    r = run_bass_kernel_spmd(nc, [arrays], core_ids=[0])
    return r.results[0]["out"].reshape(1, T, D)
```
